# Optimizing a Trainium2 kernel written in Bass

```python
import jax, jax.numpy as jnp
from jax import lax
import numpy as np

D_MODEL = 1024
BATCH = 1
SEQ = 512
DEPTH = 1

HEAD_DIM = 64
D_MIX = D_MODEL
N_HEADS = D_MIX // HEAD_DIM
NSA_HEADS = N_HEADS // 2
NSA_KV = 2
NSA_GROUP = NSA_HEADS // NSA_KV
SWA_HEADS = N_HEADS - NSA_HEADS
SWA_KV = 1
SWA_GROUP = SWA_HEADS // SWA_KV
NSA_CMP_LEN = 32
NSA_CMP_STRIDE = 16
NSA_CMP_HIDDEN = 256
NSA_SEL_BLOCK = 64
NSA_TOPN = 16
NSA_WINDOW = 512
SWA_WINDOW = 128
Q_BLOCK = 128
FORCE_SCORE = 1.0e4
PEER_HEADS = 8
PEER_NKEYS = 128
PEER_EXPERTS = PEER_NKEYS * PEER_NKEYS
PEER_DKEY = 256
PEER_TOPK = 16
PEER_CHUNK = 128
EPS = 1e-6

kernel_name = 'hymba_nsa_swa_peer_layer'

def split_sizes():
    hd = HEAD_DIM
    return [NSA_HEADS * hd,
            NSA_KV * hd, NSA_KV * hd,
            NSA_KV * hd, NSA_KV * hd,
            NSA_KV * hd, NSA_KV * hd,
            NSA_HEADS * 3,
            SWA_HEADS * hd,
            SWA_KV * hd, SWA_KV * hd]

def alibi_slopes(n):
    return (2.0 ** (-8.0 * (np.arange(n) + 1) / n)).astype(np.float32)

def rms_norm(x, g):
    xf = x.astype(jnp.float32)
    y = xf * lax.rsqrt(jnp.mean(xf * xf, axis=-1, keepdims=True) + EPS)
    return (y * g.astype(jnp.float32)).astype(x.dtype)

def masked_softmax(s, valid):
    s = jnp.where(valid, s.astype(jnp.float32), -jnp.inf)
    m = jnp.max(s, axis=-1, keepdims=True)
    m = jnp.where(jnp.isfinite(m), m, 0.0)
    e = jnp.exp(s - m)
    return e / jnp.maximum(jnp.sum(e, axis=-1, keepdims=True), 1e-30)

def compress(kv, pe, w1, w2):
    B, T, G, dh = kv.shape
    n_cmp = (T - NSA_CMP_LEN) // NSA_CMP_STRIDE + 1
    idx = np.arange(n_cmp)[:, None] * NSA_CMP_STRIDE + np.arange(NSA_CMP_LEN)[None, :]
    blocks = kv[:, idx] + pe[None, None, :, None, :]
    flat = blocks.transpose(0, 1, 3, 2, 4).reshape(B, n_cmp, G, NSA_CMP_LEN * dh)
    return jax.nn.gelu(flat @ w1) @ w2

def nsa_attention(q, kc_raw, vc_raw, ks, vs, kw, vw, gates,
                  pe_k, w1_k, w2_k, pe_v, w1_v, w2_v, slopes):
    B, T, G, Hg, dh = q.shape
    scale = dh ** -0.5
    kc = compress(kc_raw, pe_k, w1_k, w2_k)
    vc = compress(vc_raw, pe_v, w1_v, w2_v)
    n_cmp = kc.shape[1]
    n_sel = T // NSA_SEL_BLOCK
    k_top = min(NSA_TOPN, n_sel)
    cmp_end = jnp.asarray(np.arange(n_cmp) * NSA_CMP_STRIDE + NSA_CMP_LEN - 1, jnp.int32)
    c0 = np.arange(n_cmp)[:, None] * NSA_CMP_STRIDE
    s0 = np.arange(n_sel)[None, :] * NSA_SEL_BLOCK
    overlap = jnp.asarray(((c0 < s0 + NSA_SEL_BLOCK) & (c0 + NSA_CMP_LEN > s0)).astype(np.float32))
    ks_blk = ks.reshape(B, n_sel, NSA_SEL_BLOCK, G, dh).transpose(0, 3, 1, 2, 4)
    vs_blk = vs.reshape(B, n_sel, NSA_SEL_BLOCK, G, dh).transpose(0, 3, 1, 2, 4)
    kw_pad = jnp.pad(kw, ((0, 0), (NSA_WINDOW, 0), (0, 0), (0, 0)))
    vw_pad = jnp.pad(vw, ((0, 0), (NSA_WINDOW, 0), (0, 0), (0, 0)))
    gsig = jax.nn.sigmoid(gates.astype(jnp.float32))
    sl = jnp.asarray(slopes).reshape(G, Hg)[None, :, :, None, None]
    bi = jnp.arange(B)[:, None, None, None]
    gi = jnp.arange(G)[None, :, None, None]

    def block(i):
        q0 = i * Q_BLOCK
        qb = lax.dynamic_slice_in_dim(q, q0, Q_BLOCK, axis=1)
        tq = q0 + jnp.arange(Q_BLOCK)
        dist_c = tq[:, None] - cmp_end[None, :]
        s_c = jnp.einsum('bqghd,bngd->bghqn', qb, kc).astype(jnp.float32) * scale
        p_c = masked_softmax(s_c - sl * dist_c.astype(jnp.float32), dist_c >= 0)
        o_c = jnp.einsum('bghqn,bngd->bqghd', p_c.astype(vc.dtype), vc)
        imp = jnp.einsum('bgqn,ns->bgqs', jnp.sum(p_c, axis=2), overlap)
        blk_t = (tq // NSA_SEL_BLOCK)[:, None]
        j = jnp.arange(n_sel)[None, :]
        imp = jnp.where((j == 0) | (j == blk_t) | (j == blk_t - 1), FORCE_SCORE, imp)
        imp = jnp.where(j <= blk_t, imp, -jnp.inf)
        top_s, top_i = lax.top_k(imp, k_top)
        blk_ok = jnp.isfinite(top_s)
        k_sel = ks_blk[bi, gi, top_i].reshape(B, G, Q_BLOCK, k_top * NSA_SEL_BLOCK, dh)
        v_sel = vs_blk[bi, gi, top_i].reshape(B, G, Q_BLOCK, k_top * NSA_SEL_BLOCK, dh)
        pos = (top_i[..., None] * NSA_SEL_BLOCK + jnp.arange(NSA_SEL_BLOCK)).reshape(
            B, G, Q_BLOCK, k_top * NSA_SEL_BLOCK)
        dist_s = tq[None, None, :, None] - pos
        ok_s = jnp.broadcast_to(blk_ok[..., None], blk_ok.shape + (NSA_SEL_BLOCK,)).reshape(
            dist_s.shape) & (dist_s >= 0)
        s_s = jnp.einsum('bqghd,bgqkd->bghqk', qb, k_sel).astype(jnp.float32) * scale
        s_s = s_s - sl * dist_s[:, :, None].astype(jnp.float32)
        p_s = masked_softmax(s_s, ok_s[:, :, None])
        o_s = jnp.einsum('bghqk,bgqkd->bqghd', p_s.astype(v_sel.dtype), v_sel)
        kwb = lax.dynamic_slice_in_dim(kw_pad, q0, Q_BLOCK + NSA_WINDOW, axis=1)
        vwb = lax.dynamic_slice_in_dim(vw_pad, q0, Q_BLOCK + NSA_WINDOW, axis=1)
        pos_w = q0 - NSA_WINDOW + jnp.arange(Q_BLOCK + NSA_WINDOW)
        dist_w = tq[:, None] - pos_w[None, :]
        ok_w = (dist_w >= 0) & (dist_w < NSA_WINDOW) & (pos_w >= 0)[None, :]
        s_w = jnp.einsum('bqghd,bkgd->bghqk', qb, kwb).astype(jnp.float32) * scale
        p_w = masked_softmax(s_w - sl * dist_w.astype(jnp.float32), ok_w)
        o_w = jnp.einsum('bghqk,bkgd->bqghd', p_w.astype(vwb.dtype), vwb)
        gb = lax.dynamic_slice_in_dim(gsig, q0, Q_BLOCK, axis=1)
        o = gb[..., 0:1] * o_c + gb[..., 1:2] * o_s + gb[..., 2:3] * o_w
        return o.astype(q.dtype)

    out = lax.map(block, jnp.arange(T // Q_BLOCK))
    return out.transpose(1, 0, 2, 3, 4, 5).reshape(B, T, G * Hg * dh)

def swa_attention(q, k, v, sinks, slopes):
    B, T, H, dh = q.shape
    KV = k.shape[2]
    Hg = H // KV
    nb = T // Q_BLOCK
    scale = dh ** -0.5
    qb = q.reshape(B, nb, Q_BLOCK, KV, Hg, dh)
    pad = ((0, 0), (Q_BLOCK, 0), (0, 0), (0, 0))
    kp = jnp.pad(k, pad).reshape(B, nb + 1, Q_BLOCK, KV, dh)
    vp = jnp.pad(v, pad).reshape(B, nb + 1, Q_BLOCK, KV, dh)
    kwin = jnp.concatenate([kp[:, :-1], kp[:, 1:]], axis=2)
    vwin = jnp.concatenate([vp[:, :-1], vp[:, 1:]], axis=2)
    dist = (Q_BLOCK + np.arange(Q_BLOCK)[:, None] - np.arange(2 * Q_BLOCK)[None, :])
    kpos = np.arange(nb)[:, None] * Q_BLOCK - Q_BLOCK + np.arange(2 * Q_BLOCK)[None, :]
    valid = ((dist >= 0) & (dist < SWA_WINDOW))[None] & (kpos >= 0)[:, None, :]
    s = jnp.einsum('bnqghd,bnkgd->bnghqk', qb, kwin).astype(jnp.float32) * scale
    s = s - jnp.asarray(slopes).reshape(KV, Hg)[:, :, None, None] * dist.astype(np.float32)
    s = jnp.where(jnp.asarray(valid)[None, :, None, None], s, -jnp.inf)
    sink = jnp.broadcast_to(sinks.astype(jnp.float32).reshape(1, 1, KV, Hg, 1, 1), s.shape[:-1] + (1,))
    p = jax.nn.softmax(jnp.concatenate([s, sink], axis=-1), axis=-1)[..., :-1]
    o = jnp.einsum('bnghqk,bnkgd->bnqghd', p.astype(vwin.dtype), vwin)
    return o.reshape(B, T, H * dh)

def peer_ffn(h, wq, keys, u, v):
    B, T, D = h.shape
    q = (h @ wq).reshape(B, T, PEER_HEADS, 2, PEER_DKEY // 2)
    s = jnp.einsum('bthcd,hcnd->bthcn', q, keys).astype(jnp.float32)
    s1, i1 = lax.top_k(s[..., 0, :], PEER_TOPK)
    s2, i2 = lax.top_k(s[..., 1, :], PEER_TOPK)
    cand = (s1[..., :, None] + s2[..., None, :]).reshape(B, T, PEER_HEADS, PEER_TOPK * PEER_TOPK)
    cidx = (i1[..., :, None] * PEER_NKEYS + i2[..., None, :]).reshape(cand.shape)
    cs, ci = lax.top_k(cand, PEER_TOPK)
    eidx = jnp.take_along_axis(cidx, ci, axis=-1)
    gate = jax.nn.softmax(cs, axis=-1)
    n_tok = B * T
    n_chunk = n_tok // PEER_CHUNK
    n_sel = PEER_HEADS * PEER_TOPK
    hf = h.reshape(n_chunk, PEER_CHUNK, D)
    ef = eidx.reshape(n_chunk, PEER_CHUNK, n_sel)
    gf = gate.reshape(n_chunk, PEER_CHUNK, n_sel)

    def chunk(args):
        hc, ec, gc = args
        uc = u[ec]
        act = jax.nn.gelu(jnp.einsum('cd,ced->ce', hc, uc).astype(jnp.float32))
        vc = v[ec]
        return jnp.einsum('ce,ced->cd', (gc * act).astype(vc.dtype), vc)

    out = lax.map(chunk, (hf, ef, gf))
    return out.reshape(B, T, D).astype(h.dtype)

def setup_inputs(seed: int = 0) -> dict:
    key = jax.random.key(seed)
    ks = jax.random.split(key, 20)
    d_in = sum(split_sizes())
    hd = HEAD_DIM
    L = NSA_CMP_LEN
    nrm = lambda k, shape, s: jax.random.normal(k, shape, jnp.float32) * s
    return {
        'x': jax.random.normal(ks[0], (BATCH, SEQ, D_MODEL), jnp.float32),
        'ln1_g': 1.0 + nrm(ks[1], (DEPTH, D_MODEL), 0.02),
        'w_in': nrm(ks[2], (DEPTH, D_MODEL, d_in), D_MODEL ** -0.5),
        'cmp_pe_k': nrm(ks[3], (DEPTH, L, hd), 0.1),
        'cmp_w1_k': nrm(ks[4], (DEPTH, L * hd, NSA_CMP_HIDDEN), (L * hd) ** -0.5),
        'cmp_w2_k': nrm(ks[5], (DEPTH, NSA_CMP_HIDDEN, hd), NSA_CMP_HIDDEN ** -0.5),
        'cmp_pe_v': nrm(ks[6], (DEPTH, L, hd), 0.1),
        'cmp_w1_v': nrm(ks[7], (DEPTH, L * hd, NSA_CMP_HIDDEN), (L * hd) ** -0.5),
        'cmp_w2_v': nrm(ks[8], (DEPTH, NSA_CMP_HIDDEN, hd), NSA_CMP_HIDDEN ** -0.5),
        'swa_sinks': nrm(ks[9], (DEPTH, SWA_HEADS), 0.5),
        'w_out': nrm(ks[10], (DEPTH, D_MIX, D_MODEL), D_MIX ** -0.5),
        'ln2_g': 1.0 + nrm(ks[11], (DEPTH, D_MODEL), 0.02),
        'peer_wq': nrm(ks[12], (DEPTH, D_MODEL, PEER_HEADS * PEER_DKEY), D_MODEL ** -0.5),
        'peer_keys': nrm(ks[13], (DEPTH, PEER_HEADS, 2, PEER_NKEYS, PEER_DKEY // 2), (PEER_DKEY // 2) ** -0.5),
        'peer_u': nrm(ks[14], (DEPTH, PEER_EXPERTS, D_MODEL), D_MODEL ** -0.5),
        'peer_v': nrm(ks[15], (DEPTH, PEER_EXPERTS, D_MODEL), PEER_HEADS ** -0.5),
        'lnf_g': 1.0 + nrm(ks[16], (D_MODEL,), 0.02),
    }

def reference(x, ln1_g, w_in, cmp_pe_k, cmp_w1_k, cmp_w2_k, cmp_pe_v, cmp_w1_v, cmp_w2_v,
              swa_sinks, w_out, ln2_g, peer_wq, peer_keys, peer_u, peer_v, lnf_g):
    B, T, _ = x.shape
    hd = HEAD_DIM
    split_idx = [int(c) for c in np.cumsum(split_sizes())[:-1]]
    slopes = alibi_slopes(N_HEADS)
    swa_slopes = slopes[:SWA_HEADS]
    nsa_slopes = slopes[SWA_HEADS:]
    h = x
    for l in range(DEPTH):
        a = rms_norm(h, ln1_g[l])
        proj = a @ w_in[l]
        q_n, kc, vc, kss, vss, kw, vw, gt, q_s, k_s, v_s = jnp.split(proj, split_idx, axis=-1)
        kv4 = lambda t: t.reshape(B, T, NSA_KV, hd)
        o_n = nsa_attention(q_n.reshape(B, T, NSA_KV, NSA_GROUP, hd),
                            kv4(kc), kv4(vc), kv4(kss), kv4(vss), kv4(kw), kv4(vw),
                            gt.reshape(B, T, NSA_KV, NSA_GROUP, 3),
                            cmp_pe_k[l], cmp_w1_k[l], cmp_w2_k[l],
                            cmp_pe_v[l], cmp_w1_v[l], cmp_w2_v[l], nsa_slopes)
        o_s = swa_attention(q_s.reshape(B, T, SWA_HEADS, hd),
                            k_s.reshape(B, T, SWA_KV, hd), v_s.reshape(B, T, SWA_KV, hd),
                            swa_sinks[l], swa_slopes)
        h = h + jnp.concatenate([o_n, o_s], axis=-1) @ w_out[l]
        h = h + peer_ffn(rms_norm(h, ln2_g[l]), peer_wq[l], peer_keys[l], peer_u[l], peer_v[l])
    return rms_norm(h, lnf_g)


_drawn_inputs = setup_inputs


def setup_inputs(seed=0):
    import zlib

    import numpy as np

    out = dict(_drawn_inputs(seed))
    spreads = {}
    factors = {'ln1_g': 2.956,
     'cmp_pe_k': 5.681,
     'lnf_g': 8.181,
     'cmp_pe_v': 4.859,
     'swa_sinks': 8.0,
     'ln2_g': 5.7}
    for name, (base, spread) in spreads.items():
        noise = np.random.default_rng([zlib.crc32(name.encode()), seed]).standard_normal(out[name].shape)
        drawn = base * np.exp(spread * noise) if base else spread * noise
        out[name] = __import__('jax').numpy.asarray(drawn.astype(out[name].dtype))
    for name, factor in factors.items():
        out[name] = (out[name] * factor).astype(out[name].dtype)
    return out
```

```python
from contextlib import ExitStack

import numpy as np

import concourse.bass as bass
from concourse import mybir
from concourse.alu_op_type import AluOpType as ALU

ACT = mybir.ActivationFunctionType
AX = mybir.AxisListType
F32 = mybir.dt.float32
F32R = mybir.dt.float32r
U32 = mybir.dt.uint32

P = 128
SEQ = 512
D = 1024
KD = D // P
TT = SEQ // P
HD = 64
NSA_HEADS = SWA_HEADS = 8
PAIRS = 4
CMP_LEN, CMP_STRIDE, CMP_HID = 32, 16, 256
NCMP = (SEQ - CMP_LEN) // CMP_STRIDE + 1
LP = CMP_LEN // 2
CC = 2 * NCMP + 1
SWA_WIN = 128
PH = 8
NK = 128
TOPK = 16
SEL = PH * TOPK
EPS = 1e-6
MASKED = 1e30
CLAMP = 1e20
KV_TILES = 5
Q_TILES = 8
V_S, V_W, V_SWA, GATES = 0, 128, 256, 320
NAT = 344
BG = 4
GROUPS = NK // BG
TC = 32
HALF = D // 2


def load(eng, out, in_, sem):
    eng.dma_start(out, in_).then_inc(sem, 16)


def hold(eng, passed):
    eng.sem_inc(passed, 1)


class Mem:

    def __init__(self, nc, ctx):
        self.nc, self.ctx = nc, ctx

    def sb(self, name, shape, dt=F32):
        return self.ctx.enter_context(self.nc.sbuf_tensor(name, shape, dt))

    def ps(self, name, shape, dt=F32):
        return self.ctx.enter_context(self.nc.psum_tensor(name, shape, dt))

    def sem(self, *names):
        got = [self.ctx.enter_context(self.nc.semaphore(n)) for n in names]
        return got if len(got) > 1 else got[0]


def norm_transposed(nc, tag, src, src_ready, gain, gain_ready, ident, dst, hi=None, lo=None):
    with ExitStack() as ctx:
        m = Mem(nc, ctx)
        sq = m.sb(tag + "sq", [P, D])
        ss = m.sb(tag + "ss", [P, TT])
        ms = m.sb(tag + "ms", [P, TT])
        half = m.sb(tag + "half", [P, TT])
        rstd = m.sb(tag + "rstd", [P, TT])
        xn = m.sb(tag + "xn", [P, TT, D])
        psT = m.ps(tag + "psT", [P, 2, SEQ])
        squared, mean, rooted, scaled, turned, copied, high, low = m.sem(
            *[tag + n for n in ("squared", "mean", "rooted", "scaled", "turned", "copied", "high", "low")])
        with nc.Block() as block:

            @block.scalar
            def _(act):
                for s, v in src_ready:
                    act.wait_ge(s, v)
                for t in range(TT):
                    act.activation(sq[:, :], src[:, t, :], ACT.Square,
                                   accum_out=ss[:, t:t + 1]).then_inc(squared, 1)
                    act.wait_ge(squared, t + 1)
                for s, v in gain_ready:
                    act.wait_ge(s, v)
                for k in range(KD):
                    act.wait_ge(turned, k + 1)
                    act.activation(dst[:, k, :], psT[:, k % 2, :], ACT.Copy,
                                   scale=gain[:, k:k + 1]).then_inc(copied, 1)
                    if hi is not None:
                        act.wait_ge(copied, k + 1)
                        act.copy(hi[:, k, :], dst[:, k, :]).then_inc(high, 1)

            @block.gpsimd
            def _(pool):
                pool.memset(half[:, :], -0.5).then_inc(mean, 1)
                pool.wait_ge(squared, TT)
                pool.tensor_scalar(ms[:, :], ss[:, :], 1.0 / D, EPS, ALU.mult, ALU.add).then_inc(mean, 1)
                pool.wait_ge(mean, 2)
                pool.tensor_tensor(rstd[:, :], ms[:, :], half[:, :], ALU.pow).then_inc(rooted, 1)

            @block.vector
            def _(dve):
                for s, v in src_ready:
                    dve.wait_ge(s, v)
                dve.wait_ge(rooted, 1)
                for t in range(TT):
                    dve.tensor_scalar(xn[:, t, :], src[:, t, :], rstd[:, t:t + 1], None,
                                      ALU.mult).then_inc(scaled, 1)
                if lo is not None:
                    for k in range(KD):
                        dve.wait_ge(high, k + 1)
                        dve.tensor_tensor(lo[:, k, :], dst[:, k, :], hi[:, k, :].bitcast(F32),
                                          ALU.subtract).then_inc(low, 1)

            @block.tensor
            def _(pe):
                for s, v in gain_ready:
                    pe.wait_ge(s, v)
                pe.wait_ge(scaled, TT)
                for k in range(KD):
                    if k >= 2:
                        pe.wait_ge(copied, k - 1)
                    for t in range(TT):
                        mm = pe.transpose(psT[:, k % 2, t * P:(t + 1) * P], xn[:, t, k * P:(k + 1) * P],
                                          ident[:, :])
                    mm.then_inc(turned, 1)


def pe_softmax_steps(pe, i, steps, b):
    N = len(steps)
    for n in range(N + 2):
        if n < N:
            s = steps[n]
            if n >= 2:
                pe.wait_ge(b.shifted, i * N + n - 1)
            pe.matmul(b.psS[:, n % 2, 0:s.width], s.q, s.k, start=True, stop=True).then_inc(b.scored, 1)
        if b.between and n in b.between:
            b.between[n](pe)
        if 1 <= n <= N:
            s = steps[n - 1]
            pe.wait_ge(b.expd, i * N + n)
            if n - 1 >= 2:
                pe.wait_ge(b.copied[(n - 1) % 2], i * (N // 2) + (n - 1) // 2)
            for c in range(s.width // P):
                mm = pe.transpose(b.psT[:, (n - 1) % 2, c * P:(c + 1) * P],
                                  b.S[:, (n - 1) % 3, c * P:(c + 1) * P], b.ident[:, :])
            mm.then_inc(b.turned, 1)
        if n >= 2:
            s, r = steps[n - 2], n - 2
            pe.wait_ge(b.copied[r % 2], i * (N // 2) + r // 2 + 1)
            if r % 4 == 0 and r >= 8:
                pe.wait_ge(b.taken, i * b.phases + r // 4 - 1)
            for c in range(s.width // P):
                mm = pe.matmul(b.psO[:, (r // 4) % 2, (r % 4) * HD:(r % 4 + 1) * HD],
                               b.PT[:, r % 2, c * P:(c + 1) * P], s.v[c],
                               start=(c == 0), stop=(c == s.width // P - 1))
            mm.then_inc(b.weighed, 1)


def act_softmax_step(act, i, n, steps, b):
    N = len(steps)
    if n < N:
        s = steps[n]
        act.wait_ge(b.shifted, i * N + n + 1)
        act.activation(b.S[:, n % 3, 0:s.width], b.S[:, n % 3, 0:s.width], ACT.Exp,
                       bias=b.nmax[:, n:n + 1], scale=-1.0, accum_out=b.sums[:, n:n + 1]).then_inc(b.expd, 1)
    r = n - 1
    if 0 <= r < N and r % 2 == 0:
        act.wait_ge(b.turned, i * N + r + 1)
        if r >= 2:
            act.wait_ge(b.weighed, i * N + r - 1)
        act.copy(b.PT[:, 0, 0:steps[r].width], b.psT[:, 0, 0:steps[r].width]).then_inc(b.copied[0], 1)


def dve_softmax_step(dve, i, n, steps, b):
    N = len(steps)
    if n < N:
        s = steps[n]
        dve.wait_ge(b.scored, i * N + n + 1)
        if n >= 3:
            dve.wait_ge(b.turned, i * N + n - 2)
        hold(dve, b.passed)
        dve.tensor_tensor_reduce(b.S[:, n % 3, 0:s.width], s.bias, b.psS[:, n % 2, 0:s.width], 1.0,
                                 s.start, ALU.add, ALU.min, b.nmax[:, n:n + 1]).then_inc(b.shifted, 1)
    r = n - 1
    if 0 <= r < N and r % 2 == 1:
        dve.wait_ge(b.turned, i * N + r + 1)
        if r >= 2:
            dve.wait_ge(b.weighed, i * N + r - 1)
        dve.tensor_copy(b.PT[:, 1, 0:steps[r].width], b.psT[:, 1, 0:steps[r].width]).then_inc(b.copied[1], 1)


class Step:
    def __init__(self, width, q, k, v, bias, start):
        self.width, self.q, self.k, self.v, self.bias, self.start = width, q, k, v, bias, start


class Bundle:

    def __init__(self, m, tag, n, phases, psS, psT, psO, ident):
        self.tag = tag
        self.phases, self.psS, self.psT, self.psO, self.ident = phases, psS, psT, psO, ident
        self.S = m.sb(tag + "S", [P, 3, SEQ])
        self.PT = m.sb(tag + "PT", [P, 2, SEQ])
        self.nmax = m.sb(tag + "nmax", [P, n])
        self.sums = m.sb(tag + "sums", [P, n])
        self.scored, self.shifted, self.expd, self.turned, c0, c1, self.weighed, self.taken = m.sem(
            *[tag + x for x in ("scored", "shifted", "expd", "turned", "copied0", "copied1", "weighed", "taken")])
        self.copied = [c0, c1]
        self.passed = m.sem(tag + "passed")
        self.between = {}


def attention(nc, m, aT, ident, oT, w):
    wt = m.sb("wt", [P, 2, KD, P])
    ksT = m.sb("ksT", [P, SEQ])
    kwT = m.sb("kwT", [P, SEQ])
    kdT = m.sb("kdT", [P, SEQ])
    nat = m.sb("nat", [P, TT, NAT])
    gsig = m.sb("gsig", [P, TT, 3, NSA_HEADS])
    kcT = m.sb("kcT", [P, NCMP])
    vcn = m.sb("vcn", [NCMP, 2, HD])
    Tbase = m.sb("Tbase", [P, SEQ])
    Tcmp = m.sb("Tcmp", [P, TT, NCMP])
    Tswa = m.sb("Tswa", [P, 2 * P])
    slopes = m.sb("slopes", [P, 2 * NSA_HEADS])
    sinks = m.sb("sinks", [P, SWA_HEADS])
    nsink = m.sb("nsink", [P, SWA_HEADS])
    tables, nsinked = m.sem("tables", "nsinked")

    with ExitStack() as ctx:
        k = Mem(nc, ctx)
        wn = k.sb("wn", [P, KD, NAT])
        X = k.sb("X", [P, 2, LP, CC])
        w1 = k.sb("w1", [P, 2, LP, CMP_HID])
        w2 = k.sb("w2", [P, 2, 2, HD])
        pe_sb = k.sb("pe_sb", [P, 2, LP])
        cb = k.sb("cb", [P, 4])
        hid = k.sb("hid", [P, 4, 2 * NCMP])
        ge = k.sb("ge", [P, TT, 3 * NSA_HEADS])
        psA = k.ps("psA", [P, 2, 512])
        psN = k.ps("psN", [P, 2, 512])
        psH = k.ps("psH", [P, 2, 512])
        psK = k.ps("psK", [P, 512])
        psV = k.ps("psV", [P, 512])
        wt_in = k.sem("wt_in0", "wt_in1")
        wn_in, w1_in, w2_in, pe_in = k.sem("wn_in", "w1_in", "w2_in", "pe_in")
        (projected, kept, keptx, pe_put, natured, nat_kept, gexp, gadd, gdone, hidden, bias_put, gelud,
         kc_made, kc_kept) = k.sem("projected", "kept", "keptx", "pe_put", "natured", "nat_kept", "gexp", "gadd",
                                   "gdone", "hidden", "bias_put", "gelud", "kc_made", "kc_kept")
        with nc.Block() as block:

            @block.sync
            def _(sp):
                for n in range(KV_TILES):
                    if n >= 2:
                        sp.wait_ge(projected, n - 1)
                    load(sp, wt[:, n % 2], w["w_tiles"][n].rearrange("p (k c) -> p k c", k=KD), wt_in[n % 2])
                    if n == 1:
                        load(sp, pe_sb[:, :, :], w["pe"].rearrange("p (a l) -> p a l", a=2), pe_in)
                        load(sp, w1[:, :, :, :], w["w1"].rearrange("p (a l c) -> p a l c", a=2, l=LP), w1_in)
                load(sp, wn[:, :, :], w["w_nat"].rearrange("p (k c) -> p k c", k=KD), wn_in)
                load(sp, w2[:, :, :, :], w["w2"].rearrange("p (a l c) -> p a l c", a=2, l=2), w2_in)
                load(sp, Tbase[:, :], w["t_nsa"], tables)
                load(sp, Tcmp[:, :, :], w["t_cmp"].rearrange("p (a c) -> p a c", a=TT), tables)
                load(sp, Tswa[:, :], w["t_swa"], tables)
                load(sp, slopes[:, :], w["slopes"], tables)
                load(sp, sinks[:, :], w["sinks"].partition_broadcast(P), tables)

            @block.tensor
            def _(pe):
                for n in range(KV_TILES):
                    pe.wait_ge(wt_in[n % 2], 16 * (n // 2 + 1))
                    if n >= 2:
                        pe.wait_ge(keptx if n == 3 else kept, 9 if n == 4 else 8)
                    for c in range(KD):
                        mm = pe.matmul(psA[:, n % 2, :], wt[:, n % 2, c, :], aT[:, c, :],
                                       start=(c == 0), stop=(c == KD - 1))
                    mm.then_inc(projected, 1)
                pe.wait_ge(keptx, 8)
                pe.wait_ge(kept, 8)
                pe.wait_ge(pe_put, 1)
                pe.wait_ge(w1_in, 16)
                for kv in range(2):
                    for hc in range(2):
                        for lp in range(LP):
                            mm = pe.matmul(psH[:, kv, hc * 64:hc * 64 + CC], w1[:, kv, lp, hc * P:(hc + 1) * P],
                                           X[:, kv, lp, :], start=(lp == 0), stop=(lp == LP - 1))
                        mm.then_inc(hidden, 1)
                pe.wait_ge(wn_in, 16)
                for t in range(TT):
                    if t >= 2:
                        pe.wait_ge(nat_kept, t - 1)
                    for c in range(KD):
                        mm = pe.matmul(psN[:, t % 2, 0:NAT], aT[:, c, t * P:(t + 1) * P], wn[:, c, :],
                                       start=(c == 0), stop=(c == KD - 1))
                    mm.then_inc(natured, 1)
                pe.wait_ge(gelud, 4)
                pe.wait_ge(w2_in, 16)
                for g in range(2):
                    for hc in range(2):
                        mm = pe.matmul(psK[g * HD:(g + 1) * HD, 0:NCMP], w2[:, 0, hc, :],
                                       hid[:, hc, g * NCMP:(g + 1) * NCMP], start=(hc == 0), stop=(hc == 1))
                mm.then_inc(kc_made, 1)
                for g in range(2):
                    for hc in range(2):
                        mm = pe.matmul(psV[0:NCMP, g * HD:(g + 1) * HD],
                                       hid[:, 2 + hc, g * NCMP:(g + 1) * NCMP], w2[:, 1, hc, :],
                                       start=(hc == 0), stop=(hc == 1))
                mm.then_inc(kc_made, 1)

            def spread(copy, kv, par, done):
                for g in range(2):
                    for q in range(2):
                        raw = psA[g * HD:(g + 1) * HD, kv, :].rearrange("p (n l a) -> p a l n", a=2, l=LP // 2)
                        copy(X[par * HD:(par + 1) * HD, kv, q * 8:(q + 1) * 8, g * NCMP:(g + 1) * NCMP],
                             raw[:, par, :, q:q + NCMP]).then_inc(done, 1)

            @block.scalar
            def _(act):
                act.wait_ge(projected, 1)
                spread(act.copy, 0, 0, kept)
                spread(act.copy, 0, 1, kept)
                for n, dst in ((2, ksT), (3, kwT), (4, kdT)):
                    act.wait_ge(projected, n + 1)
                    act.copy(dst[:, :], psA[:, n % 2, :]).then_inc(kept, 1)
                for j in range(4):
                    act.wait_ge(bias_put, 2 * (j // 2) + 2)
                    act.activation(hid[:, j, :], psH[:, j // 2, (j % 2) * 64:(j % 2) * 64 + 2 * NCMP],
                                   ACT.Gelu_apprx_tanh, bias=cb[:, j:j + 1]).then_inc(gelud, 1)
                act.wait_ge(nat_kept, TT)
                act.activation(ge[:, :, :], nat[:, :, GATES:NAT], ACT.Exp, scale=-1.0).then_inc(gexp, 1)

            @block.vector
            def _(dve):
                dve.wait_ge(pe_in, 16)
                dve.tensor_copy(X[:, :, :, CC - 1], pe_sb[:, :, :]).then_inc(pe_put, 1)
                dve.wait_ge(projected, 2)
                spread(dve.tensor_copy, 1, 0, keptx)
                spread(dve.tensor_copy, 1, 1, keptx)
                for j in range(4):
                    dve.wait_ge(hidden, 2 * (j // 2) + 2)
                    dve.tensor_copy(cb[:, j:j + 1],
                                    psH[:, j // 2, (j % 2) * 64 + CC - 1:(j % 2) * 64 + CC]).then_inc(bias_put, 1)
                for t in range(TT):
                    dve.wait_ge(natured, t + 1)
                    dve.tensor_copy(nat[:, t, :], psN[:, t % 2, 0:NAT]).then_inc(nat_kept, 1)
                dve.wait_ge(gexp, 1)
                dve.tensor_scalar(ge[:, :, :], ge[:, :, :], 1.0, None, ALU.add).then_inc(gadd, 1)
                dve.wait_ge(gadd, 1)
                dve.reciprocal(gsig[:, :, :, :], ge[:, :, :].rearrange("p t (c h) -> p t c h", c=3)).then_inc(gdone, 1)
                dve.wait_ge(kc_made, 1)
                dve.tensor_copy(kcT[:, :], psK[:, 0:NCMP]).then_inc(kc_kept, 1)
                dve.wait_ge(kc_made, 2)
                dve.tensor_copy(vcn[:, :, :], psV[0:NCMP, 0:P].rearrange("p (g d) -> p g d", g=2)).then_inc(kc_kept, 1)
                dve.wait_ge(tables, 80)
                dve.tensor_scalar(nsink[:, :], sinks[:, :], -1.0, None, ALU.mult).then_inc(nsinked, 1)

    with ExitStack() as ctx:
        k = Mem(nc, ctx)
        qT = k.sb("qT", [P, SEQ])
        Th = k.sb("Th", [P, 2, SEQ])
        Tc = k.sb("Tc", [P, 2, TT, NCMP])
        gp = k.sb("gp", [P, 3, 2, TT])
        fac = k.sb("fac", [P, 6, TT])
        Sc = k.sb("Sc", [P, 2, TT, NCMP])
        cmin = k.sb("cmin", [P, 2 * TT])
        csum = k.sb("csum", [P, 2 * TT])
        PTc = k.sb("PTc", [NCMP, 2, TT, P])
        part = k.sb("part", [P, TT, HD])
        op = k.sb("op", [P, TT, 2, HD])
        psS = k.ps("psS", [P, 2, 512])
        psT = k.ps("psT", [P, 2, 512])
        psO = k.ps("psO", [P, 2, 512])
        psC = k.ps("psC", [P, 2, 512])
        b = Bundle(k, "n_", 16, 6, psS, psT, psO, ident)
        (wt_in, q_made, q_kept, biased, c_scored, c_chain, c_exp, c_turned, c_copied, c_weighed, facs, o_part,
         o_turned, o_kept, c_sum) = k.sem("nwt_in", "q_made", "q_kept", "biased", "c_scored", "c_chain", "c_exp",
                                          "c_turned", "c_copied", "c_weighed", "facs", "o_part", "o_turned",
                                          "o_kept", "c_sum")
        steps = []
        for hh in range(2):
            r = slice(hh * HD, (hh + 1) * HD)
            for kT, voff in ((ksT, V_S), (kwT, V_W)):
                for t in range(TT):
                    width = (t + 1) * P
                    steps.append(Step(width, qT[r, t * P:(t + 1) * P], kT[r, 0:width],
                                      [nat[:, c, voff + hh * HD:voff + (hh + 1) * HD] for c in range(t + 1)],
                                      Th[:, hh, SEQ - width:SEQ], CLAMP))
        N = len(steps)
        with nc.Block() as block:

            @block.sync
            def _(sp):
                with sp.Fori(0, PAIRS) as i:
                    sp.wait_ge(q_made, i)
                    load(sp, wt[:, 0], w["w_tiles"][bass.ds(i + KV_TILES, 1)].rearrange(
                        "a p (k c) -> p (a k) c", k=KD), wt_in)

            @block.tensor
            def _(pe):
                with pe.Fori(0, PAIRS) as i:
                    pe.wait_ge(wt_in, i * 16 + 16)
                    pe.wait_ge(o_kept, i)
                    for c in range(KD):
                        mm = pe.matmul(psC[:, 0, :], wt[:, 0, c, :], aT[:, c, :], start=(c == 0), stop=(c == KD - 1))
                    mm.then_inc(q_made, 1)
                    pe.wait_ge(q_kept, i + 1)
                    for hh in range(2):
                        r = slice(hh * HD, (hh + 1) * HD)
                        for t in range(TT):
                            mm = pe.matmul(psC[:, hh, t * NCMP:(t + 1) * NCMP], qT[r, t * P:(t + 1) * P], kcT[r, :],
                                           start=True, stop=True)
                        mm.then_inc(c_scored, 1)

                    def turn_compressed(pe):
                        pe.wait_ge(c_exp, i + 1)
                        for hh in range(2):
                            for t in range(TT):
                                mm = pe.transpose(psC[0:NCMP, hh, t * P:(t + 1) * P], Sc[:, hh, t, :], ident[:, :])
                            mm.then_inc(c_turned, 1)

                    b.between = {8: turn_compressed}
                    pe_softmax_steps(pe, i, steps, b)
                    for hh in range(2):
                        pe.wait_ge(c_copied, i * 2 + hh + 1)
                        pe.wait_ge(b.taken, i * 6 + hh + 3)
                        for t in range(TT):
                            mm = pe.matmul(psO[:, hh, t * HD:(t + 1) * HD], PTc[:, hh, t, :], vcn[:, hh, :],
                                           start=True, stop=True)
                        mm.then_inc(c_weighed, 1)
                    pe.wait_ge(b.taken, i * 6 + 6)
                    for t in range(TT):
                        mm = pe.transpose(psC[:, 0, t * P:(t + 1) * P], op[:, t, :, :], ident[:, :])
                    mm.then_inc(o_turned, 1)

            @block.scalar
            def _(act):
                with act.Fori(0, PAIRS) as i:
                    act.wait_ge(q_made, i + 1)
                    act.activation(qT[:, :], psC[:, 0, :], ACT.Copy, scale=-(HD ** -0.5)).then_inc(q_kept, 1)
                    for n in range(N + 1):
                        act_softmax_step(act, i, n, steps, b)
                        if n == 4:
                            act.wait_ge(c_chain, i * 4 + 4)
                            act.activation(Sc[:, :, :, :], Sc[:, :, :, :], ACT.Exp, scale=-1.0).then_inc(c_exp, 1)
                        if n == 10:
                            for hh in range(2):
                                act.wait_ge(c_turned, i * 2 + hh + 1)
                                act.copy(PTc[:, hh, :, :], psC[0:NCMP, hh, :].rearrange("p (t q) -> p t q", t=TT)
                                         ).then_inc(c_copied, 1)
                    act.wait_ge(o_turned, i + 1)
                    act.copy(oT[:, bass.ds(i, 1), :].rearrange("p a t -> p (a t)"), psC[:, 0, :]).then_inc(o_kept, 1)

            @block.vector
            def _(dve):
                with dve.Fori(0, PAIRS) as i:
                    for hh in range(2):
                        s = slopes[:, bass.ds(i + 8 + 4 * hh, 1)]
                        dve.tensor_scalar(Th[:, hh, :], Tbase[:, :], s, None, ALU.mult).then_inc(biased, 1)
                        dve.tensor_scalar(Tc[:, hh, :, :], Tcmp[:, :, :], s, None, ALU.mult).then_inc(biased, 1)
                        dve.tensor_copy(gp[:, :, hh, :], gsig[:, :, :, bass.ds(i + 4 * hh, 1)].rearrange(
                            "p t c a -> p c (t a)")).then_inc(biased, 1)
                    dve.wait_ge(biased, i * 6 + 6)

                    def compressed():
                        dve.wait_ge(c_scored, i * 2 + 1)
                        dve.tensor_tensor(Sc[:, 0, :, :], Tc[:, 0, :, :],
                                          psC[:, 0, 0:TT * NCMP].rearrange("p (t n) -> p t n", t=TT),
                                          ALU.add).then_inc(c_chain, 1)
                        dve.wait_ge(c_scored, i * 2 + 2)
                        dve.tensor_tensor(Sc[:, 1, :, :], Tc[:, 1, :, :],
                                          psC[:, 1, 0:TT * NCMP].rearrange("p (t n) -> p t n", t=TT),
                                          ALU.add).then_inc(c_chain, 1)
                        dve.wait_ge(c_chain, i * 4 + 2)
                        flat = Sc[:, :, :, :].rearrange("p h t n -> p (h t) n")
                        dve.tensor_reduce(cmin[:, :], flat, AX.X, ALU.min).then_inc(c_sum, 1)
                        dve.wait_ge(c_sum, i * 4 + 1)
                        dve.tensor_scalar(cmin[:, :], cmin[:, :], CLAMP, None, ALU.min).then_inc(c_chain, 1)
                        dve.wait_ge(c_chain, i * 4 + 3)
                        dve.tensor_tensor(flat, flat, cmin[:, :].unsqueeze(2).to_broadcast([P, 2 * TT, NCMP]),
                                          ALU.subtract).then_inc(c_chain, 1)

                    def factor(phase, sums, done):
                        c, hh = ((1, 2)[phase % 2], phase // 2) if phase < 4 else (0, phase - 4)
                        f = fac[:, phase, :]
                        dve.tensor_scalar(f, sums, 1e-30, None, ALU.max).then_inc(facs, 1)
                        dve.wait_ge(facs, i * 18 + 3 * phase + 1)
                        dve.reciprocal(f, f).then_inc(facs, 1)
                        dve.wait_ge(facs, i * 18 + 3 * phase + 2)
                        dve.tensor_tensor(f, f, gp[:, c, hh, :], ALU.mult).then_inc(facs, 1)
                        dve.wait_ge(facs, i * 18 + 3 * phase + 3)
                        return f.unsqueeze(2).to_broadcast([P, TT, HD]), hh

                    def take(phase, bank, sums, first):
                        f, hh = factor(phase, sums, b.taken)
                        o = psO[:, bank, 0:TT * HD].rearrange("p (t d) -> p t d", t=TT)
                        if first:
                            dve.tensor_tensor(op[:, :, hh, :], f, o, ALU.mult).then_inc(b.taken, 1)
                        else:
                            if phase != 1:
                                dve.wait_ge(b.taken, i * 6 + phase)
                            dve.tensor_tensor(part[:, :, :], f, o, ALU.mult).then_inc(o_part, 1)
                            dve.wait_ge(o_part, i * 4 + {1: 1, 3: 2, 4: 3, 5: 4}[phase])
                            dve.wait_ge(b.taken, i * 6 + phase)
                            dve.tensor_tensor(op[:, :, hh, :], op[:, :, hh, :], part[:, :, :],
                                              ALU.add).then_inc(b.taken, 1)

                    for n in range(N + 2):
                        dve_softmax_step(dve, i, n, steps, b)
                        if n == 2:
                            compressed()
                        if n >= 6 and (n - 6) % 4 == 0 and n < N + 2:
                            ph = (n - 6) // 4
                            if ph < 3:
                                dve.wait_ge(b.weighed, i * N + 4 * ph + 4)
                                take(ph, ph % 2, b.sums[:, 4 * ph:4 * ph + 4], ph % 2 == 0)
                    dve.wait_ge(c_exp, i + 1)
                    dve.tensor_reduce(csum[:, :], Sc[:, :, :, :].rearrange("p h t n -> p (h t) n"), AX.X,
                                      ALU.add).then_inc(c_sum, 1)
                    dve.wait_ge(b.weighed, i * N + 16)
                    take(3, 1, b.sums[:, 12:16], False)
                    for hh in range(2):
                        dve.wait_ge(c_sum, i * 4 + 2)
                        dve.wait_ge(c_weighed, i * 2 + hh + 1)
                        take(4 + hh, hh, csum[:, hh * TT:(hh + 1) * TT], False)
                    dve.tensor_scalar(cmin[:, 0:1], cmin[:, 0:1], 1.0, None, ALU.mult).then_inc(c_sum, 2)

    with ExitStack() as ctx:
        k = Mem(nc, ctx)
        qT = k.sb("sqT", [P, SEQ])
        Th = k.sb("sTh", [P, 2, 2 * P])
        ns = k.sb("ns", [P, 2])
        fac = k.sb("sfac", [P, 2, TT])
        es = k.sb("es", [P, 2, TT])
        op = k.sb("sop", [P, TT, 2, HD])
        psS = k.ps("spsS", [P, 2, 512])
        psT = k.ps("spsT", [P, 2, 512])
        psO = k.ps("spsO", [P, 2, 512])
        psC = k.ps("spsC", [P, 512])
        b = Bundle(k, "s_", 8, 2, psS, psT, psO, ident)
        wt_in, q_made, q_kept, biased, s_chain, s_exp, o_turned, o_kept = k.sem(
            "swt_in", "sq_made", "sq_kept", "sbiased", "s_chain", "s_exp", "so_turned", "so_kept")
        steps = []
        for hh in range(2):
            r = slice(hh * HD, (hh + 1) * HD)
            for t in range(TT):
                k0 = max(t - 1, 0)
                width = (t + 1 - k0) * P
                steps.append(Step(width, qT[r, t * P:(t + 1) * P], kdT[r, k0 * P:k0 * P + width],
                                  [nat[:, c, V_SWA:V_SWA + HD] for c in range(k0, t + 1)],
                                  Th[:, hh, 2 * P - width:2 * P], ns[:, hh:hh + 1]))
        N = len(steps)
        with nc.Block() as block:

            @block.sync
            def _(sp):
                with sp.Fori(0, PAIRS) as i:
                    sp.wait_ge(q_made, i)
                    load(sp, wt[:, 0], w["w_tiles"][bass.ds(i + KV_TILES + PAIRS, 1)].rearrange(
                        "a p (k c) -> p (a k) c", k=KD), wt_in)

            @block.tensor
            def _(pe):
                with pe.Fori(0, PAIRS) as i:
                    pe.wait_ge(wt_in, i * 16 + 16)
                    pe.wait_ge(o_kept, i)
                    for c in range(KD):
                        mm = pe.matmul(psC[:, :], wt[:, 0, c, :], aT[:, c, :], start=(c == 0), stop=(c == KD - 1))
                    mm.then_inc(q_made, 1)
                    pe.wait_ge(q_kept, i + 1)
                    pe_softmax_steps(pe, i, steps, b)
                    pe.wait_ge(b.taken, i * 2 + 2)
                    for t in range(TT):
                        mm = pe.transpose(psC[:, t * P:(t + 1) * P], op[:, t, :, :], ident[:, :])
                    mm.then_inc(o_turned, 1)

            @block.scalar
            def _(act):
                with act.Fori(0, PAIRS) as i:
                    act.wait_ge(q_made, i + 1)
                    act.activation(qT[:, :], psC[:, :], ACT.Copy, scale=-(HD ** -0.5)).then_inc(q_kept, 1)
                    for n in range(N + 1):
                        act_softmax_step(act, i, n, steps, b)
                    act.wait_ge(s_chain, i * 5 + 1)
                    act.activation(es[:, :, :], es[:, :, :], ACT.Exp).then_inc(s_exp, 1)
                    act.wait_ge(o_turned, i + 1)
                    act.copy(oT[:, bass.ds(i + PAIRS, 1), :].rearrange("p a t -> p (a t)"), psC[:, :]).then_inc(o_kept, 1)

            @block.vector
            def _(dve):
                with dve.Fori(0, PAIRS) as i:
                    for hh in range(2):
                        dve.tensor_scalar(Th[:, hh, :], Tswa[:, :], slopes[:, bass.ds(i * 2 + hh, 1)], None,
                                          ALU.mult).then_inc(biased, 1)
                    dve.tensor_copy(ns[:, :], nsink[:, bass.ds(i * 2, 2)]).then_inc(biased, 1)
                    dve.wait_ge(biased, i * 3 + 3)
                    for n in range(N + 1):
                        dve_softmax_step(dve, i, n, steps, b)
                    dve.wait_ge(b.shifted, i * N + N)
                    dve.tensor_tensor(es[:, :, :], b.nmax[:, :].rearrange("p (h t) -> p h t", h=2),
                                      ns[:, :].unsqueeze(2).to_broadcast([P, 2, TT]),
                                      ALU.subtract).then_inc(s_chain, 1)
                    dve.wait_ge(s_exp, i + 1)
                    dve.wait_ge(b.expd, i * N + N)
                    dve.tensor_tensor(fac[:, :, :], es[:, :, :], b.sums[:, :].rearrange("p (h t) -> p h t", h=2),
                                      ALU.add).then_inc(s_chain, 1)
                    dve.wait_ge(s_chain, i * 5 + 2)
                    dve.reciprocal(fac[:, :, :], fac[:, :, :]).then_inc(s_chain, 3)
                    dve.wait_ge(s_chain, i * 5 + 5)
                    dve.wait_ge(b.weighed, i * N + N)
                    for hh in range(2):
                        dve.tensor_tensor(op[:, :, hh, :], fac[:, hh, :].unsqueeze(2).to_broadcast([P, TT, HD]),
                                          psO[:, hh, 0:TT * HD].rearrange("p (t d) -> p t d", t=TT),
                                          ALU.mult).then_inc(b.taken, 1)


def project_out(nc, oT, acc, w):
    with ExitStack() as ctx:
        m = Mem(nc, ctx)
        wo = m.sb("wo", [P, KD, D])
        ps = m.ps("psW", [P, 4, 512])
        wo_in = m.sem("wo_in0", "wo_in1")
        made, added = m.sem("wo_made", "wo_added")
        with nc.Block() as block:

            @block.sync
            def _(sp):
                for c in range(2):
                    load(sp, wo[:, c * 4:(c + 1) * 4, :],
                         w["w_out"][:, c * 4 * D:(c + 1) * 4 * D].rearrange("p (k n) -> p k n", n=D), wo_in[c])

            @block.tensor
            def _(pe):
                for n in range(2 * TT):
                    t, h = n // 2, n % 2
                    if n >= 4:
                        pe.wait_ge(added, n - 3)
                    for c in range(KD):
                        if n == 0 and c % 4 == 0:
                            pe.wait_ge(wo_in[c // 4], 16)
                        mm = pe.matmul(ps[:, n % 4, :], oT[:, c, t * P:(t + 1) * P],
                                       wo[:, c, h * HALF:(h + 1) * HALF], start=(c == 0), stop=(c == KD - 1))
                    mm.then_inc(made, 1)

            @block.vector
            def _(dve):
                for n in range(2 * TT):
                    t, h = n // 2, n % 2
                    dve.wait_ge(made, n + 1)
                    a = acc[:, t, h * HALF:(h + 1) * HALF]
                    dve.tensor_tensor(a, a, ps[:, n % 4, :], ALU.add).then_inc(added, 1)


def choose_experts(nc, hT, iota, sel_w, sel_e, w):
    with ExitStack() as ctx:
        m = Mem(nc, ctx)
        wq = m.sb("wq", [P, 2, KD, P])
        keys = m.sb("keys", [P, 2, NK])
        qp = m.sb("qp", [P, 2, SEQ])
        sc = m.sb("sc", [P, 2, TT, NK])
        rest = m.sb("rest", [P, 2, TT, NK])
        top = m.sb("top", [P, 2, TT, TOPK])
        at = m.sb("at", [P, 2, TT, TOPK], U32)
        atf = m.sb("atf", [P, 2, TT, TOPK])
        cand = m.sb("cand", [P, TT, TOPK * TOPK])
        crest = m.sb("crest", [P, TT, TOPK * TOPK])
        best = m.sb("best", [P, TT, TOPK])
        cat = m.sb("cat", [P, TT, TOPK], U32)
        ab = m.sb("ab", [P, 2, TT, TOPK], U32)
        abf = m.sb("abf", [P, 2, TT, TOPK])
        eq = m.sb("eq", [P, 2 * TT, TOPK, TOPK])
        gsum = m.sb("gsum", [P, TT * PH])
        psQ = m.ps("psQ", [P, 2, 512])
        psS = m.ps("psS2", [P, 2, TT, NK])
        wq_in = m.sem("wq_in0", "wq_in1")
        passed = m.sem("e_passed")
        (keys_in, q_made, q_kept, s_made, s_kept, max1, cut1, max2, at2, cands, cmax1, ccut1, cmax2, cat2, split,
         fl, eqd, mulled, picked, g1) = m.sem(
            "keys_in", "pq_made", "pq_kept", "ps_made", "ps_kept", "max1", "cut1", "max2", "at2", "cands", "cmax1",
            "ccut1", "cmax2", "cat2", "split", "fl", "eqd", "mulled", "picked", "g1")
        with nc.Block() as block:

            @block.sync
            def _(sp):
                with sp.Fori(0, PH) as h:
                    for c in range(2):
                        sp.wait_ge(q_made, h * 2)
                        load(sp, wq[:, c], w["wq"][bass.ds(h * 2 + c, 1)].rearrange(
                            "a p (k c) -> p (a k) c", k=KD), wq_in[c])
                    sp.wait_ge(s_made, h * 2)
                    load(sp, keys[:, :, :], w["keys"][bass.ds(h, 1)].rearrange(
                        "a p (c n) -> p (a c) n", c=2), keys_in)

            @block.tensor
            def _(pe):
                with pe.Fori(0, PH) as h:
                    for c in range(2):
                        pe.wait_ge(wq_in[c], h * 16 + 16)
                        for k in range(KD):
                            mm = pe.matmul(psQ[:, c, :], wq[:, c, k, :], hT[:, k, :],
                                           start=(k == 0), stop=(k == KD - 1))
                        mm.then_inc(q_made, 1)
                    pe.wait_ge(keys_in, h * 16 + 16)
                    for c in range(2):
                        pe.wait_ge(q_kept, h * 2 + c + 1)
                        pe.wait_ge(s_kept, h * 2)
                        for t in range(TT):
                            mm = pe.matmul(psS[:, c, t, :], qp[:, c, t * P:(t + 1) * P], keys[:, c, :],
                                           start=True, stop=True)
                        mm.then_inc(s_made, 1)

            @block.scalar
            def _(act):
                with act.Fori(0, PH) as h:
                    for c in range(2):
                        act.wait_ge(s_made, h * 2)
                        act.wait_ge(q_made, h * 2 + c + 1)
                        act.copy(qp[:, c, :], psQ[:, c, :]).then_inc(q_kept, 1)
                    act.wait_ge(cut1, h * 16)
                    for c in range(2):
                        act.wait_ge(s_made, h * 2 + c + 1)
                        act.copy(sc[:, c, :, :], psS[:, c, :, :]).then_inc(s_kept, 1)

                act.wait_ge(g1, 1)
                act.activation(sel_w[:, :, :], sel_w[:, :, :], ACT.Exp).then_inc(g1, 1)

            @block.gpsimd
            def _(pool):
                with pool.Fori(0, PH) as h:
                    pool.wait_ge(eqd, h + 1)
                    for c in range(2):
                        for t in range(TT):
                            e = eq[:, c * TT + t, :, :]
                            pool.tensor_tensor(e, e, atf[:, c, t, :].unsqueeze(1).to_broadcast([P, TOPK, TOPK]),
                                               ALU.mult).then_inc(mulled, 1)

            @block.vector
            def _(dve):
                ct = [(c, t) for c in range(2) for t in range(TT)]
                with dve.Fori(0, PH) as h:
                    for c, t in ct:
                        if t == 0:
                            dve.wait_ge(s_kept, h * 2 + c + 1)
                            hold(dve, passed)
                        dve.max(top[:, c, t, 0:8], sc[:, c, t, :]).then_inc(max1, 1)
                    dve.wait_ge(max1, h * 8 + 8)
                    hold(dve, passed)
                    for c, t in ct:
                        dve.max_index(at[:, c, t, 0:8], top[:, c, t, 0:8], sc[:, c, t, :]).then_inc(cut1, 1)
                        dve.match_replace(rest[:, c, t, :], top[:, c, t, 0:8], sc[:, c, t, :],
                                          -3.0e38).then_inc(cut1, 1)
                    dve.wait_ge(cut1, h * 16 + 16)
                    hold(dve, passed)
                    for c, t in ct:
                        dve.max(top[:, c, t, 8:16], rest[:, c, t, :]).then_inc(max2, 1)
                    dve.wait_ge(max2, h * 8 + 8)
                    dve.tensor_tensor(cand[:, :, :].rearrange("p t (a b) -> p t a b", a=TOPK),
                                      top[:, 0].unsqueeze(3).to_broadcast([P, TT, TOPK, TOPK]),
                                      top[:, 1].unsqueeze(2).to_broadcast([P, TT, TOPK, TOPK]),
                                      ALU.add).then_inc(cands, 1)
                    for c, t in ct:
                        dve.max_index(at[:, c, t, 8:16], top[:, c, t, 8:16], rest[:, c, t, :]).then_inc(at2, 1)
                    dve.wait_ge(cands, h + 1)
                    hold(dve, passed)
                    for t in range(TT):
                        dve.max(best[:, t, 0:8], cand[:, t, :]).then_inc(cmax1, 1)
                    dve.wait_ge(cmax1, h * 4 + 4)
                    hold(dve, passed)
                    for t in range(TT):
                        dve.max_index(cat[:, t, 0:8], best[:, t, 0:8], cand[:, t, :]).then_inc(ccut1, 1)
                        dve.match_replace(crest[:, t, :], best[:, t, 0:8], cand[:, t, :], -3.0e38).then_inc(ccut1, 1)
                    dve.wait_ge(at2, h * 8 + 8)
                    dve.wait_ge(mulled, h * 8)
                    dve.tensor_copy(atf[:, :, :, :], at[:, :, :, :]).then_inc(fl, 1)
                    dve.wait_ge(ccut1, h * 8 + 8)
                    hold(dve, passed)
                    for t in range(TT):
                        dve.max(best[:, t, 8:16], crest[:, t, :]).then_inc(cmax2, 1)
                    dve.wait_ge(cmax2, h * 4 + 4)
                    hold(dve, passed)
                    for t in range(TT):
                        dve.max_index(cat[:, t, 8:16], best[:, t, 8:16], crest[:, t, :]).then_inc(cat2, 1)
                    dve.wait_ge(cat2, h * 4 + 4)
                    dve.tensor_single_scalar(ab[:, 0, :, :], cat[:, :, :], 4, ALU.logical_shift_right).then_inc(split, 1)
                    dve.tensor_single_scalar(ab[:, 1, :, :], cat[:, :, :], 15, ALU.bitwise_and).then_inc(split, 1)
                    dve.wait_ge(split, h * 2 + 2)
                    dve.tensor_copy(abf[:, :, :, :], ab[:, :, :, :]).then_inc(fl, 1)
                    dve.wait_ge(fl, h * 2 + 2)
                    dve.tensor_tensor(eq[:, :, :, :].rearrange("p c s j -> p (c s) j"),
                                      abf[:, :, :, :].rearrange("p c t s -> p (c t s)").unsqueeze(2).to_broadcast(
                                          [P, 2 * TT * TOPK, TOPK]),
                                      iota[:, 0:TOPK].unsqueeze(1).to_broadcast([P, 2 * TT * TOPK, TOPK]),
                                      ALU.is_equal).then_inc(eqd, 1)
                    dve.wait_ge(cmax2, h * 4 + 4)
                    dve.tensor_tensor(sel_w[:, :, bass.ds(h * TOPK, TOPK)], best[:, :, :],
                                      best[:, :, 0:1].to_broadcast([P, TT, TOPK]), ALU.subtract).then_inc(picked, 1)
                    dve.wait_ge(mulled, h * 8 + 8)
                    for c in range(2):
                        dve.tensor_reduce(sel_e[:, c, :, bass.ds(h * TOPK, TOPK)],
                                          eq[:, c * TT:(c + 1) * TT, :, :], AX.X, ALU.add).then_inc(picked, 1)
                dve.wait_ge(picked, 3 * PH)
                dve.engine_nop().then_inc(g1, 1)
                dve.wait_ge(g1, 2)
                slots = sel_w[:, :, :].rearrange("p t (h s) -> p (t h) s", s=TOPK)
                dve.tensor_reduce(gsum[:, :], slots, AX.X, ALU.add).then_inc(g1, 1)
                dve.wait_ge(g1, 3)
                dve.reciprocal(gsum[:, :], gsum[:, :]).then_inc(g1, 1)
                dve.wait_ge(g1, 4)
                dve.tensor_tensor(slots, slots, gsum[:, :].unsqueeze(2).to_broadcast([P, TT * PH, TOPK]),
                                  ALU.mult).then_inc(g1, 1)


def gate_matrix(nc, ident, iota, sel_w, sel_e, gates):
    QUADS = TC // 4
    with ExitStack() as ctx:
        m = Mem(nc, ctx)
        e1T = m.sb("e1T", [P, SEQ])
        e2T = m.sb("e2T", [P, SEQ])
        wT = m.sb("wT", [P, SEQ])
        wh = m.sb("wh", [P, SEQ], F32R)
        wl = m.sb("wl", [P, SEQ])
        e2c = m.sb("e2c", [P, 2, 4])
        hot = m.sb("hot", [P, 2, 3, 4, P], F32R)
        stage = m.sb("stage", [P, 2, NK, TC])
        psT = m.ps("gpsT", [P, 3, SEQ])
        psG = m.ps("psG", [P, 2, 4, P])
        col, pool_passed = m.sem("g_col", "g_passed")
        turned, kept, high, low, hots2, hots1, summed, staged = m.sem(
            "g_turned", "g_kept", "g_high", "g_low", "hots2", "hots1", "g_summed", "g_staged")
        stored = m.sem("g_stored0", "g_stored1")
        with nc.Block() as block:

            @block.tensor
            def _(pe):
                for n, src in enumerate((sel_e[:, 0], sel_e[:, 1], sel_w)):
                    for t in range(TT):
                        mm = pe.transpose(psT[:, n, t * P:(t + 1) * P], src[:, t, :], ident[:, :])
                    mm.then_inc(turned, 1)
                with pe.Fori(0, SEQ // TC // 2) as i:
                    for q in range(2 * QUADS):
                        n = i * (2 * QUADS) + q
                        pe.wait_ge(hots2, n * 4 + 4)
                        pe.wait_ge(hots1, n * 8 + 8)
                        if q >= 2:
                            pe.wait_ge(staged, n - 1)
                        else:
                            pe.wait_ge(staged, i * (2 * QUADS))
                        for a in range(4):
                            pe.matmul(psG[:, q % 2, a, :], hot[:, q % 2, 0, a, :], hot[:, q % 2, 1, a, :],
                                      start=True, stop=False)
                            mm = pe.matmul(psG[:, q % 2, a, :], hot[:, q % 2, 0, a, :], hot[:, q % 2, 2, a, :],
                                           start=False, stop=True)
                        mm.then_inc(summed, 1)

            @block.gpsimd
            def _(pool):
                pool.wait_ge(kept, 2)
                with pool.Fori(0, SEQ // TC // 2) as i:
                    for q in range(2 * QUADS):
                        if q >= 2:
                            pool.wait_ge(summed, i * (2 * QUADS) + q - 1)
                        else:
                            pool.wait_ge(summed, i * (2 * QUADS))
                        hold(pool, pool_passed)
                        pool.tensor_copy(e2c[:, q % 2, :], e2T[:, bass.ds(i * (2 * TC) + q * 4, 4)]).then_inc(col, 1)
                        pool.wait_ge(col, i * (2 * QUADS) + q + 1)
                        hold(pool, pool_passed)
                        for a in range(4):
                            pool.tensor_scalar(hot[:, q % 2, 0, a, :], iota[:, :], e2c[:, q % 2, a:a + 1], None,
                                               ALU.is_equal).then_inc(hots2, 1)

            @block.vector
            def _(dve):
                for n, dst in enumerate((e1T, e2T, wT)):
                    dve.wait_ge(turned, n + 1)
                    dve.tensor_copy(dst[:, :], psT[:, n, :]).then_inc(kept, 1)
                dve.wait_ge(kept, 3)
                dve.tensor_copy(wh[:, :], wT[:, :]).then_inc(high, 1)
                dve.wait_ge(high, 1)
                dve.tensor_tensor(wl[:, :], wT[:, :], wh[:, :].bitcast(F32), ALU.subtract).then_inc(low, 1)
                dve.wait_ge(low, 1)
                with dve.Fori(0, SEQ // TC // 2) as i:
                    for q in range(2 * QUADS):
                        if q >= 2:
                            dve.wait_ge(summed, i * (2 * QUADS) + q - 1)
                        else:
                            dve.wait_ge(summed, i * (2 * QUADS))
                        for a in range(4):
                            t = i * (2 * TC) + q * 4 + a
                            for part, g in ((1, wh[:, bass.ds(t, 1)].bitcast(F32)), (2, wl[:, bass.ds(t, 1)])):
                                dve.tensor_scalar(hot[:, q % 2, part, a, :], iota[:, :], e1T[:, bass.ds(t, 1)], g,
                                                  ALU.is_equal, ALU.mult).then_inc(hots1, 1)

            @block.scalar
            def _(act):
                with act.Fori(0, SEQ // TC // 2) as i:
                    for q in range(2 * QUADS):
                        act.wait_ge(summed, i * (2 * QUADS) + q + 1)
                        s = q // QUADS
                        if q % QUADS == 0:
                            act.wait_ge(stored[s], i * 16)
                        t = (q % QUADS) * 4
                        act.copy(stage[:, s, :, t:t + 4], psG[:, q % 2, :, :].rearrange("p a i -> p i a")
                                 ).then_inc(staged, 1)

            @block.sync
            def _(sp):
                with sp.Fori(0, SEQ // TC // 2) as i:
                    for s in range(2):
                        sp.wait_ge(staged, i * (2 * QUADS) + (s + 1) * QUADS)
                        sp.dma_start(gates[bass.ds(i * 2 + s, 1)].rearrange("a p i t -> p (a i) t"),
                                     stage[:, s, :, :]).then_inc(stored[s], 16)
                for s in range(2):
                    sp.wait_ge(stored[s], 16 * (SEQ // TC // 2))


def from_one(eng, sem, value):
    if not isinstance(value, int) or value > 0:
        eng.wait_ge(sem, value)


def experts(nc, acc, h_hi, h_lo, gates, w):
    with ExitStack() as ctx:
        m = Mem(nc, ctx)
        u_raw = m.sb("u_raw", [P, BG, KD, P])
        u_hi = m.sb("u_hi", [P, 2, KD, P], F32R)
        u_lo = m.sb("u_lo", [P, 2, KD, P], F32R)
        v_raw = m.sb("v_raw", [P, 2, BG, HALF])
        v_hi = m.sb("v_hi", [P, BG, HALF], F32R)
        v_lo = m.sb("v_lo", [P, BG, HALF], F32R)
        g_sb = m.sb("g_sb", [P, 2, SEQ // TC, BG, TC])
        activ = m.sb("activ", [P, 2, SEQ])
        gated = m.sb("gated", [P, 2, SEQ])
        w_hi = m.sb("w_hi", [P, 2, BG, SEQ], F32R)
        w_lo = m.sb("w_lo", [P, 2, BG, SEQ], F32R)
        psA = m.ps("psA2", [P, 2, 512])
        psB = m.ps("psB", [P, TT, HALF])
        u_in = m.sem(*[f"u_in{k}" for k in range(BG)])
        v_in = m.sem("v_in0", "v_in1")
        g_in = m.sem("g_in0", "g_in1")
        (u_high, u_low, v_high, v_low, a_made, gelued, multiplied, w_high, w_low, b_step, b_made, drained) = m.sem(
            "u_high", "u_low", "v_high", "v_low", "a_made", "gelued", "multiplied", "w_high", "w_low", "b_step",
            "b_made", "drained")

        def pe_a(pe, b, k):
            pe.wait_ge(u_low, b + 1)
            from_one(pe, gelued, b - 1)
            for c in range(KD):
                pe.matmul(psA[:, k % 2, :], u_hi[:, k % 2, c, :], h_hi[:, c, :], start=(c == 0), stop=False)
                pe.matmul(psA[:, k % 2, :], u_hi[:, k % 2, c, :], h_lo[:, c, :], start=False, stop=False)
                mm = pe.matmul(psA[:, k % 2, :], u_lo[:, k % 2, c, :], h_hi[:, c, :], start=False,
                               stop=(c == KD - 1))
            mm.then_inc(a_made, 1)

        def pe_b(pe, g, par, half):
            if half == 0:
                pe.wait_ge(w_low, g * 4 + 4)
            for blk in range(BG):
                pe.wait_ge(v_low, g * 8 + (half * 4 + blk + 1))
                for t in range(TT):
                    if blk == 0:
                        pe.wait_ge(drained, g * 8 + (half * 4 + t + 1))
                    ts = slice(t * P, (t + 1) * P)
                    pe.matmul(psB[:, t, :], w_hi[:, par, blk, ts], v_hi[:, blk, :], start=(blk == 0), stop=False)
                    pe.matmul(psB[:, t, :], w_hi[:, par, blk, ts], v_lo[:, blk, :], start=False, stop=False)
                    mm = pe.matmul(psB[:, t, :], w_lo[:, par, blk, ts], v_hi[:, blk, :], start=False,
                                   stop=(blk == BG - 1))
                    if blk == BG - 1:
                        mm.then_inc(b_made, 1)
                if blk < BG - 1:
                    mm.then_inc(b_step, 1)

        def slot_free(eng, g, half, blk):
            if blk < BG - 1:
                from_one(eng, b_step, (g * 2 + half - 1) * 3 + blk + 1)
            else:
                from_one(eng, b_made, (g * 2 + half) * 4)

        def act_u(act, gb, k):
            act.wait_ge(u_in[k], gb * 16 + 16)
            from_one(act, a_made, gb * 4 + k - 1)
            act.copy(u_hi[:, k % 2, :, :], u_raw[:, k, :, :]).then_inc(u_high, 1)

        def act_w(act, gb, par, k):
            b = gb * 4 + k
            act.wait_ge(a_made, b + 1)
            from_one(act, multiplied, b - 1)
            act.activation(activ[:, k % 2, :], psA[:, k % 2, :], ACT.Gelu_apprx_tanh).then_inc(gelued, 1)
            act.wait_ge(multiplied, b + 1)
            from_one(act, b_made, (gb - 1) * 8)
            act.copy(w_hi[:, par, k, :], gated[:, k % 2, :]).then_inc(w_high, 1)

        def act_v(act, g, half, blk):
            act.wait_ge(v_in[half], g * 16 + 16)
            slot_free(act, g, half, blk)
            act.copy(v_hi[:, blk, :], v_raw[:, half, blk, :]).then_inc(v_high, 1)

        def dve_u(dve, gb, k):
            dve.wait_ge(u_high, gb * 4 + k + 1)
            dve.tensor_tensor(u_lo[:, k % 2, :, :], u_raw[:, k, :, :], u_hi[:, k % 2, :, :].bitcast(F32),
                              ALU.subtract).then_inc(u_low, 1)

        def dve_w(dve, gb, par, k, g_count):
            b = gb * 4 + k
            dve.wait_ge(g_in[par], g_count)
            from_one(dve, w_low, b - 1)
            dve.wait_ge(gelued, b + 1)
            dve.tensor_tensor(gated[:, k % 2, :].rearrange("p (c t) -> p c t", t=TC),
                              activ[:, k % 2, :].rearrange("p (c t) -> p c t", t=TC),
                              g_sb[:, par, :, k, :], ALU.mult).then_inc(multiplied, 1)
            dve.wait_ge(w_high, b + 1)
            dve.tensor_tensor(w_lo[:, par, k, :], gated[:, k % 2, :], w_hi[:, par, k, :].bitcast(F32),
                              ALU.subtract).then_inc(w_low, 1)

        def dve_v(dve, g, half, blk):
            dve.wait_ge(v_high, g * 8 + (half * 4 + blk + 1))
            dve.tensor_tensor(v_lo[:, blk, :], v_raw[:, half, blk, :], v_hi[:, blk, :].bitcast(F32),
                              ALU.subtract).then_inc(v_low, 1)

        def dve_drain(dve, g, half):
            for t in range(TT):
                dve.wait_ge(b_made, g * 8 + (half * 4 + t + 1))
                a = acc[:, t, half * HALF:(half + 1) * HALF]
                dve.tensor_tensor(a, a, psB[:, t, :], ALU.add).then_inc(drained, 1)

        def sp_u(sp, gb, k):
            from_one(sp, u_low, gb * 4 + k - 3)
            load(sp, u_raw[:, k, :, :], w["uT"][bass.ds(gb * 4 + k, 1)].rearrange(
                "a p (k e) -> p (a k) e", k=KD), u_in[k])

        def sp_v(sp, g, half):
            from_one(sp, v_low, g * 8 + (half * 4 - 4))
            load(sp, v_raw[:, half, :, :], w["v"][bass.ds(g * 4, 4), :, half * HALF:(half + 1) * HALF].rearrange(
                "b p d -> p b d"), v_in[half])

        def sp_g(sp, gb, par):
            from_one(sp, multiplied, gb * 4 - 4)
            load(sp, g_sb[:, par, :, :, :], gates[:, :, bass.ds(gb * 4, 4), :].rearrange(
                "c p i t -> p c (i t)"), g_in[par])

        def sp_turn(sp, g, par, u=True, v=True):
            if u:
                sp_g(sp, g + 2, par)
                sp_u(sp, g + 2, 0)
                sp_u(sp, g + 2, 1)
            if v:
                sp_v(sp, g + 1, 0)
            if u:
                sp_u(sp, g + 2, 2)
                sp_u(sp, g + 2, 3)
            if v:
                sp_v(sp, g + 1, 1)

        def pe_turn(pe, g, par, a=True):
            for half in range(2):
                if a:
                    for k in (2 * half, 2 * half + 1):
                        pe_a(pe, (g + 1) * 4 + k, k)
                pe_b(pe, g, par, half)

        def next_u(split, eng, gb, k):
            split(eng, gb + k // 2, (k + 2) % 4)

        def act_turn(act, g, par, a=True, u=True, v=True):
            for half in range(2):
                if a:
                    for k in (2 * half, 2 * half + 1):
                        if u or k < 2:
                            next_u(act_u, act, g + 1, k)
                        act_w(act, g + 1, 1 - par, k)
                if half == 0 or v:
                    for blk in range(BG):
                        act_v(act, g + half, 1 - half, blk)

        def dve_turn(dve, g, par, g_count, a=True, u=True, v=True):
            for half in range(2):
                if a:
                    for k in (2 * half, 2 * half + 1):
                        if u or k < 2:
                            next_u(dve_u, dve, g + 1, k)
                        dve_w(dve, g + 1, 1 - par, k, g_count)
                if half == 0 or v:
                    for blk in range(BG):
                        dve_v(dve, g + half, 1 - half, blk)
                dve_drain(dve, g, half)

        LOOPS = (GROUPS - 2) // 2
        with nc.Block() as block:

            @block.sync
            def _(sp):
                sp_g(sp, 0, 0)
                for k in range(BG):
                    sp_u(sp, 0, k)
                sp_v(sp, 0, 0)
                sp_g(sp, 1, 1)
                for k in range(BG):
                    sp_u(sp, 1, k)
                sp_v(sp, 0, 1)
                with sp.Fori(0, LOOPS) as i:
                    for par in range(2):
                        sp_turn(sp, i * 2 + par, par)
                sp_turn(sp, GROUPS - 2, 0, u=False)

            @block.tensor
            def _(pe):
                for k in range(BG):
                    pe_a(pe, k, k)
                with pe.Fori(0, LOOPS) as i:
                    for par in range(2):
                        pe_turn(pe, i * 2 + par, par)
                pe_turn(pe, GROUPS - 2, 0)
                pe_turn(pe, GROUPS - 1, 1, a=False)

            @block.scalar
            def _(act):
                act_u(act, 0, 0)
                act_u(act, 0, 1)
                for k in range(BG):
                    next_u(act_u, act, 0, k)
                    act_w(act, 0, 0, k)
                for blk in range(BG):
                    act_v(act, 0, 0, blk)
                with act.Fori(0, LOOPS) as i:
                    for par in range(2):
                        act_turn(act, i * 2 + par, par)
                act_turn(act, GROUPS - 2, 0, u=False)
                act_turn(act, GROUPS - 1, 1, a=False, v=False)

            @block.vector
            def _(dve):
                dve.engine_nop().then_inc(drained, TT)
                dve_u(dve, 0, 0)
                dve_u(dve, 0, 1)
                for k in range(BG):
                    next_u(dve_u, dve, 0, k)
                    dve_w(dve, 0, 0, k, 16)
                for blk in range(BG):
                    dve_v(dve, 0, 0, blk)
                with dve.Fori(0, LOOPS) as i:
                    for par in range(2):
                        dve_turn(dve, i * 2 + par, par, (i + 1 + par) * 16)
                dve_turn(dve, GROUPS - 2, 0, (GROUPS // 2) * 16, u=False)
                dve_turn(dve, GROUPS - 1, 1, 0, a=False, v=False)


def final_norm(nc, acc, out, w):
    with ExitStack() as ctx:
        m = Mem(nc, ctx)
        gain = m.sb("f_gain", [P, D])
        sq = m.sb("f_sq", [P, D])
        ss = m.sb("f_ss", [P, TT])
        ms = m.sb("f_ms", [P, TT])
        half = m.sb("f_half", [P, TT])
        rstd = m.sb("f_rstd", [P, TT])
        gain_in, squared, mean, rooted, scaled, out_done = m.sem("f_gain_in", "f_squared", "f_mean", "f_rooted",
                                                                 "f_scaled", "out_done")
        with nc.Block() as block:

            @block.sync
            def _(sp):
                load(sp, gain[:, :], w["lnf"].partition_broadcast(P), gain_in)
                for t in range(TT):
                    sp.wait_ge(scaled, t + 1)
                    sp.dma_start(out[t * P:(t + 1) * P, :], acc[:, t, :]).then_inc(out_done, 16)
                sp.wait_ge(out_done, 16 * TT)

            @block.scalar
            def _(act):
                for t in range(TT):
                    act.activation(sq[:, :], acc[:, t, :], ACT.Square, accum_out=ss[:, t:t + 1]).then_inc(squared, 1)
                    act.wait_ge(squared, t + 1)

            @block.gpsimd
            def _(pool):
                pool.memset(half[:, :], -0.5).then_inc(mean, 1)
                pool.wait_ge(squared, TT)
                pool.tensor_scalar(ms[:, :], ss[:, :], 1.0 / D, EPS, ALU.mult, ALU.add).then_inc(mean, 1)
                pool.wait_ge(mean, 2)
                pool.tensor_tensor(rstd[:, :], ms[:, :], half[:, :], ALU.pow).then_inc(rooted, 1)

            @block.vector
            def _(dve):
                dve.wait_ge(gain_in, 16)
                dve.wait_ge(rooted, 1)
                for t in range(TT):
                    dve.scalar_tensor_tensor(out=acc[:, t, :], in0=acc[:, t, :], scalar=rstd[:, t:t + 1],
                                             in1=gain[:, :], op0=ALU.mult, op1=ALU.mult).then_inc(scaled, 1)


def program(nc, w, out):
    with ExitStack() as ctx:
        m = Mem(nc, ctx)
        acc = m.sb("acc", [P, TT, D])
        ident = m.sb("ident", [P, P])
        gains = m.sb("gains", [P, 2, KD])
        iota = m.sb("iota", [P, P])
        x_in, small_in = m.sem("x_in", "small_in")
        with nc.Block() as block:

            @block.sync
            def _(sp):
                load(sp, acc[:, :, :], w["x"].rearrange("(t p) d -> p t d", p=P), x_in)
                load(sp, ident[:, :], w["ident"], small_in)
                load(sp, iota[:, :], w["iota"], small_in)
                load(sp, gains[:, :, :], w["gains"].rearrange("p (a k) -> p a k", a=2), small_in)

        with ExitStack() as ctx2:
            m2 = Mem(nc, ctx2)
            oT = m2.sb("oT", [P, KD, SEQ])
            with ExitStack() as ctx3:
                m3 = Mem(nc, ctx3)
                aT = m3.sb("aT", [P, KD, SEQ])
                norm_transposed(nc, "n1", acc, [(x_in, 16)], gains[:, 0, :], [(small_in, 48)], ident, aT)
                attention(nc, m3, aT, ident, oT, w)
            project_out(nc, oT, acc, w)

        gates = nc.dram_tensor("gate_scratch", (SEQ // TC, P, NK, TC), F32, kind="Internal").ap()
        h_hi = m.sb("h_hi", [P, KD, SEQ], F32R)
        h_lo = m.sb("h_lo", [P, KD, SEQ], F32R)
        with ExitStack() as ctx2:
            m2 = Mem(nc, ctx2)
            sel_w = m2.sb("sel_w", [P, TT, SEL])
            sel_e = m2.sb("sel_e", [P, 2, TT, SEL])
            with ExitStack() as ctx3:
                hT = Mem(nc, ctx3).sb("hT", [P, KD, SEQ])
                norm_transposed(nc, "n2", acc, [], gains[:, 1, :], [(small_in, 48)], ident, hT, h_hi, h_lo)
                choose_experts(nc, hT, iota, sel_w, sel_e, w)
            gate_matrix(nc, ident, iota, sel_w, sel_e, gates)
        experts(nc, acc, h_hi, h_lo, gates, w)
        final_norm(nc, acc, out, w)


def constants():
    q = np.arange(P)[:, None]
    dist = 384 + q - np.arange(SEQ)[None]
    t_nsa = np.where(dist >= 0, dist, MASKED)
    tq = np.arange(SEQ).reshape(TT, P).T[:, :, None]
    dc = tq - (np.arange(NCMP) * CMP_STRIDE + CMP_LEN - 1)[None, None]
    t_cmp = np.where(dc >= 0, dc, MASKED).reshape(P, -1)
    ds = P + q - np.arange(2 * P)[None]
    t_swa = np.where((ds >= 0) & (ds < SWA_WIN), ds, MASKED)
    n = NSA_HEADS + SWA_HEADS
    slopes = (2.0 ** (-8.0 * (np.arange(n) + 1) / n)).astype(np.float32)
    f = lambda a: np.ascontiguousarray(a, np.float32)
    return {"t_nsa": f(t_nsa), "t_cmp": f(t_cmp), "t_swa": f(t_swa),
            "slopes": f(np.broadcast_to(slopes, (P, n))), "ident": f(np.eye(P)),
            "iota": f(np.broadcast_to(np.arange(P), (P, P)))}


def layouts(x, ln1_g, w_in, cmp_pe_k, cmp_w1_k, cmp_w2_k, cmp_pe_v, cmp_w1_v, cmp_w2_v, swa_sinks, w_out,
            ln2_g, peer_wq, peer_keys, peer_u, peer_v, lnf_g):
    c = np.ascontiguousarray
    w_in = np.asarray(w_in)[0]
    cut = np.cumsum([512, 128, 128, 128, 128, 128, 128, 24, 512, 64, 64])[:-1]
    q_n, kc, vc, ks, vs, kw, vw, gt, q_s, k_s, v_s = np.split(w_in, cut, axis=1)
    head = lambda q, h: q[:, h * HD:(h + 1) * HD]
    tiles = [kc, vc, ks, kw, np.concatenate([k_s, k_s], 1)]
    tiles += [np.concatenate([head(q_n, j), head(q_n, j + 4)], 1) for j in range(PAIRS)]
    tiles += [q_s[:, j * P:(j + 1) * P] for j in range(PAIRS)]
    chunked = lambda a: a.reshape(KD, P, -1).transpose(1, 0, 2).reshape(P, -1)
    gates = gt.reshape(D, NSA_HEADS, 3).transpose(0, 2, 1).reshape(D, 24)
    nat = np.concatenate([vs, vw, v_s, gates], 1)
    pe = [np.asarray(a)[0].reshape(LP, 2, HD).transpose(1, 2, 0).reshape(P, LP) for a in (cmp_pe_k, cmp_pe_v)]
    w1 = [np.asarray(a)[0].reshape(LP, P, CMP_HID).transpose(1, 0, 2).reshape(P, -1) for a in (cmp_w1_k, cmp_w1_v)]
    w2 = [np.asarray(a)[0].reshape(2, P, HD).transpose(1, 0, 2).reshape(P, -1) for a in (cmp_w2_k, cmp_w2_v)]
    wo = np.asarray(w_out)[0].reshape(16, HD, D)
    order = [h for j in range(PAIRS) for h in (j, j + 4)] + list(range(8, 16))
    wo = chunked(wo[order].reshape(D, D))
    wq = np.asarray(peer_wq)[0].reshape(KD, P, PH * 2, P).transpose(2, 1, 0, 3).reshape(PH * 2, P, KD * P)
    keys = np.asarray(peer_keys)[0].transpose(0, 3, 1, 2).reshape(PH, P, 2 * NK)
    uT = np.asarray(peer_u)[0].reshape(NK, P, KD, P).transpose(0, 3, 2, 1).reshape(NK, P, KD * P)
    v = np.asarray(peer_v)[0].reshape(NK, P, D)
    return {"x": c(np.asarray(x)[0]), "gains": c(np.concatenate(
        [np.asarray(g)[0].reshape(KD, P).T for g in (ln1_g, ln2_g)], 1)),
        "w_tiles": c(np.stack([chunked(a) for a in tiles])), "w_nat": c(chunked(nat)),
        "pe": c(np.concatenate(pe, 1)), "w1": c(np.concatenate(w1, 1)), "w2": c(np.concatenate(w2, 1)),
        "sinks": c(np.asarray(swa_sinks)[0]), "w_out": c(wo), "wq": c(wq), "keys": c(keys),
        "uT": c(uT), "v": c(v), "lnf": c(np.asarray(lnf_g))}


def kernel(**inputs):
    import concourse.bacc as _bacc
    from concourse.bass_utils import run_bass_kernel_spmd as _run

    nc = _bacc.Bacc("TRN2", target_bir_lowering=False, num_devices=1)
    arrays = {**layouts(**inputs), **constants()}
    w = {n: nc.dram_tensor(f"in_{n}", a.shape, mybir.dt.from_np(a.dtype), kind="ExternalInput").ap()
         for n, a in arrays.items()}
    out = nc.dram_tensor("out", (SEQ, D), F32, kind="ExternalOutput").ap()
    program(nc, w, out)
    r = _run(nc, [{f"in_{n}": a for n, a in arrays.items()}], core_ids=[0])
    return r.results[0]["out"].reshape(1, SEQ, D)
```

```python
from contextlib import ExitStack

import numpy as np

import concourse.bass as bass
from concourse import mybir
from concourse.alu_op_type import AluOpType as ALU

ACT = mybir.ActivationFunctionType
AX = mybir.AxisListType
F32 = mybir.dt.float32
F32R = mybir.dt.float32r
BF16 = mybir.dt.bfloat16
U32 = mybir.dt.uint32

P = 128
SEQ = 512
D = 1024
KD = D // P
TT = SEQ // P
HD = 64
NSA_HEADS = SWA_HEADS = 8
PAIRS = 4
CMP_LEN, CMP_STRIDE, CMP_HID = 32, 16, 256
NCMP = (SEQ - CMP_LEN) // CMP_STRIDE + 1
LP = CMP_LEN // 2
CC = 2 * NCMP + 1
SWA_WIN = 128
PH = 8
NK = 128
TOPK = 16
SEL = PH * TOPK
EPS = 1e-6
MASKED = 1e30
CLAMP = 1e20
KV_TILES = 5
Q_TILES = 8
V_S, V_W, V_SWA, GATES = 0, 128, 256, 320
NAT = 344
BG = 4
GROUPS = NK // BG
TC = 32
EARLY0 = PH + 4
EARLY = EARLY0 + SEQ // TC
HALF = D // 2


def load(eng, out, in_, sem):
    eng.dma_start(out, in_).then_inc(sem, 16)


def from_one(eng, sem, value):
    if not isinstance(value, int) or value > 0:
        eng.wait_ge(sem, value)


def hold(eng, passed):
    eng.sem_inc(passed, 1)


def prime(eng, sem, n):
    eng.sem_inc(sem, n)


class Mem:

    def __init__(self, nc, ctx):
        self.nc, self.ctx = nc, ctx

    def sb(self, name, shape, dt=F32):
        return self.ctx.enter_context(self.nc.sbuf_tensor(name, shape, dt))

    def ps(self, name, shape, dt=F32):
        return self.ctx.enter_context(self.nc.psum_tensor(name, shape, dt))

    def sem(self, *names):
        got = [self.ctx.enter_context(self.nc.semaphore(n)) for n in names]
        return got if len(got) > 1 else got[0]


def norm_transposed(nc, tag, src, src_ready, gain, gain_ready, ident, dst, hi=None, lo=None):
    with ExitStack() as ctx:
        m = Mem(nc, ctx)
        sq = m.sb(tag + "sq", [P, D])
        ss = m.sb(tag + "ss", [P, TT])
        ms = m.sb(tag + "ms", [P, TT])
        half = m.sb(tag + "half", [P, TT])
        rstd = m.sb(tag + "rstd", [P, TT])
        xn = m.sb(tag + "xn", [P, TT, D])
        psT = m.ps(tag + "psT", [P, 2, SEQ])
        squared, mean, rooted, scaled, turned, copied, high, low = m.sem(
            *[tag + n for n in ("squared", "mean", "rooted", "scaled", "turned", "copied", "high", "low")])
        with nc.Block() as block:

            @block.scalar
            def _(act):
                for s, v in src_ready:
                    act.wait_ge(s, v)
                for t in range(TT):
                    act.activation(sq[:, :], src[:, t, :], ACT.Square,
                                   accum_out=ss[:, t:t + 1]).then_inc(squared, 1)
                    act.wait_ge(squared, t + 1)
                for s, v in gain_ready:
                    act.wait_ge(s, v)
                for k in range(KD):
                    act.wait_ge(turned, k + 1)
                    act.activation(dst[:, k, :], psT[:, k % 2, :], ACT.Copy,
                                   scale=gain[:, k:k + 1]).then_inc(copied, 1)
                    if hi is not None:
                        act.wait_ge(copied, k + 1)
                        act.copy(hi[:, k, :], dst[:, k, :]).then_inc(high, 1)

            @block.gpsimd
            def _(pool):
                pool.memset(half[:, :], -0.5).then_inc(mean, 1)
                pool.wait_ge(squared, TT)
                pool.tensor_scalar(ms[:, :], ss[:, :], 1.0 / D, EPS, ALU.mult, ALU.add).then_inc(mean, 1)
                pool.wait_ge(mean, 2)
                pool.tensor_tensor(rstd[:, :], ms[:, :], half[:, :], ALU.pow).then_inc(rooted, 1)

            @block.vector
            def _(dve):
                for s, v in src_ready:
                    dve.wait_ge(s, v)
                dve.wait_ge(rooted, 1)
                for t in range(TT):
                    dve.tensor_scalar(xn[:, t, :], src[:, t, :], rstd[:, t:t + 1], None,
                                      ALU.mult).then_inc(scaled, 1)
                if lo is not None:
                    for k in range(KD):
                        dve.wait_ge(high, k + 1)
                        dve.tensor_tensor(lo[:, k, :], dst[:, k, :], hi[:, k, :].bitcast(F32),
                                          ALU.subtract).then_inc(low, 1)

            @block.tensor
            def _(pe):
                for s, v in gain_ready:
                    pe.wait_ge(s, v)
                pe.wait_ge(scaled, TT)
                for k in range(KD):
                    if k >= 2:
                        pe.wait_ge(copied, k - 1)
                    for t in range(TT):
                        mm = pe.transpose(psT[:, k % 2, t * P:(t + 1) * P], xn[:, t, k * P:(k + 1) * P],
                                          ident[:, :])
                    mm.then_inc(turned, 1)


def pe_scores(pe, i, n, b):
    s = b.steps[n % b.N]
    b.wait_ready(pe, b.pe_ready, i, n)
    from_one(pe, b.shifted, i * b.N + (n - 1))
    pe.matmul(b.psS[:, n % 2, 0:s.width], s.q, s.k, start=True, stop=True).then_inc(b.scored, 1)


def pe_turn(pe, i, r, b):
    pe.wait_ge(b.expd, i * b.N + (r + 1))
    from_one(pe, b.copied[r % 2], i * (b.N // 2) + r // 2)
    for c in range(b.steps[r % b.N].width // P):
        mm = pe.transpose(b.psT[:, r % 2, c * P:(c + 1) * P], b.S[:, r % 4, c * P:(c + 1) * P], b.ident[:, :])
    mm.then_inc(b.turned, 1)


def pe_weigh(pe, i, r, b):
    s = b.steps[r]
    pe.wait_ge(b.copied[r % 2], i * (b.N // 2) + (r // 2 + 1))
    if r % 4 == 0:
        pe.wait_ge(b.taken, i * b.phases + (r // 4 + 1))
    for c in range(s.width // P):
        mm = pe.matmul(b.psO[:, (r // 4) % 2, (r % 4) * HD:(r % 4 + 1) * HD],
                       b.PT[:, r % 2, c * P:(c + 1) * P], s.v[c], start=(c == 0), stop=(c == s.width // P - 1))
    mm.then_inc(b.weighed, 1)


def act_exp(act, i, n, b):
    m, s = n % b.N, b.steps[n % b.N]
    act.wait_ge(b.shifted, i * b.N + (n + 1))
    act.activation(b.S[:, n % 4, 0:s.width], b.S[:, n % 4, 0:s.width], ACT.Exp,
                   bias=b.nmax[:, m:m + 1], scale=-1.0, accum_out=b.sums[:, m:m + 1]).then_inc(b.expd, 1)


def dve_shift(dve, i, n, b):
    m, s = n % b.N, b.steps[n % b.N]
    b.wait_ready(dve, b.dve_ready, i, n)
    dve.wait_ge(b.scored, i * b.N + (n + 1))
    from_one(dve, b.turned, i * b.N + (n - 3))
    hold(dve, b.passed)
    dve.tensor_tensor_reduce(b.S[:, n % 4, 0:s.width], s.bias, b.psS[:, n % 2, 0:s.width], 1.0,
                             s.start, ALU.add, ALU.min, b.nmax[:, m:m + 1]).then_inc(b.shifted, 1)


def copy_turned(eng, copy, i, r, b):
    width = b.steps[r % b.N].width
    eng.wait_ge(b.turned, i * b.N + (r + 1))
    from_one(eng, b.weighed, i * b.N + (r - 1))
    copy(b.PT[:, r % 2, 0:width], b.psT[:, r % 2, 0:width]).then_inc(b.copied[r % 2], 1)


class Step:
    def __init__(self, width, q, k, v, bias, start):
        self.width, self.q, self.k, self.v, self.bias, self.start = width, q, k, v, bias, start


class Bundle:

    def __init__(self, m, steps, phases, psS, psT, psO, ident):
        self.steps, self.N, self.phases = steps, len(steps), phases
        self.psS, self.psT, self.psO, self.ident = psS, psT, psO, ident
        self.S = m.sb("S", [P, 4, SEQ])
        self.PT = m.sb("PT", [P, 2, SEQ])
        self.nmax = m.sb("nmax", [P, self.N])
        self.sums = m.sb("sums", [P, self.N])
        self.scored, self.shifted, self.expd, self.turned, c0, c1, self.weighed, self.taken, self.passed = m.sem(
            "scored", "shifted", "expd", "turned", "copied0", "copied1", "weighed", "taken", "passed")
        self.copied = [c0, c1]
        self.pe_ready, self.dve_ready = {}, {}

    def wait_ready(self, eng, ready, i, n):
        if n % self.N in ready:
            sem, per_pair = ready[n % self.N]
            eng.wait_ge(sem, i * per_pair + per_pair * (n // self.N + 1))


def attention(nc, m, a_hi, a_lo, ident, oT, w):
    qN = m.sb("qN", [P, SEQ])
    qS = m.sb("qS", [P, SEQ])
    wt = m.sb("wt", [P, 2, KD, P])
    wt_hi = m.sb("wt_hi", [P, 2, KD, P], F32R)
    wt_lo = m.sb("wt_lo", [P, 2, KD, P], F32R)
    ksT = m.sb("ksT", [P, SEQ])
    kwT = m.sb("kwT", [P, SEQ])
    kdT = m.sb("kdT", [P, SEQ])
    nat = m.sb("nat", [P, TT, NAT])
    gsig = m.sb("gsig", [P, TT, 3, NSA_HEADS])
    kcT = m.sb("kcT", [P, NCMP])
    vcn = m.sb("vcn", [NCMP, 2, HD])
    Tbase = m.sb("Tbase", [P, SEQ])
    Tcmp = m.sb("Tcmp", [P, TT, NCMP])
    Tswa = m.sb("Tswa", [P, 2 * P])
    slopes = m.sb("slopes", [P, 2 * NSA_HEADS])
    sinks = m.sb("sinks", [P, SWA_HEADS])
    nsink = m.sb("nsink", [P, SWA_HEADS])
    tables, nsinked = m.sem("tables", "nsinked")

    with ExitStack() as ctx:
        k = Mem(nc, ctx)
        wn = k.sb("wn", [P, KD, NAT])
        wn_hi = k.sb("wn_hi", [P, KD, NAT], F32R)
        wn_lo = k.sb("wn_lo", [P, KD, NAT], F32R)
        X = k.sb("X", [P, 2, LP, CC])
        w1 = k.sb("w1", [P, 2, LP, CMP_HID])
        w2 = k.sb("w2", [P, 2, 2, HD])
        pe_sb = k.sb("pe_sb", [P, 2, LP])
        cb = k.sb("cb", [P, 4])
        hid = k.sb("hid", [P, 4, 2 * NCMP])
        ge = k.sb("ge", [P, TT, 3 * NSA_HEADS])
        psA = k.ps("psA", [P, 2, 512])
        psN = k.ps("psN", [P, 2, 512])
        psH = k.ps("psH", [P, 2, 512])
        psK = k.ps("psK", [P, 512])
        psV = k.ps("psV", [P, 512])
        wt_in = k.sem("wt_in0", "wt_in1")
        wn_in, w1_in, w2_in, pe_in = k.sem("wn_in", "w1_in", "w2_in", "pe_in")
        wt_high, wt_low, wn_high, wn_low = k.sem("wt_high", "wt_low", "wn_high", "wn_low")
        (projected, kept, keptx, pe_put, natured, nat_kept, gexp, gadd, gdone, hidden, bias_put, gelud,
         kc_made, kc_kept) = k.sem("projected", "kept", "keptx", "pe_put", "natured", "nat_kept", "gexp", "gadd",
                                   "gdone", "hidden", "bias_put", "gelud", "kc_made", "kc_kept")

        FIRST_TILES = [*range(KV_TILES), KV_TILES, KV_TILES + PAIRS]
        dsts = (None, None, ksT, kwT, kdT, qN, qS)
        NT = len(FIRST_TILES)

        def sp_tile(sp, n, s):
            from_one(sp, wt_low, n - 1)
            load(sp, wt[:, s], w["w_tiles"][FIRST_TILES[n]].rearrange("p (k c) -> p k c", k=KD), wt_in[s])

        def act_tile(act, n, s, landed):
            act.wait_ge(wt_in[s], landed)
            from_one(act, projected, n - 1)
            act.copy(wt_hi[:, s], wt[:, s]).then_inc(wt_high, 1)

        def dve_tile(dve, n, s):
            dve.wait_ge(wt_high, n + 1)
            dve.tensor_tensor(wt_lo[:, s], wt[:, s], wt_hi[:, s].bitcast(F32), ALU.subtract).then_inc(wt_low, 1)

        def pe_tile(pe, n, s):
            pe.wait_ge(wt_low, n + 1)
            for c in range(KD):
                pe.matmul(psA[:, s, :], wt_hi[:, s, c, :], a_hi[:, c, :], start=(c == 0), stop=False)
                pe.matmul(psA[:, s, :], wt_hi[:, s, c, :], a_lo[:, c, :], start=False, stop=False)
                mm = pe.matmul(psA[:, s, :], wt_lo[:, s, c, :], a_hi[:, c, :], start=False, stop=(c == KD - 1))
            mm.then_inc(projected, 1)

        KEPT = 8
        with nc.Block() as block:

            @block.sync
            def _(sp):
                for n in range(NT):
                    sp_tile(sp, n, n % 2)
                    if n == 1:
                        load(sp, pe_sb[:, :, :], w["pe"].rearrange("p (a l) -> p a l", a=2), pe_in)
                load(sp, w1[:, :, :, :], w["w1"].rearrange("p (a l c) -> p a l c", a=2, l=LP), w1_in)
                load(sp, wn[:, :, :], w["w_nat"].rearrange("p (k c) -> p k c", k=KD), wn_in)
                load(sp, w2[:, :, :, :], w["w2"].rearrange("p (a l c) -> p a l c", a=2, l=2), w2_in)
                load(sp, Tbase[:, :], w["t_nsa"], tables)
                load(sp, Tcmp[:, :, :], w["t_cmp"].rearrange("p (a c) -> p a c", a=TT), tables)
                load(sp, Tswa[:, :], w["t_swa"], tables)
                load(sp, slopes[:, :], w["slopes"], tables)
                load(sp, sinks[:, :], w["sinks"].partition_broadcast(P), tables)

            @block.tensor
            def _(pe):
                for n in range(NT):
                    if n >= 2:
                        pe.wait_ge(keptx if n == 3 else kept, KEPT + (n - 3 if n >= 4 else 0))
                    pe_tile(pe, n, n % 2)
                pe.wait_ge(keptx, 8)
                pe.wait_ge(kept, 8)
                pe.wait_ge(pe_put, 1)
                pe.wait_ge(w1_in, 16)
                for kv in range(2):
                    for hc in range(2):
                        for lp in range(LP):
                            mm = pe.matmul(psH[:, kv, hc * 64:hc * 64 + CC], w1[:, kv, lp, hc * P:(hc + 1) * P],
                                           X[:, kv, lp, :], start=(lp == 0), stop=(lp == LP - 1))
                        mm.then_inc(hidden, 1)
                pe.wait_ge(wn_low, 1)
                for t in range(TT):
                    if t >= 2:
                        pe.wait_ge(nat_kept, t - 1)
                    ts = slice(t * P, (t + 1) * P)
                    for c in range(KD):
                        pe.matmul(psN[:, t % 2, 0:NAT], a_hi[:, c, ts], wn_hi[:, c, :], start=(c == 0), stop=False)
                        pe.matmul(psN[:, t % 2, 0:NAT], a_hi[:, c, ts], wn_lo[:, c, :], start=False, stop=False)
                        mm = pe.matmul(psN[:, t % 2, 0:NAT], a_lo[:, c, ts], wn_hi[:, c, :], start=False,
                                       stop=(c == KD - 1))
                    mm.then_inc(natured, 1)
                pe.wait_ge(gelud, 4)
                pe.wait_ge(w2_in, 16)
                for g in range(2):
                    for hc in range(2):
                        mm = pe.matmul(psK[g * HD:(g + 1) * HD, 0:NCMP], w2[:, 0, hc, :],
                                       hid[:, hc, g * NCMP:(g + 1) * NCMP], start=(hc == 0), stop=(hc == 1))
                mm.then_inc(kc_made, 1)
                for g in range(2):
                    for hc in range(2):
                        mm = pe.matmul(psV[0:NCMP, g * HD:(g + 1) * HD],
                                       hid[:, 2 + hc, g * NCMP:(g + 1) * NCMP], w2[:, 1, hc, :],
                                       start=(hc == 0), stop=(hc == 1))
                mm.then_inc(kc_made, 1)

            def spread(copy, kv, par, done):
                for g in range(2):
                    for q in range(2):
                        raw = psA[g * HD:(g + 1) * HD, kv, :].rearrange("p (n l a) -> p a l n", a=2, l=LP // 2)
                        copy(X[par * HD:(par + 1) * HD, kv, q * 8:(q + 1) * 8, g * NCMP:(g + 1) * NCMP],
                             raw[:, par, :, q:q + NCMP]).then_inc(done, 1)

            @block.scalar
            def _(act):
                act_tile(act, 0, 0, 16)
                act_tile(act, 1, 1, 16)
                for n, dst in enumerate(dsts):
                    act.wait_ge(projected, n + 1)
                    if n == 0:
                        spread(act.copy, 0, 0, kept)
                        spread(act.copy, 0, 1, kept)
                    elif 2 <= n < KV_TILES:
                        act.copy(dst[:, :], psA[:, n % 2, :]).then_inc(kept, 1)
                    elif n >= KV_TILES:
                        act.activation(dst[:, :], psA[:, n % 2, :], ACT.Copy, scale=-(HD ** -0.5)).then_inc(kept, 1)
                    if n + 2 < NT:
                        act_tile(act, n + 2, n % 2, 16 * (n // 2 + 2))
                act.wait_ge(wn_in, 16)
                act.copy(wn_hi[:, :, :], wn[:, :, :]).then_inc(wn_high, 1)
                for j in range(4):
                    act.wait_ge(bias_put, 2 * (j // 2) + 2)
                    act.activation(hid[:, j, :], psH[:, j // 2, (j % 2) * 64:(j % 2) * 64 + 2 * NCMP],
                                   ACT.Gelu_apprx_tanh, bias=cb[:, j:j + 1]).then_inc(gelud, 1)
                act.wait_ge(nat_kept, TT)
                act.activation(ge[:, :, :], nat[:, :, GATES:NAT], ACT.Exp, scale=-1.0).then_inc(gexp, 1)

            @block.vector
            def _(dve):
                dve.wait_ge(pe_in, 16)
                dve.tensor_copy(X[:, :, :, CC - 1], pe_sb[:, :, :]).then_inc(pe_put, 1)
                for n in range(NT):
                    if n == 3:
                        dve.wait_ge(projected, 2)
                        spread(dve.tensor_copy, 1, 0, keptx)
                        spread(dve.tensor_copy, 1, 1, keptx)
                    dve_tile(dve, n, n % 2)
                dve.wait_ge(wn_high, 1)
                dve.tensor_tensor(wn_lo[:, :, :], wn[:, :, :], wn_hi[:, :, :].bitcast(F32),
                                  ALU.subtract).then_inc(wn_low, 1)
                for j in range(4):
                    dve.wait_ge(hidden, 2 * (j // 2) + 2)
                    dve.tensor_copy(cb[:, j:j + 1],
                                    psH[:, j // 2, (j % 2) * 64 + CC - 1:(j % 2) * 64 + CC]).then_inc(bias_put, 1)
                for t in range(TT):
                    dve.wait_ge(natured, t + 1)
                    dve.tensor_copy(nat[:, t, :], psN[:, t % 2, 0:NAT]).then_inc(nat_kept, 1)
                dve.wait_ge(gexp, 1)
                dve.tensor_scalar(ge[:, :, :], ge[:, :, :], 1.0, None, ALU.add).then_inc(gadd, 1)
                dve.wait_ge(gadd, 1)
                dve.reciprocal(gsig[:, :, :, :], ge[:, :, :].rearrange("p t (c h) -> p t c h", c=3)).then_inc(gdone, 1)
                dve.wait_ge(kc_made, 1)
                dve.tensor_copy(kcT[:, :], psK[:, 0:NCMP]).then_inc(kc_kept, 1)
                dve.wait_ge(kc_made, 2)
                dve.tensor_copy(vcn[:, :, :], psV[0:NCMP, 0:P].rearrange("p (g d) -> p g d", g=2)).then_inc(kc_kept, 1)
                dve.wait_ge(tables, 80)
                dve.tensor_scalar(nsink[:, :], sinks[:, :], -1.0, None, ALU.mult).then_inc(nsinked, 1)

    with ExitStack() as ctx:
        k = Mem(nc, ctx)
        Th = k.sb("Th", [P, 2, SEQ])
        sTh = k.sb("sTh", [P, 2, 2 * P])
        Tc = k.sb("Tc", [P, 2, TT, NCMP])
        ns = k.sb("ns", [P, 2])
        gp = k.sb("gp", [P, 3, 2, TT])
        fac = k.sb("fac", [P, 6, TT])
        sfac = k.sb("sfac", [P, 2, TT])
        es = k.sb("es", [P, 2, TT])
        Sc = k.sb("Sc", [P, 2, TT, NCMP])
        cmin = k.sb("cmin", [P, 2 * TT])
        csum = k.sb("csum", [P, 2 * TT])
        PTc = k.sb("PTc", [NCMP, 2, TT, P])
        part = k.sb("part", [P, TT, HD])
        op = k.sb("op", [P, TT, 2, HD])
        sop = k.sb("sop", [P, TT, 2, HD])
        psS = k.ps("psS", [P, 2, 512])
        psT = k.ps("psT", [P, 2, 512])
        psO = k.ps("psO", [P, 2, 512])
        psC = k.ps("psC", [P, 512])
        psQ = k.ps("psQ", [P, 512])
        q_in = k.sem("qw_in0", "qw_in1")
        q_high, q_low, q_made, qn_kept, qs_kept = k.sem("qw_high", "qw_low", "q_made", "qn_kept", "qs_kept")
        (nsa_ready, swa_ready, gated, c_scored, c_chain, c_sum, c_exp, c_turned, c_copied, c_weighed, c_taken, facs,
         o_added, o_turned, o_kept, s_chain, s_exp, so_turned, so_kept, pool_passed, act_passed) = k.sem(
            "nsa_ready", "swa_ready", "gated", "c_scored", "c_chain", "c_sum", "c_exp", "c_turned", "c_copied",
            "c_weighed", "c_taken", "facs", "o_added", "o_turned", "o_kept", "s_chain", "s_exp", "so_turned",
            "so_kept", "p_passed", "a_passed")
        steps = []
        for hh in range(2):
            r = slice(hh * HD, (hh + 1) * HD)
            for kT, voff in ((ksT, V_S), (kwT, V_W)):
                for t in range(TT):
                    width = (t + 1) * P
                    steps.append(Step(width, qN[r, t * P:(t + 1) * P], kT[r, 0:width],
                                      [nat[:, c, voff + hh * HD:voff + (hh + 1) * HD] for c in range(t + 1)],
                                      Th[:, hh, SEQ - width:SEQ], CLAMP))
        NSA = len(steps)
        for hh in range(2):
            r = slice(hh * HD, (hh + 1) * HD)
            for t in range(TT):
                k0 = max(t - 1, 0)
                width = (t + 1 - k0) * P
                steps.append(Step(width, qS[r, t * P:(t + 1) * P], kdT[r, k0 * P:k0 * P + width],
                                  [nat[:, c, V_SWA:V_SWA + HD] for c in range(k0, t + 1)],
                                  sTh[:, hh, 2 * P - width:2 * P], ns[:, hh:hh + 1]))
        b = Bundle(k, steps, 6, psS, psT, psO, ident)
        N = b.N
        b.pe_ready = {0: (qn_kept, 1), NSA: (qs_kept, 1)}
        b.dve_ready = {0: (nsa_ready, 4), NSA: (swa_ready, 3)}
        LEAD = 3

        def turns(eng, turn):
            with eng.Fori(0, PAIRS - 1) as i:
                turn(eng, i, False)
            turn(eng, PAIRS - 1, True)

        def pe_compressed_scores(pe, i):
            pe.wait_ge(so_kept, i + 1)
            pe.wait_ge(qs_kept, i + 1)
            for hh, ps in enumerate((psC, psQ)):
                r = slice(hh * HD, (hh + 1) * HD)
                for t in range(TT):
                    mm = pe.matmul(ps[:, t * NCMP:(t + 1) * NCMP], qN[r, t * P:(t + 1) * P], kcT[r, :],
                                   start=True, stop=True)
                mm.then_inc(c_scored, 1)

        def pe_compressed_turn(pe, i, hh):
            if hh == 0:
                pe.wait_ge(c_exp, i + 1)
            else:
                pe.wait_ge(c_copied, i * 2 + 1)
            for t in range(TT):
                mm = pe.transpose(psC[0:NCMP, t * P:(t + 1) * P], Sc[:, hh, t, :], ident[:, :])
            mm.then_inc(c_turned, 1)

        def pe_compressed_weigh(pe, i):
            pe.wait_ge(c_copied, i * 2 + 2)
            for hh in range(2):
                for t in range(TT):
                    x = hh * TT + t
                    mm = pe.matmul(psC[:, x * HD:(x + 1) * HD], PTc[:, hh, t, :], vcn[:, hh, :],
                                   start=True, stop=True)
            mm.then_inc(c_weighed, 1)

        SPREAD = {n: (0, 24 * (n - 6) // 11, 24 * (n - 5) // 11) for n in range(6, 17)}
        SPREAD.update({n: (1, 24 * (n - 18) // 9, 24 * (n - 17) // 9) for n in range(18, 27)})

        def pe_queries(pe, i, s, first, end):
            if first == 0:
                pe.wait_ge(q_low, i * 2 + (s + 3))
                if s == 0:
                    pe.wait_ge(c_chain, i * 4 + 2)
                else:
                    pe.wait_ge(qn_kept, i + 2)
            for x in range(first, end):
                c, j = x // 3, x % 3
                u, a = ((wt_hi, a_hi), (wt_hi, a_lo), (wt_lo, a_hi))[j]
                mm = pe.matmul(psQ[:, :], u[:, s, c, :], a[:, c, :], start=(x == 0), stop=(x == 3 * KD - 1))
            if end == 3 * KD:
                mm.then_inc(q_made, 1)

        def pe_out_nsa(pe, i):
            pe.wait_ge(o_added, i * 4 + 5)
            for t in range(TT):
                mm = pe.transpose(psC[:, t * P:(t + 1) * P], op[:, t, :, :], ident[:, :])
            mm.then_inc(o_turned, 1)

        def pe_out_swa(pe, i):
            pe.wait_ge(b.taken, i * 6 + 8)
            pe.wait_ge(o_kept, i + 1)
            for t in range(TT):
                mm = pe.transpose(psC[:, t * P:(t + 1) * P], sop[:, t, :, :], ident[:, :])
            mm.then_inc(so_turned, 1)

        def pe_pair(pe, i, last):
            extra = {4: pe_compressed_scores, 8: lambda *a: pe_compressed_turn(*a, 0),
                     10: lambda *a: pe_compressed_turn(*a, 1), 13: pe_compressed_weigh, 22: pe_out_nsa}
            for n in range(LEAD, N + LEAD):
                if n < N or not last:
                    pe_scores(pe, i, n, b)
                if n in extra:
                    extra[n](pe, i)
                if n in SPREAD and not last:
                    pe_queries(pe, i, *SPREAD[n])
                if n - 2 < N or not last:
                    pe_turn(pe, i, n - 2, b)
                pe_weigh(pe, i, n - LEAD, b)
            pe_out_swa(pe, i)

        def act_pair(act, i, last):
            for n in range(LEAD, N + LEAD):
                if n < N or not last:
                    act_exp(act, i, n, b)
                if n == 6:
                    act.wait_ge(c_chain, i * 4 + 4)
                    act.activation(Sc[:, :, :, :], Sc[:, :, :, :], ACT.Exp, scale=-1.0).then_inc(c_exp, 1)
                if n in (9, 11):
                    hh = (n - 9) // 2
                    act.wait_ge(c_turned, i * 2 + (hh + 1))
                    act.copy(PTc[:, hh, :, :], psC[0:NCMP, :].rearrange("p (t q) -> p t q", t=TT)
                             ).then_inc(c_copied, 1)
                if n in (3, 12) and not last:
                    s = n // 12
                    act.wait_ge(q_in[s], i * 16 + 16)
                    act.wait_ge(q_made, i * 2 + (s + 1))
                    act.copy(wt_hi[:, s], wt[:, s]).then_inc(q_high, 1)
                if n == 17 and not last:
                    act.wait_ge(q_made, i * 2 + 3)
                    act.activation(qN[:, :], psQ[:, :], ACT.Copy, scale=-(HD ** -0.5)).then_inc(qn_kept, 1)
                if n == 23:
                    act.wait_ge(o_turned, i + 1)
                    act.copy(oT[:, bass.ds(i, 1), :].rearrange("p a t -> p (a t)"), psC[:, :]).then_inc(o_kept, 1)
                if n == 25:
                    act.wait_ge(s_chain, i * 5 + 1)
                    act.activation(es[:, :, :], es[:, :, :], ACT.Exp).then_inc(s_exp, 1)
                if n % 2 == 0 and (n - 2 < N or not last):
                    copy_turned(act, act.copy, i, n - 2, b)
            if not last:
                act.wait_ge(q_made, i * 2 + 4)
                act.activation(qS[:, :], psQ[:, :], ACT.Copy, scale=-(HD ** -0.5)).then_inc(qs_kept, 1)
            act.wait_ge(so_turned, i + 1)
            act.copy(oT[:, bass.ds(i + PAIRS, 1), :].rearrange("p a t -> p (a t)"), psC[:, :]).then_inc(so_kept, 1)

        def dve_gates(dve, i):
            for hh in range(2):
                dve.tensor_copy(gp[:, :, hh, :], gsig[:, :, :, bass.ds(i + 4 * hh, 1)].rearrange(
                    "p t c a -> p c (t a)")).then_inc(gated, 1)

        def dve_compressed(dve, i):
            for hh, ps in enumerate((psC, psQ)):
                dve.wait_ge(c_scored, i * 2 + (hh + 1))
                dve.tensor_tensor(Sc[:, hh, :, :], Tc[:, hh, :, :],
                                  ps[:, 0:TT * NCMP].rearrange("p (t n) -> p t n", t=TT),
                                  ALU.add).then_inc(c_chain, 1)
            dve.wait_ge(c_chain, i * 4 + 2)
            flat = Sc[:, :, :, :].rearrange("p h t n -> p (h t) n")
            dve.tensor_reduce(cmin[:, :], flat, AX.X, ALU.min).then_inc(c_sum, 1)
            dve.wait_ge(c_sum, i * 2 + 1)
            dve.tensor_scalar(cmin[:, :], cmin[:, :], CLAMP, None, ALU.min).then_inc(c_chain, 1)
            dve.wait_ge(c_chain, i * 4 + 3)
            dve.tensor_tensor(flat, flat, cmin[:, :].unsqueeze(2).to_broadcast([P, 2 * TT, NCMP]),
                              ALU.subtract).then_inc(c_chain, 1)

        def dve_compressed_sums(dve, i):
            dve.wait_ge(c_exp, i + 1)
            dve.tensor_reduce(csum[:, :], Sc[:, :, :, :].rearrange("p h t n -> p (h t) n"), AX.X,
                              ALU.add).then_inc(c_sum, 1)

        def factor(dve, i, use, c, hh, sums):
            f = fac[:, use, :]
            dve.tensor_scalar(f, sums, 1e-30, None, ALU.max).then_inc(facs, 1)
            dve.wait_ge(facs, i * 18 + (3 * use + 1))
            dve.reciprocal(f, f).then_inc(facs, 1)
            dve.wait_ge(facs, i * 18 + (3 * use + 2))
            dve.tensor_tensor(f, f, gp[:, c, hh, :], ALU.mult).then_inc(facs, 1)
            dve.wait_ge(facs, i * 18 + (3 * use + 3))
            return f.unsqueeze(2).to_broadcast([P, TT, HD])

        def dve_take(dve, i, phase):
            hh, c = phase // 2, (1, 2)[phase % 2]
            if phase == 0:
                dve.wait_ge(gated, i * 2 + 2)
            f = factor(dve, i, phase, c, hh, b.sums[:, 4 * phase:4 * phase + 4])
            dve.wait_ge(b.weighed, i * N + (4 * phase + 4))
            o = psO[:, phase % 2, 0:TT * HD].rearrange("p (t d) -> p t d", t=TT)
            if c == 1:
                dve.tensor_tensor(op[:, :, hh, :], f, o, ALU.mult).then_inc(b.taken, 1)
                return
            dve.wait_ge(o_added, i * 4 + (hh + 1))
            dve.tensor_tensor(part[:, :, :], f, o, ALU.mult).then_inc(b.taken, 1)
            dve.wait_ge(b.taken, i * 6 + (phase + 3))
            dve.tensor_tensor(op[:, :, hh, :], op[:, :, hh, :], part[:, :, :], ALU.add).then_inc(o_added, 1)

        def dve_take_compressed(dve, i, hh):
            if hh == 0:
                dve.wait_ge(c_sum, i * 2 + 2)
            f = factor(dve, i, 4 + hh, 0, hh, csum[:, hh * TT:(hh + 1) * TT])
            dve.wait_ge(c_weighed, i + 1)
            dve.wait_ge(o_added, i * 4 + (hh + 3))
            dve.tensor_tensor(part[:, :, :], f, psC[:, hh * TT * HD:(hh + 1) * TT * HD].rearrange("p (t d) -> p t d", t=TT),
                              ALU.mult).then_inc(c_taken, 1)
            dve.wait_ge(c_taken, i * 2 + (hh + 1))
            dve.tensor_tensor(op[:, :, hh, :], op[:, :, hh, :], part[:, :, :], ALU.add).then_inc(o_added, 1)

        def dve_sinks(dve, i):
            dve.wait_ge(b.shifted, i * N + N)
            dve.tensor_tensor(es[:, :, :], b.nmax[:, NSA:N].rearrange("p (h t) -> p h t", h=2),
                              ns[:, :].unsqueeze(2).to_broadcast([P, 2, TT]), ALU.subtract).then_inc(s_chain, 1)

        def dve_window_factors(dve, i):
            dve.wait_ge(s_exp, i + 1)
            dve.wait_ge(b.expd, i * N + N)
            dve.tensor_tensor(sfac[:, :, :], es[:, :, :], b.sums[:, NSA:N].rearrange("p (h t) -> p h t", h=2),
                              ALU.add).then_inc(s_chain, 1)
            dve.wait_ge(s_chain, i * 5 + 2)
            dve.reciprocal(sfac[:, :, :], sfac[:, :, :]).then_inc(s_chain, 3)

        def dve_take_windows(dve, i):
            dve.wait_ge(s_chain, i * 5 + 5)
            for hh in range(2):
                dve.wait_ge(b.weighed, i * N + (NSA + 4 * hh + 4))
                dve.tensor_tensor(sop[:, :, hh, :], sfac[:, hh, :].unsqueeze(2).to_broadcast([P, TT, HD]),
                                  psO[:, hh, 0:TT * HD].rearrange("p (t d) -> p t d", t=TT),
                                  ALU.mult).then_inc(b.taken, 1)

        def dve_pair(dve, i, last):
            for n in range(LEAD, N + LEAD):
                if n < N or not last:
                    dve_shift(dve, i, n, b)
                if n % 2 == 1:
                    copy_turned(dve, dve.tensor_copy, i, n - 2, b)
                if n == 4:
                    dve_gates(dve, i)
                if n == 5:
                    dve_compressed(dve, i)
                if n == 10:
                    dve_compressed_sums(dve, i)
                if n in (7, 11, 15, 19):
                    dve_take(dve, i, (n - 7) // 4)
                if n == 20:
                    for hh in range(2):
                        dve_take_compressed(dve, i, hh)
                if n == 24:
                    dve_sinks(dve, i)
                if n == 26:
                    dve_window_factors(dve, i)
            dve_take_windows(dve, i)

        def pool_nsa(pool, i):
            for hh in range(2):
                s = slopes[:, bass.ds(i + (8 + 4 * hh), 1)]
                pool.tensor_tensor(Th[:, hh, :], Tbase[:, :], s.to_broadcast([P, SEQ]), ALU.mult).then_inc(nsa_ready, 1)
                pool.tensor_tensor(Tc[:, hh, :, :], Tcmp[:, :, :], s.unsqueeze(2).to_broadcast([P, TT, NCMP]),
                                   ALU.mult).then_inc(nsa_ready, 1)

        def pool_swa(pool, i):
            for hh in range(2):
                s = slopes[:, bass.ds(i * 2 + hh, 1)]
                pool.tensor_tensor(sTh[:, hh, :], Tswa[:, :], s.to_broadcast([P, 2 * P]),
                                   ALU.mult).then_inc(swa_ready, 1)
            pool.tensor_copy(ns[:, :], nsink[:, bass.ds(i * 2, 2)]).then_inc(swa_ready, 1)

        with nc.Block() as block:

            @block.sync
            def _(sp):
                with sp.Fori(0, PAIRS - 1) as i:
                    for s in range(2):
                        sp.wait_ge(q_low, i * 2 + (s + 1))
                        load(sp, wt[:, s], w["w_tiles"][bass.ds(i + (KV_TILES + PAIRS * s + 1), 1)].rearrange(
                            "a p (k c) -> p (a k) c", k=KD), q_in[s])

            @block.tensor
            def _(pe):
                prime(pe, q_made, 2)
                prime(pe, b.taken, 2)
                for n in range(LEAD):
                    pe_scores(pe, 0, n, b)
                pe_turn(pe, 0, 0, b)
                turns(pe, pe_pair)

            @block.scalar
            def _(act):
                prime(act, o_kept, 1)
                prime(act, so_kept, 1)
                prime(act, qn_kept, 1)
                prime(act, qs_kept, 1)
                for n in range(LEAD):
                    act_exp(act, 0, n, b)
                copy_turned(act, act.copy, 0, 0, b)
                turns(act, act_pair)

            @block.vector
            def _(dve):
                prime(dve, o_added, 1)
                for n in range(LEAD):
                    dve_shift(dve, 0, n, b)
                turns(dve, dve_pair)

            @block.gpsimd
            def _(pool):
                pool_nsa(pool, 0)
                pool_swa(pool, 0)
                prime(pool, q_low, 2)
                with pool.Fori(0, PAIRS - 1) as i:
                    for s in range(2):
                        pool.wait_ge(q_high, i * 2 + (s + 1))
                        pool.tensor_tensor(wt_lo[:, s], wt[:, s], wt_hi[:, s].bitcast(F32),
                                           ALU.subtract).then_inc(q_low, 1)
                    pool.wait_ge(b.shifted, i * N + NSA)
                    hold(pool, pool_passed)
                    pool_nsa(pool, i + 1)
                    pool.wait_ge(b.shifted, i * N + N)
                    pool.wait_ge(s_chain, i * 5 + 1)
                    hold(pool, pool_passed)
                    pool_swa(pool, i + 1)


def project_out(nc, oT, acc, w):
    with ExitStack() as ctx:
        m = Mem(nc, ctx)
        wo = m.sb("wo", [P, KD, D])
        ps = m.ps("psW", [P, 4, 512])
        wo_in = m.sem("wo_in0", "wo_in1")
        made, added = m.sem("wo_made", "wo_added")
        with nc.Block() as block:

            @block.sync
            def _(sp):
                for c in range(2):
                    load(sp, wo[:, c * 4:(c + 1) * 4, :],
                         w["w_out"][:, c * 4 * D:(c + 1) * 4 * D].rearrange("p (k n) -> p k n", n=D), wo_in[c])

            @block.tensor
            def _(pe):
                for n in range(2 * TT):
                    t, h = n // 2, n % 2
                    if n >= 4:
                        pe.wait_ge(added, n - 3)
                    for c in range(KD):
                        if n == 0 and c % 4 == 0:
                            pe.wait_ge(wo_in[c // 4], 16)
                        mm = pe.matmul(ps[:, n % 4, :], oT[:, c, t * P:(t + 1) * P],
                                       wo[:, c, h * HALF:(h + 1) * HALF], start=(c == 0), stop=(c == KD - 1))
                    mm.then_inc(made, 1)

            @block.vector
            def _(dve):
                for n in range(2 * TT):
                    t, h = n // 2, n % 2
                    dve.wait_ge(made, n + 1)
                    a = acc[:, t, h * HALF:(h + 1) * HALF]
                    dve.tensor_tensor(a, a, ps[:, n % 4, :], ALU.add).then_inc(added, 1)


class Activations:

    AHEAD = 4

    def __init__(self, m, h_hi, h_lo, uT):
        self.h_hi, self.h_lo, self.uT = h_hi, h_lo, uT
        self.raw = m.sb("u_raw", [P, 2, KD, P])
        self.hi = m.sb("u_hi", [P, 2, KD, P], F32R)
        self.lo = m.sb("u_lo", [P, 2, KD, P], F32R)
        self.ps = m.ps("psA2", [P, 2, 512])
        self.landed = m.sem("u_in0", "u_in1")
        self.high, self.low, self.made, self.gelued = m.sem("u_high", "u_low", "a_made", "gelued")

    def prime(self, sp, pe, act, pool):
        for eng, sems in ((pe, [self.made]), (act, [self.high, self.gelued]), (pool, [self.low])):
            if eng is not None:
                for sem in sems:
                    prime(eng, sem, self.AHEAD)

    def load(self, sp, b, s):
        sp.wait_ge(self.low, b + (self.AHEAD - 1))
        load(sp, self.raw[:, s, :, :], self.uT[bass.ds(b, 1)].rearrange("a p (k e) -> p (a k) e", k=KD),
             self.landed[s])

    def split_high(self, act, b, s, landed):
        act.wait_ge(self.landed[s], landed)
        act.wait_ge(self.made, b + (self.AHEAD - 1))
        act.copy(self.hi[:, s, :, :], self.raw[:, s, :, :]).then_inc(self.high, 1)

    def split_low(self, eng, b, s):
        eng.wait_ge(self.high, b + (self.AHEAD + 1))
        eng.tensor_tensor(self.lo[:, s, :, :], self.raw[:, s, :, :], self.hi[:, s, :, :].bitcast(F32),
                          ALU.subtract).then_inc(self.low, 1)

    def product(self, pe, b, s, first=0, end=KD):
        if first == 0:
            pe.wait_ge(self.low, b + (self.AHEAD + 1))
            pe.wait_ge(self.gelued, b + (self.AHEAD - 1))
        for c in range(first, end):
            pe.matmul(self.ps[:, s, :], self.hi[:, s, c, :], self.h_hi[:, c, :], start=(c == 0), stop=False)
            pe.matmul(self.ps[:, s, :], self.hi[:, s, c, :], self.h_lo[:, c, :], start=False, stop=False)
            mm = pe.matmul(self.ps[:, s, :], self.lo[:, s, c, :], self.h_hi[:, c, :], start=False,
                           stop=(c == KD - 1))
        if end == KD:
            mm.then_inc(self.made, 1)

    def gelu(self, act, b, s, out, passed=None):
        act.wait_ge(self.made, b + (self.AHEAD + 1))
        if passed is not None:
            hold(act, passed)
        act.activation(out, self.ps[:, s, :], ACT.Gelu_apprx_tanh).then_inc(self.gelued, 1)


def block_of(early, b):
    return early[:, bass.ds(b, 1), :].rearrange("p a t -> p (a t)")


def choose_experts(nc, sel_w, sel_e, w, blocks, early):
    with ExitStack() as ctx:
        m = Mem(nc, ctx)
        wq = m.sb("wq", [P, 2, KD, P])
        wq_hi = m.sb("wq_hi", [P, 2, KD, P], F32R)
        wq_lo = m.sb("wq_lo", [P, 2, KD, P], F32R)
        keys = m.sb("keys", [P, 2, NK])
        qp = m.sb("qp", [P, 2, SEQ])
        sc = m.sb("sc", [P, 2, TT, NK])
        rest = m.sb("rest", [P, 2, TT, NK])
        top = m.sb("top", [P, 2, TT, TOPK])
        at = m.sb("at", [P, 2, TT, TOPK], U32)
        atf = m.sb("atf", [P, 2, TT, TOPK])
        cand = m.sb("cand", [P, TT, TOPK * TOPK])
        crest = m.sb("crest", [P, TT, TOPK * TOPK])
        best = m.sb("best", [P, TT, TOPK])
        cat = m.sb("cat", [P, TT, TOPK], U32)
        ab = m.sb("ab", [P, 2, TT, TOPK], U32)
        abf = m.sb("abf", [P, 2, TT, TOPK])
        eq = m.sb("eq", [P, 2 * TT, TOPK, TOPK])
        gsum = m.sb("gsum", [P, TT * PH])
        psQ = m.ps("psQ2", [P, 2, 512])
        psS = m.ps("psS2", [P, 2, TT, NK])
        wq_in = m.sem("wq_in0", "wq_in1")
        wq_high, wq_low = m.sem("wq_high", "wq_low")
        passed, a_passed, pool_passed = m.sem("e_passed", "ea_passed", "ep_passed")
        (keys_in, q_made, q_kept, s_made, s_kept, max1, cut1, max2, at2, cands, cmax1, ccut1, cmax2, cat2, split,
         eqd, mulled, picked, g1) = m.sem(
            "keys_in", "pq_made", "pq_kept", "ps_made", "ps_kept", "max1", "cut1", "max2", "at2", "cands", "cmax1",
            "ccut1", "cmax2", "cat2", "split", "eqd", "mulled", "picked", "g1")
        with nc.Block() as block:

            @block.sync
            def _(sp):
                load(sp, blocks.raw[:, 0, :, :], w["uT"][0].rearrange("p (k e) -> p k e", k=KD), blocks.landed[0])
                load(sp, blocks.raw[:, 1, :, :], w["uT"][1].rearrange("p (k e) -> p k e", k=KD), blocks.landed[1])
                with sp.Fori(0, PH // 2) as i:
                    for par in range(2):
                        h = i * 2 + par
                        for c in range(2):
                            sp.wait_ge(wq_low, h * 2 + (c + 1))
                            load(sp, wq[:, c], w["wq"][bass.ds(h * 2 + c, 1)].rearrange(
                                "a p (k c) -> p (a k) c", k=KD), wq_in[c])
                        sp.wait_ge(s_made, h * 2 + 2)
                        load(sp, keys[:, :, :], w["keys"][bass.ds(h, 1)].rearrange(
                            "a p (c n) -> p (a c) n", c=2), keys_in)
                        blocks.load(sp, h + 2, par)
                for b in range(PH, PH + 2):
                    blocks.load(sp, b + 2, b % 2)

            @block.tensor
            def _(pe):
                blocks.prime(None, pe, None, None)
                prime(pe, q_made, 2)
                prime(pe, s_made, 2)
                with pe.Fori(0, PH // 2) as i:
                    for par in range(2):
                        h = i * 2 + par
                        for c in range(2):
                            pe.wait_ge(wq_low, h * 2 + (c + 3))
                            for k in range(KD):
                                pe.matmul(psQ[:, c, :], wq_hi[:, c, k, :], blocks.h_hi[:, k, :], start=(k == 0),
                                          stop=False)
                                pe.matmul(psQ[:, c, :], wq_hi[:, c, k, :], blocks.h_lo[:, k, :], start=False,
                                          stop=False)
                                mm = pe.matmul(psQ[:, c, :], wq_lo[:, c, k, :], blocks.h_hi[:, k, :], start=False,
                                               stop=(k == KD - 1))
                            mm.then_inc(q_made, 1)
                        blocks.product(pe, h, par)
                        pe.wait_ge(keys_in, h * 16 + 16)
                        for c in range(2):
                            pe.wait_ge(q_kept, h * 2 + c + 1)
                            pe.wait_ge(s_kept, h * 2 + 2)
                            for t in range(TT):
                                mm = pe.matmul(psS[:, c, t, :], qp[:, c, t * P:(t + 1) * P], keys[:, c, :],
                                               start=True, stop=True)
                            mm.then_inc(s_made, 1)
                for b in range(PH, PH + 2):
                    blocks.product(pe, b, b % 2)

            def act_head(act, h, i, par, split_next=True):
                for c in range(2):
                    act.wait_ge(s_made, h * 2 + 2)
                    act.wait_ge(q_made, h * 2 + (c + 3))
                    act.copy(qp[:, c, :], psQ[:, c, :]).then_inc(q_kept, 1)
                if split_next:
                    for c in range(2):
                        act.wait_ge(wq_in[c], h * 16 + 32)
                        act.copy(wq_hi[:, c, :, :], wq[:, c, :, :]).then_inc(wq_high, 1)
                blocks.gelu(act, h, par, block_of(early, h), a_passed)
                blocks.split_high(act, h + 2, par, i * 16 + 32)
                act.wait_ge(cut1, h * 16 + 16)
                for c in range(2):
                    act.wait_ge(s_made, h * 2 + (c + 3))
                    act.copy(sc[:, c, :, :], psS[:, c, :, :]).then_inc(s_kept, 1)

            @block.scalar
            def _(act):
                blocks.prime(None, None, act, None)
                for s in range(2):
                    blocks.split_high(act, s, s, 16)
                prime(act, s_kept, 2)
                for c in range(2):
                    act.wait_ge(wq_in[c], 16)
                    act.copy(wq_hi[:, c, :, :], wq[:, c, :, :]).then_inc(wq_high, 1)
                with act.Fori(0, PH // 2 - 1) as i:
                    for par in range(2):
                        act_head(act, i * 2 + par, i, par)
                act_head(act, PH - 2, PH // 2 - 1, 0)
                act_head(act, PH - 1, PH // 2 - 1, 1, split_next=False)
                for b in range(PH, PH + 2):
                    blocks.gelu(act, b, b % 2, early[:, b, :])
                    blocks.split_high(act, b + 2, b % 2, 16 * ((b + 2) // 2 + 1))

                act.wait_ge(g1, 1)
                act.activation(sel_w[:, :, :], sel_w[:, :, :], ACT.Exp).then_inc(g1, 1)

            @block.gpsimd
            def _(pool):
                blocks.prime(None, None, None, pool)
                for s in range(2):
                    blocks.split_low(pool, s, s)
                prime(pool, mulled, 1)
                with pool.Fori(0, PH // 2) as i:
                    for par in range(2):
                        h = i * 2 + par
                        blocks.split_low(pool, h + 2, par)
                        pool.wait_ge(picked, h * 3 + 3)
                        pool.wait_ge(split, h * 4 + 4)
                        hold(pool, pool_passed)
                        for j in range(TOPK):
                            pool.tensor_scalar(eq[:, :, :, j], abf[:, :, :, :].rearrange("p c t s -> p (c t) s"), float(j),
                                               None, ALU.is_equal).then_inc(eqd, 1)
                        pool.wait_ge(eqd, h * TOPK + TOPK)
                        pool.tensor_tensor(eq[:, :, :, :], eq[:, :, :, :],
                                           atf[:, :, :, :].rearrange("p c t j -> p (c t) j").unsqueeze(2).to_broadcast(
                                               [P, 2 * TT, TOPK, TOPK]), ALU.mult).then_inc(mulled, 1)

            def dve_wq(dve, h):
                for c in range(2):
                    dve.wait_ge(wq_high, h * 2 + (c + 1))
                    dve.tensor_tensor(wq_lo[:, c, :, :], wq[:, c, :, :], wq_hi[:, c, :, :].bitcast(F32),
                                      ALU.subtract).then_inc(wq_low, 1)

            def dve_pick(dve, h):
                dve.wait_ge(mulled, h + 2)
                for c in range(2):
                    dve.tensor_reduce(sel_e[:, c, :, bass.ds(h * TOPK, TOPK)],
                                      eq[:, c * TT:(c + 1) * TT, :, :], AX.X, ALU.add).then_inc(picked, 1)

            def dve_head(dve, h, h_before, split_next=True):
                ct = [(c, t) for c in range(2) for t in range(TT)]
                if split_next:
                    dve_wq(dve, h + 1)
                for c, t in ct:
                    if t == 0:
                        dve.wait_ge(s_kept, h * 2 + (c + 3))
                        hold(dve, passed)
                    dve.max(top[:, c, t, 0:8], sc[:, c, t, :]).then_inc(max1, 1)
                dve.wait_ge(max1, h * 8 + 8)
                hold(dve, passed)
                for c, t in ct:
                    dve.max_index(at[:, c, t, 0:8], top[:, c, t, 0:8], sc[:, c, t, :]).then_inc(cut1, 1)
                    dve.match_replace(rest[:, c, t, :], top[:, c, t, 0:8], sc[:, c, t, :],
                                      -3.0e38).then_inc(cut1, 1)
                dve.wait_ge(cut1, h * 16 + 32)
                hold(dve, passed)
                for c, t in ct:
                    dve.max(top[:, c, t, 8:16], rest[:, c, t, :]).then_inc(max2, 1)
                dve.wait_ge(max2, h * 8 + 8)
                dve.tensor_tensor(cand[:, :, :].rearrange("p t (a b) -> p t a b", a=TOPK),
                                  top[:, 0].unsqueeze(3).to_broadcast([P, TT, TOPK, TOPK]),
                                  top[:, 1].unsqueeze(2).to_broadcast([P, TT, TOPK, TOPK]),
                                  ALU.add).then_inc(cands, 1)
                for c, t in ct:
                    dve.max_index(at[:, c, t, 8:16], top[:, c, t, 8:16], rest[:, c, t, :]).then_inc(at2, 1)
                dve.wait_ge(cands, h + 1)
                hold(dve, passed)
                for t in range(TT):
                    dve.max(best[:, t, 0:8], cand[:, t, :]).then_inc(cmax1, 1)
                dve.wait_ge(cmax1, h * 4 + 4)
                hold(dve, passed)
                for t in range(TT):
                    dve.max_index(cat[:, t, 0:8], best[:, t, 0:8], cand[:, t, :]).then_inc(ccut1, 1)
                    dve.match_replace(crest[:, t, :], best[:, t, 0:8], cand[:, t, :], -3.0e38).then_inc(ccut1, 1)
                dve.wait_ge(at2, h * 8 + 8)
                if h_before is not None:
                    dve_pick(dve, h_before)
                dve.tensor_copy(atf[:, :, :, :], at[:, :, :, :]).then_inc(split, 1)
                dve.wait_ge(ccut1, h * 8 + 8)
                hold(dve, passed)
                for t in range(TT):
                    dve.max(best[:, t, 8:16], crest[:, t, :]).then_inc(cmax2, 1)
                dve.wait_ge(cmax2, h * 4 + 4)
                hold(dve, passed)
                for t in range(TT):
                    dve.max_index(cat[:, t, 8:16], best[:, t, 8:16], crest[:, t, :]).then_inc(cat2, 1)
                dve.wait_ge(cat2, h * 4 + 4)
                dve.tensor_single_scalar(ab[:, 0, :, :], cat[:, :, :], 4, ALU.logical_shift_right).then_inc(split, 1)
                dve.tensor_single_scalar(ab[:, 1, :, :], cat[:, :, :], 15, ALU.bitwise_and).then_inc(split, 1)
                dve.wait_ge(split, h * 4 + 3)
                dve.tensor_copy(abf[:, :, :, :], ab[:, :, :, :]).then_inc(split, 1)
                dve.wait_ge(cmax2, h * 4 + 4)
                dve.tensor_tensor(sel_w[:, :, bass.ds(h * TOPK, TOPK)], best[:, :, :],
                                  best[:, :, 0:1].to_broadcast([P, TT, TOPK]), ALU.subtract).then_inc(picked, 1)

            @block.vector
            def _(dve):
                prime(dve, cut1, 16)
                prime(dve, picked, 3)
                prime(dve, wq_low, 2)
                dve_wq(dve, 0)
                dve_head(dve, 0, None)
                with dve.Fori(1, PH - 1) as h:
                    dve_head(dve, h, h - 1)
                dve_head(dve, PH - 1, PH - 2, split_next=False)
                dve_pick(dve, PH - 1)
                dve.wait_ge(picked, 3 * PH + 3)
                dve.engine_nop().then_inc(g1, 1)
                dve.wait_ge(g1, 2)
                slots = sel_w[:, :, :].rearrange("p t (h s) -> p (t h) s", s=TOPK)
                dve.tensor_reduce(gsum[:, :], slots, AX.X, ALU.add).then_inc(g1, 1)
                dve.wait_ge(g1, 3)
                dve.reciprocal(gsum[:, :], gsum[:, :]).then_inc(g1, 1)
                dve.wait_ge(g1, 4)
                dve.tensor_tensor(slots, slots, gsum[:, :].unsqueeze(2).to_broadcast([P, TT * PH, TOPK]),
                                  ALU.mult).then_inc(g1, 1)


def gate_matrix(nc, ident, iota, sel_w, sel_e, gates, blocks, early):
    QUADS = TC // 4
    RING = 4
    with ExitStack() as ctx:
        m = Mem(nc, ctx)
        e1T = m.sb("e1T", [P, SEQ], BF16)
        e2T = m.sb("e2T", [P, SEQ], BF16)
        iota4 = m.sb("iota4", [P, P, 4], BF16)
        rest = m.sb("w_rest", [P, 3, SEQ])
        parts = m.sb("w_part", [P, 3, SEQ], BF16)
        hot = m.sb("hot", [P, RING, 5, P, 4], BF16)
        stage = m.sb("stage", [P, 2, NK, TC])
        psT = m.ps("gpsT", [P, 2, SEQ])
        psG = m.ps("psG", [P, RING, 4, P])
        pool_passed, laid = m.sem("g_passed", "iota_laid")
        turned, kept, high, low, one_hot, scaled, scaled2, summed, staged, a_passed = m.sem(
            "g_turned", "g_kept", "g_high", "g_low", "one_hot", "hot_scaled", "hot_scaled2", "g_summed", "g_staged",
            "ga_passed")
        stored = m.sem("g_stored0", "g_stored1")
        PARTS = {n: (s, 2 * j, 2 * j + 2) for s in range(2) for j, n in enumerate(range(8 * s, 8 * s + 8, 2))}
        MADE = (6, 14)
        with nc.Block() as block:

            @block.tensor
            def _(pe):
                for n, src in enumerate((sel_e[:, 0], sel_e[:, 1], sel_w)):
                    if n == 2:
                        pe.wait_ge(kept, 1)
                    for t in range(TT):
                        mm = pe.transpose(psT[:, n % 2, t * P:(t + 1) * P], src[:, t, :], ident[:, :])
                    mm.then_inc(turned, 1)
                for b in range(PH + 2, EARLY0):
                    blocks.product(pe, b, b % 2)
                prime(pe, summed, RING)
                with pe.Fori(0, SEQ // TC // 2) as i:
                    for q in range(2 * QUADS):
                        n = i * (2 * QUADS) + q
                        pe.wait_ge(scaled, n * 2 + 2)
                        pe.wait_ge(scaled2, n + 1)
                        pe.wait_ge(staged, n + 1)
                        for a in range(4):
                            for part in range(3):
                                mm = pe.matmul(psG[:, q % RING, a, :], hot[:, q % RING, 0, :, a],
                                               hot[:, q % RING, part + 2, :, a], start=(part == 0),
                                               stop=(part == 2))
                        mm.then_inc(summed, 1)
                        if q in PARTS:
                            s, first, end = PARTS[q]
                            blocks.product(pe, i * 2 + (EARLY0 + s), s, first, end)

            def spread(e, i, q):
                return e[:, bass.ds(i * (2 * TC) + q * 4, 4)].unsqueeze(1).to_broadcast([P, P, 4])

            @block.gpsimd
            def _(pool):
                for b in range(PH + 2, EARLY0 + 1):
                    blocks.split_low(pool, b, b % 2)
                pool.wait_ge(low, 2)
                with pool.Fori(0, SEQ // TC // 2) as i:
                    for q in range(2 * QUADS):
                        pool.wait_ge(one_hot, i * (4 * QUADS) + q * 2 + 2)
                        hold(pool, pool_passed)
                        pool.tensor_tensor(hot[:, q % RING, 4, :, :], hot[:, q % RING, 1, :, :],
                                           spread(parts[:, 2, :], i, q), ALU.mult).then_inc(scaled2, 1)
                        if q == 3:
                            blocks.split_low(pool, i * 2 + (EARLY0 + 1), 1)
                blocks.split_low(pool, EARLY + 1, 1)

            @block.vector
            def _(dve):
                dve.tensor_copy(iota4[:, :, :], iota[:, :].unsqueeze(2).to_broadcast([P, P, 4])).then_inc(laid, 1)
                for n, dst in enumerate((e1T[:, :], e2T[:, :], rest[:, 0, :])):
                    dve.wait_ge(turned, n + 1)
                    dve.tensor_copy(dst, psT[:, n % 2, :]).then_inc(kept, 1)
                dve.wait_ge(kept, 3)
                for n in range(3):
                    dve.tensor_copy(parts[:, n, :], rest[:, n, :]).then_inc(high, 1)
                    dve.wait_ge(high, n + 1)
                    if n < 2:
                        dve.tensor_tensor(rest[:, n + 1, :], rest[:, n, :], parts[:, n, :],
                                          ALU.subtract).then_inc(low, 1)
                        dve.wait_ge(low, n + 1)
                dve.wait_ge(laid, 1)
                with dve.Fori(0, SEQ // TC // 2) as i:
                    for q in range(2 * QUADS):
                        dve.wait_ge(summed, i * (2 * QUADS) + q + 1)
                        for n, e in ((1, e1T), (0, e2T)):
                            dve.tensor_tensor(hot[:, q % RING, n, :, :], iota4[:, :, :], spread(e[:, :], i, q),
                                              ALU.is_equal).then_inc(one_hot, 1)
                        dve.wait_ge(one_hot, i * (4 * QUADS) + q * 2 + 1)
                        for n in range(2):
                            dve.tensor_tensor(hot[:, q % RING, n + 2, :, :], hot[:, q % RING, 1, :, :],
                                              spread(parts[:, n, :], i, q), ALU.mult).then_inc(scaled, 1)
                        if q == 12:
                            dve.wait_ge(blocks.low, i * 2 + (EARLY0 + 2 + blocks.AHEAD))
                            blocks.split_low(dve, i * 2 + (EARLY0 + 2), 0)

            @block.scalar
            def _(act):
                for b in range(PH + 2, EARLY0):
                    blocks.gelu(act, b, b % 2, early[:, b, :])
                    blocks.split_high(act, b + 2, b % 2, 16 * ((b + 2) // 2 + 1))
                prime(act, staged, RING)
                for s in range(2):
                    prime(act, stored[s], 16)
                with act.Fori(0, SEQ // TC // 2) as i:
                    for q in range(2 * QUADS):
                        act.wait_ge(summed, i * (2 * QUADS) + q + (RING + 1))
                        s = q // QUADS
                        if q % QUADS == 0:
                            act.wait_ge(stored[s], i * 16 + 16)
                        t = (q % QUADS) * 4
                        act.copy(stage[:, s, :, t:t + 4], psG[:, q % RING, :, :].rearrange("p a i -> p i a")
                                 ).then_inc(staged, 1)
                        if q - 1 in MADE:
                            s = MADE.index(q - 1)
                            blocks.gelu(act, i * 2 + (EARLY0 + s), s, block_of(early, i * 2 + (EARLY0 + s)), a_passed)
                            blocks.split_high(act, i * 2 + (EARLY0 + s + 2), s, i * 16 + 16 * (EARLY0 // 2 + 2))

            @block.sync
            def _(sp):
                for b in range(PH + 2, EARLY0):
                    blocks.load(sp, b + 2, b % 2)
                with sp.Fori(0, SEQ // TC // 2) as i:
                    for s in range(2):
                        blocks.load(sp, i * 2 + (EARLY0 + s + 2), s)
                        sp.wait_ge(staged, i * (2 * QUADS) + ((s + 1) * QUADS + RING))
                        sp.dma_start(gates[bass.ds(i * 2 + s, 1)].rearrange("a p i t -> p (a i) t"),
                                     stage[:, s, :, :]).then_inc(stored[s], 16)
                for s in range(2):
                    sp.wait_ge(stored[s], 16 + 16 * (SEQ // TC // 2))


def experts(nc, acc, gates, w, blocks, early):
    A = blocks.AHEAD
    with ExitStack() as ctx:
        m = Mem(nc, ctx)
        v_raw = m.sb("v_raw", [P, BG, HALF])
        v_hi = m.sb("v_hi", [P, BG, HALF], F32R)
        v_lo = m.sb("v_lo", [P, BG, HALF], F32R)
        g_sb = m.sb("g_sb", [P, 2, SEQ // TC, BG, TC])
        activ = early[:, 0:BG, :]
        w_hi = m.sb("w_hi", [P, 2, BG, SEQ], F32R)
        w_lo = m.sb("w_lo", [P, 2, BG, SEQ], F32R)
        psB = m.ps("psB", [P, TT, HALF])
        v_in = m.sem(*[f"v_in{blk}" for blk in range(BG)])
        g_in = m.sem("g_in0", "g_in1")
        (v_high, v_low, multiplied, w_high, w_low, b_step, b_made, drained) = m.sem(
            "v_high", "v_low", "multiplied", "w_high", "w_low", "b_step", "b_made", "drained")

        def pe_b(pe, g, par, half):
            if half == 0:
                pe.wait_ge(w_low, g * 4 + 4)
            for blk in range(BG):
                pe.wait_ge(v_low, g * 8 + (half * 4 + blk + 1))
                for t in range(TT):
                    if blk == 0:
                        pe.wait_ge(drained, g * 8 + (half * 4 + t + 1))
                    ts = slice(t * P, (t + 1) * P)
                    pe.matmul(psB[:, t, :], w_hi[:, par, blk, ts], v_hi[:, blk, :], start=(blk == 0), stop=False)
                    pe.matmul(psB[:, t, :], w_hi[:, par, blk, ts], v_lo[:, blk, :], start=False, stop=False)
                    mm = pe.matmul(psB[:, t, :], w_lo[:, par, blk, ts], v_hi[:, blk, :], start=False,
                                   stop=(blk == BG - 1))
                    if blk == BG - 1:
                        mm.then_inc(b_made, 1)
                if blk < BG - 1:
                    mm.then_inc(b_step, 1)

        def slot_free(eng, g, half, blk):
            if blk < BG - 1:
                from_one(eng, b_step, (g * 2 + half - 1) * 3 + blk + 1)
            else:
                from_one(eng, b_made, (g * 2 + half) * 4 + 1)

        def act_u(act, gb, k):
            blocks.split_high(act, gb * 4 + k, k % 2, gb * 32 + 16 * (k // 2 + 1))

        def w_in(b, k, made_early):
            return block_of(early, b) if made_early else activ[:, k, :]

        def act_w(act, gb, par, k, made_early):
            b = gb * 4 + k
            if not made_early:
                act.wait_ge(w_low, b - 3)
                blocks.gelu(act, b, k % 2, activ[:, k, :])
            act.wait_ge(multiplied, b + 1)
            from_one(act, b_made, (gb - 1) * 8 + 1)
            act.copy(w_hi[:, par, k, :], w_in(b, k, made_early)).then_inc(w_high, 1)

        def act_v(act, g, half, blk):
            act.wait_ge(v_in[blk], g * 32 + half * 16 + 16)
            slot_free(act, g, half, blk)
            act.copy(v_hi[:, blk, :], v_raw[:, blk, :]).then_inc(v_high, 1)

        def dve_u(dve, gb, k):
            blocks.split_low(dve, gb * 4 + k, k % 2)

        def dve_w(dve, gb, par, k, g_count, made_early):
            b = gb * 4 + k
            dve.wait_ge(g_in[par], g_count)
            if not made_early:
                dve.wait_ge(blocks.gelued, b + (A + 1))
            a = w_in(b, k, made_early)
            chunks = a.rearrange("p (c t) -> p c t", t=TC)
            dve.tensor_tensor(chunks, chunks, g_sb[:, par, :, k, :], ALU.mult).then_inc(multiplied, 1)
            dve.wait_ge(w_high, b + 1)
            dve.tensor_tensor(w_lo[:, par, k, :], a, w_hi[:, par, k, :].bitcast(F32),
                              ALU.subtract).then_inc(w_low, 1)

        def dve_v(dve, g, half, blk):
            dve.wait_ge(v_high, g * 8 + (half * 4 + blk + 1))
            dve.tensor_tensor(v_lo[:, blk, :], v_raw[:, blk, :], v_hi[:, blk, :].bitcast(F32),
                              ALU.subtract).then_inc(v_low, 1)

        def dve_drain(dve, g, half):
            for t in range(TT):
                dve.wait_ge(b_made, g * 8 + (half * 4 + t + 2))
                a = acc[:, t, half * HALF:(half + 1) * HALF]
                dve.tensor_tensor(a, a, psB[:, t, :], ALU.add).then_inc(drained, 1)

        def sp_u(sp, gb, k):
            blocks.load(sp, gb * 4 + k, k % 2)

        def sp_v(sp, g, half):
            for blk in range(BG):
                from_one(sp, v_low, g * 8 + (half * 4 + blk - 3))
                load(sp, v_raw[:, blk, :], w["v"][bass.ds(g * 4 + blk, 1), :, half * HALF:(half + 1) * HALF].rearrange(
                    "b p d -> p (b d)"), v_in[blk])

        def sp_g(sp, gb, par):
            from_one(sp, multiplied, gb * 4 - 4)
            load(sp, g_sb[:, par, :, :, :], gates[:, :, bass.ds(gb * 4, 4), :].rearrange(
                "c p i t -> p c (i t)"), g_in[par])

        ALL, EARLIER, NONE = range(3)

        def sp_turn(sp, g, par, a=ALL, u=True, v=True, gs=True):
            if gs:
                sp_g(sp, g + 2, par)
            for half in range(2):
                if a == ALL and u:
                    for k in (2 * half, 2 * half + 1):
                        sp_u(sp, g + 2, k)
                if v:
                    sp_v(sp, g + 1, half)

        def pe_turn(pe, g, par, a=ALL):
            for half in range(2):
                if a == ALL:
                    for k in (2 * half, 2 * half + 1):
                        blocks.product(pe, (g + 1) * 4 + k, k % 2)
                pe_b(pe, g, par, half)

        def next_u(split, eng, gb, k):
            split(eng, gb + k // 2, (k + 2) % 4)

        def act_turn(act, g, par, a=ALL, u=True, v=True):
            for half in range(2):
                if a != NONE:
                    for k in (2 * half, 2 * half + 1):
                        if a == ALL and (u or k < 2):
                            next_u(act_u, act, g + 1, k)
                        act_w(act, g + 1, 1 - par, k, a == EARLIER)
                if half == 0 or v:
                    for blk in range(BG):
                        act_v(act, g + half, 1 - half, blk)

        def dve_turn(dve, g, par, g_count, a=ALL, u=True, v=True):
            for half in range(2):
                if a != NONE:
                    for k in (2 * half, 2 * half + 1):
                        if a == ALL and (u or k < 2):
                            next_u(dve_u, dve, g + 1, k)
                        dve_w(dve, g + 1, 1 - par, k, g_count, a == EARLIER)
                if half == 0 or v:
                    for blk in range(BG - 1):
                        dve_v(dve, g + half, 1 - half, blk)
                dve_drain(dve, g, half)
                if half == 0 or v:
                    dve_v(dve, g + half, 1 - half, BG - 1)

        FIRST = EARLY // BG - 1
        assert EARLY % BG == 0 and FIRST % 2 == 0
        LAST = GROUPS - 2
        with nc.Block() as block:

            @block.sync
            def _(sp):
                sp_g(sp, 0, 0)
                sp_v(sp, 0, 0)
                sp_g(sp, 1, 1)
                sp_v(sp, 0, 1)
                with sp.Fori(0, FIRST // 2) as i:
                    for par in range(2):
                        sp_turn(sp, i * 2 + par, par, a=EARLIER)
                for k in (2, 3):
                    sp_u(sp, FIRST + 1, k)
                with sp.Fori(FIRST // 2, LAST // 2) as i:
                    for par in range(2):
                        sp_turn(sp, i * 2 + par, par)
                sp_turn(sp, LAST, 0, u=False, gs=False)

            @block.tensor
            def _(pe):
                prime(pe, b_made, 1)
                with pe.Fori(0, FIRST // 2) as i:
                    for par in range(2):
                        pe_turn(pe, i * 2 + par, par, a=EARLIER)
                with pe.Fori(FIRST // 2, LAST // 2) as i:
                    for par in range(2):
                        pe_turn(pe, i * 2 + par, par)
                pe_turn(pe, LAST, 0)
                pe_turn(pe, LAST + 1, 1, a=NONE)

            @block.scalar
            def _(act):
                for k in range(BG):
                    act_w(act, 0, 0, k, True)
                for blk in range(BG):
                    act_v(act, 0, 0, blk)
                with act.Fori(0, FIRST // 2) as i:
                    for par in range(2):
                        act_turn(act, i * 2 + par, par, a=EARLIER)
                with act.Fori(FIRST // 2, LAST // 2) as i:
                    for par in range(2):
                        act_turn(act, i * 2 + par, par)
                act_turn(act, LAST, 0, u=False)
                act_turn(act, LAST + 1, 1, a=NONE, v=False)

            @block.vector
            def _(dve):
                prime(dve, drained, TT)
                for k in range(BG):
                    dve_w(dve, 0, 0, k, 16, True)
                for blk in range(BG):
                    dve_v(dve, 0, 0, blk)
                with dve.Fori(0, FIRST // 2) as i:
                    for par in range(2):
                        dve_turn(dve, i * 2 + par, par, (i + 1 + par) * 16, a=EARLIER)
                with dve.Fori(FIRST // 2, LAST // 2) as i:
                    for par in range(2):
                        dve_turn(dve, i * 2 + par, par, (i + 1 + par) * 16)
                dve_turn(dve, LAST, 0, (GROUPS // 2) * 16, u=False)
                dve_turn(dve, LAST + 1, 1, 0, a=NONE, v=False)


def final_norm(nc, acc, out, w):
    with ExitStack() as ctx:
        m = Mem(nc, ctx)
        gain = m.sb("f_gain", [P, D])
        sq = m.sb("f_sq", [P, D])
        ss = m.sb("f_ss", [P, TT])
        ms = m.sb("f_ms", [P, TT])
        half = m.sb("f_half", [P, TT])
        rstd = m.sb("f_rstd", [P, TT])
        gain_in, squared, mean, rooted, scaled, out_done = m.sem("f_gain_in", "f_squared", "f_mean", "f_rooted",
                                                                 "f_scaled", "out_done")
        with nc.Block() as block:

            @block.sync
            def _(sp):
                load(sp, gain[:, :], w["lnf"].partition_broadcast(P), gain_in)
                for t in range(TT):
                    sp.wait_ge(scaled, t + 1)
                    sp.dma_start(out[t * P:(t + 1) * P, :], acc[:, t, :]).then_inc(out_done, 16)
                sp.wait_ge(out_done, 16 * TT)

            @block.scalar
            def _(act):
                for t in range(TT):
                    act.activation(sq[:, :], acc[:, t, :], ACT.Square, accum_out=ss[:, t:t + 1]).then_inc(squared, 1)
                    act.wait_ge(squared, t + 1)

            @block.gpsimd
            def _(pool):
                pool.memset(half[:, :], -0.5).then_inc(mean, 1)
                pool.wait_ge(squared, TT)
                pool.tensor_scalar(ms[:, :], ss[:, :], 1.0 / D, EPS, ALU.mult, ALU.add).then_inc(mean, 1)
                pool.wait_ge(mean, 2)
                pool.tensor_tensor(rstd[:, :], ms[:, :], half[:, :], ALU.pow).then_inc(rooted, 1)

            @block.vector
            def _(dve):
                dve.wait_ge(gain_in, 16)
                dve.wait_ge(rooted, 1)
                for t in range(TT):
                    dve.scalar_tensor_tensor(out=acc[:, t, :], in0=acc[:, t, :], scalar=rstd[:, t:t + 1],
                                             in1=gain[:, :], op0=ALU.mult, op1=ALU.mult).then_inc(scaled, 1)


def program(nc, w, out):
    with ExitStack() as ctx:
        m = Mem(nc, ctx)
        acc = m.sb("acc", [P, TT, D])
        ident = m.sb("ident", [P, P])
        gains = m.sb("gains", [P, 2, KD])
        iota = m.sb("iota", [P, P])
        x_in, small_in = m.sem("x_in", "small_in")
        with nc.Block() as block:

            @block.sync
            def _(sp):
                load(sp, acc[:, :, :], w["x"].rearrange("(t p) d -> p t d", p=P), x_in)
                load(sp, ident[:, :], w["ident"], small_in)
                load(sp, iota[:, :], w["iota"], small_in)
                load(sp, gains[:, :, :], w["gains"].rearrange("p (a k) -> p a k", a=2), small_in)

        with ExitStack() as ctx2:
            m2 = Mem(nc, ctx2)
            oT = m2.sb("oT", [P, KD, SEQ])
            with ExitStack() as ctx3:
                m3 = Mem(nc, ctx3)
                a_hi = m3.sb("a_hi", [P, KD, SEQ], F32R)
                a_lo = m3.sb("a_lo", [P, KD, SEQ], F32R)
                with ExitStack() as ctx4:
                    aT = Mem(nc, ctx4).sb("aT", [P, KD, SEQ])
                    norm_transposed(nc, "n1", acc, [(x_in, 16)], gains[:, 0, :], [(small_in, 48)], ident, aT,
                                    a_hi, a_lo)
                attention(nc, m3, a_hi, a_lo, ident, oT, w)
            project_out(nc, oT, acc, w)

        gates = nc.dram_tensor("gate_scratch", (SEQ // TC, P, NK, TC), F32, kind="Internal").ap()
        h_hi = m.sb("h_hi", [P, KD, SEQ], F32R)
        h_lo = m.sb("h_lo", [P, KD, SEQ], F32R)
        blocks = Activations(m, h_hi, h_lo, w["uT"])
        early = m.sb("early", [P, EARLY, SEQ])
        with ExitStack() as ctx2:
            m2 = Mem(nc, ctx2)
            sel_w = m2.sb("sel_w", [P, TT, SEL])
            sel_e = m2.sb("sel_e", [P, 2, TT, SEL])
            with ExitStack() as ctx3:
                hT = Mem(nc, ctx3).sb("hT", [P, KD, SEQ])
                norm_transposed(nc, "n2", acc, [], gains[:, 1, :], [(small_in, 48)], ident, hT, h_hi, h_lo)
            choose_experts(nc, sel_w, sel_e, w, blocks, early)
            gate_matrix(nc, ident, iota, sel_w, sel_e, gates, blocks, early)
        experts(nc, acc, gates, w, blocks, early)
        final_norm(nc, acc, out, w)


def constants():
    q = np.arange(P)[:, None]
    dist = 384 + q - np.arange(SEQ)[None]
    t_nsa = np.where(dist >= 0, dist, MASKED)
    tq = np.arange(SEQ).reshape(TT, P).T[:, :, None]
    dc = tq - (np.arange(NCMP) * CMP_STRIDE + CMP_LEN - 1)[None, None]
    t_cmp = np.where(dc >= 0, dc, MASKED).reshape(P, -1)
    ds = P + q - np.arange(2 * P)[None]
    t_swa = np.where((ds >= 0) & (ds < SWA_WIN), ds, MASKED)
    n = NSA_HEADS + SWA_HEADS
    slopes = (2.0 ** (-8.0 * (np.arange(n) + 1) / n)).astype(np.float32)
    f = lambda a: np.ascontiguousarray(a, np.float32)
    return {"t_nsa": f(t_nsa), "t_cmp": f(t_cmp), "t_swa": f(t_swa),
            "slopes": f(np.broadcast_to(slopes, (P, n))), "ident": f(np.eye(P)),
            "iota": f(np.broadcast_to(np.arange(P), (P, P)))}


def layouts(x, ln1_g, w_in, cmp_pe_k, cmp_w1_k, cmp_w2_k, cmp_pe_v, cmp_w1_v, cmp_w2_v, swa_sinks, w_out,
            ln2_g, peer_wq, peer_keys, peer_u, peer_v, lnf_g):
    c = np.ascontiguousarray
    w_in = np.asarray(w_in)[0]
    cut = np.cumsum([512, 128, 128, 128, 128, 128, 128, 24, 512, 64, 64])[:-1]
    q_n, kc, vc, ks, vs, kw, vw, gt, q_s, k_s, v_s = np.split(w_in, cut, axis=1)
    head = lambda q, h: q[:, h * HD:(h + 1) * HD]
    tiles = [kc, vc, ks, kw, np.concatenate([k_s, k_s], 1)]
    tiles += [np.concatenate([head(q_n, j), head(q_n, j + 4)], 1) for j in range(PAIRS)]
    tiles += [q_s[:, j * P:(j + 1) * P] for j in range(PAIRS)]
    chunked = lambda a: a.reshape(KD, P, -1).transpose(1, 0, 2).reshape(P, -1)
    gates = gt.reshape(D, NSA_HEADS, 3).transpose(0, 2, 1).reshape(D, 24)
    nat = np.concatenate([vs, vw, v_s, gates], 1)
    pe = [np.asarray(a)[0].reshape(LP, 2, HD).transpose(1, 2, 0).reshape(P, LP) for a in (cmp_pe_k, cmp_pe_v)]
    w1 = [np.asarray(a)[0].reshape(LP, P, CMP_HID).transpose(1, 0, 2).reshape(P, -1) for a in (cmp_w1_k, cmp_w1_v)]
    w2 = [np.asarray(a)[0].reshape(2, P, HD).transpose(1, 0, 2).reshape(P, -1) for a in (cmp_w2_k, cmp_w2_v)]
    wo = np.asarray(w_out)[0].reshape(16, HD, D)
    order = [h for j in range(PAIRS) for h in (j, j + 4)] + list(range(8, 16))
    wo = chunked(wo[order].reshape(D, D))
    wq = np.asarray(peer_wq)[0].reshape(KD, P, PH * 2, P).transpose(2, 1, 0, 3).reshape(PH * 2, P, KD * P)
    keys = np.asarray(peer_keys)[0].transpose(0, 3, 1, 2).reshape(PH, P, 2 * NK)
    uT = np.asarray(peer_u)[0].reshape(NK, P, KD, P).transpose(0, 3, 2, 1).reshape(NK, P, KD * P)
    v = np.asarray(peer_v)[0].reshape(NK, P, D)
    return {"x": c(np.asarray(x)[0]), "gains": c(np.concatenate(
        [np.asarray(g)[0].reshape(KD, P).T for g in (ln1_g, ln2_g)], 1)),
        "w_tiles": c(np.stack([chunked(a) for a in tiles])), "w_nat": c(chunked(nat)),
        "pe": c(np.concatenate(pe, 1)), "w1": c(np.concatenate(w1, 1)), "w2": c(np.concatenate(w2, 1)),
        "sinks": c(np.asarray(swa_sinks)[0]), "w_out": c(wo), "wq": c(wq), "keys": c(keys),
        "uT": c(uT), "v": c(v), "lnf": c(np.asarray(lnf_g))}


def kernel(**inputs):
    import concourse.bacc as _bacc
    from concourse.bass_utils import run_bass_kernel_spmd as _run

    nc = _bacc.Bacc("TRN2", target_bir_lowering=False, num_devices=1)
    arrays = {**layouts(**inputs), **constants()}
    w = {n: nc.dram_tensor(f"in_{n}", a.shape, mybir.dt.from_np(a.dtype), kind="ExternalInput").ap()
         for n, a in arrays.items()}
    out = nc.dram_tensor("out", (SEQ, D), F32, kind="ExternalOutput").ap()
    program(nc, w, out)
    r = _run(nc, [{f"in_{n}": a for n, a in arrays.items()}], core_ids=[0])
    return r.results[0]["out"].reshape(1, SEQ, D)
```

```python
from contextlib import ExitStack

import numpy as np

import concourse.bass as bass
from concourse import mybir
from concourse.alu_op_type import AluOpType as ALU

ACT = mybir.ActivationFunctionType
AX = mybir.AxisListType
F32 = mybir.dt.float32
F32R = mybir.dt.float32r
BF16 = mybir.dt.bfloat16
U32 = mybir.dt.uint32

P = 128
SEQ = 512
D = 1024
KD = D // P
TT = SEQ // P
HD = 64
NSA_HEADS = SWA_HEADS = 8
PAIRS = 4
CMP_LEN, CMP_STRIDE, CMP_HID = 32, 16, 256
NCMP = (SEQ - CMP_LEN) // CMP_STRIDE + 1
LP = CMP_LEN // 2
CC = 2 * NCMP + 1
SWA_WIN = 128
PH = 8
NK = 128
TOPK = 16
SEL = PH * TOPK
EPS = 1e-6
MASKED = 1e30
CLAMP = 1e20
KV_TILES = 5
V_S, V_W, V_SWA, GATES = 0, 128, 256, 320
NAT = 344
BG = 4
GROUPS = NK // BG
TC = 32
EARLY0 = PH + 4
EARLY = EARLY0 + SEQ // TC
HALF = D // 2


def load(eng, out, in_, sem):
    eng.dma_start(out, in_).then_inc(sem, 16)


def from_one(eng, sem, value):
    if not isinstance(value, int) or value > 0:
        eng.wait_ge(sem, value)


def hold(eng, passed):
    eng.sem_inc(passed, 1)


def prime(eng, sem, n):
    eng.sem_inc(sem, n)


class Mem:

    def __init__(self, nc, ctx):
        self.nc, self.ctx = nc, ctx

    def sb(self, name, shape, dt=F32):
        return self.ctx.enter_context(self.nc.sbuf_tensor(name, shape, dt))

    def ps(self, name, shape, dt=F32):
        return self.ctx.enter_context(self.nc.psum_tensor(name, shape, dt))

    def sem(self, *names):
        got = [self.ctx.enter_context(self.nc.semaphore(n)) for n in names]
        return got if len(got) > 1 else got[0]


def norm_transposed(nc, tag, src, src_ready, gain, gain_ready, ident, hi, lo, prefetch, sums=None):
    with ExitStack() as ctx:
        m = Mem(nc, ctx)
        sq = m.sb(tag + "sq", [P, D])
        ss = m.sb(tag + "ss", [P, TT]) if sums is None else sums
        ms = m.sb(tag + "ms", [P, TT])
        half = m.sb(tag + "half", [P, TT])
        rstd = m.sb(tag + "rstd", [P, TT])
        xn = m.sb(tag + "xn", [P, TT, D])
        psT = m.ps(tag + "psT", [P, 4, SEQ])
        squared, mean, rooted, scaled, turned, high, low = m.sem(
            *[tag + n for n in ("squared", "mean", "rooted", "scaled", "turned", "high", "low")])
        with nc.Block() as block:

            @block.sync
            def _(sp):
                prefetch(sp)

            @block.scalar
            def _(act):
                for t in range(TT if sums is None else 0):
                    for s, v in src_ready[t]:
                        act.wait_ge(s, v)
                    act.activation(sq[:, :], src[:, t, :], ACT.Square,
                                   accum_out=ss[:, t:t + 1]).then_inc(squared, 1)
                    act.wait_ge(squared, t + 1)
                for s, v in gain_ready:
                    act.wait_ge(s, v)
                for k in range(KD):
                    act.wait_ge(turned, k + 1)
                    act.activation(hi[:, k, :], psT[:, k % 4, :], ACT.Copy, scale=gain[:, k:k + 1]).then_inc(high, 1)

            @block.gpsimd
            def _(pool):
                pool.memset(half[:, :], -0.5).then_inc(mean, 1)
                if sums is None:
                    pool.wait_ge(squared, TT)
                pool.tensor_scalar(ms[:, :], ss[:, :], 1.0 / D, EPS, ALU.mult, ALU.add).then_inc(mean, 1)
                pool.wait_ge(mean, 2)
                pool.tensor_tensor(rstd[:, :], ms[:, :], half[:, :], ALU.pow).then_inc(rooted, 1)

            @block.vector
            def _(dve):
                for s, v in src_ready[TT - 1]:
                    dve.wait_ge(s, v)
                dve.wait_ge(rooted, 1)
                for t in range(TT):
                    dve.tensor_scalar(xn[:, t, :], src[:, t, :], rstd[:, t:t + 1], None,
                                      ALU.mult).then_inc(scaled, 1)
                for s, v in gain_ready:
                    dve.wait_ge(s, v)
                for k in range(KD):
                    dve.wait_ge(high, k + 1)
                    dve.scalar_tensor_tensor(out=lo[:, k, :], in0=psT[:, k % 4, :], scalar=gain[:, k:k + 1],
                                             in1=hi[:, k, :].bitcast(F32), op0=ALU.mult,
                                             op1=ALU.subtract).then_inc(low, 1)

            @block.tensor
            def _(pe):
                for s, v in gain_ready:
                    pe.wait_ge(s, v)
                for k in range(KD):
                    if k >= 4:
                        pe.wait_ge(low, k - 3)
                    for t in range(TT):
                        if k == 0:
                            pe.wait_ge(scaled, t + 1)
                        mm = pe.transpose(psT[:, k % 4, t * P:(t + 1) * P], xn[:, t, k * P:(k + 1) * P],
                                          ident[:, :])
                    mm.then_inc(turned, 1)


def pe_scores(pe, i, n, b):
    s = b.steps[n % b.N]
    b.wait_ready(pe, b.pe_ready, i, n)
    from_one(pe, b.shifted, i * b.N + (n - 1))
    pe.matmul(b.psS[:, n % 2, 0:s.width], s.q, s.k, start=True, stop=True).then_inc(b.scored, 1)


def pe_turn(pe, i, r, b):
    pe.wait_ge(b.expd, i * b.N + (r + 1))
    from_one(pe, b.copied[r % 2], i * (b.N // 2) + r // 2)
    for c in range(b.steps[r % b.N].width // P):
        mm = pe.transpose(b.psT[:, r % 2, c * P:(c + 1) * P], b.S[:, r % 4, c * P:(c + 1) * P], b.ident[:, :])
    mm.then_inc(b.turned, 1)


def pe_weigh(pe, i, r, b):
    s = b.steps[r]
    pe.wait_ge(b.copied[r % 2], i * (b.N // 2) + (r // 2 + 1))
    if r % 4 == 0:
        pe.wait_ge(b.taken, i * b.phases + (r // 4 + 1))
    for c in range(s.width // P):
        mm = pe.matmul(b.psO[:, (r // 4) % 2, (r % 4) * HD:(r % 4 + 1) * HD],
                       b.PT[:, r % 2, c * P:(c + 1) * P], s.v[c], start=(c == 0), stop=(c == s.width // P - 1))
    mm.then_inc(b.weighed, 1)


def act_exp(act, i, n, b):
    m, s = n % b.N, b.steps[n % b.N]
    act.wait_ge(b.shifted, i * b.N + (n + 1))
    act.activation(b.S[:, n % 4, 0:s.width], b.S[:, n % 4, 0:s.width], ACT.Exp,
                   bias=b.nmax[:, m:m + 1], scale=-1.0, accum_out=b.sums[:, m:m + 1]).then_inc(b.expd, 1)


def dve_shift(dve, i, n, b):
    m, s = n % b.N, b.steps[n % b.N]
    b.wait_ready(dve, b.dve_ready, i, n)
    dve.wait_ge(b.scored, i * b.N + (n + 1))
    from_one(dve, b.turned, i * b.N + (n - 3))
    hold(dve, b.passed)
    dve.tensor_tensor_reduce(b.S[:, n % 4, 0:s.width], s.bias, b.psS[:, n % 2, 0:s.width], 1.0,
                             s.start, ALU.add, ALU.min, b.nmax[:, m:m + 1]).then_inc(b.shifted, 1)


def copy_turned(eng, copy, i, r, b):
    width = b.steps[r % b.N].width
    eng.wait_ge(b.turned, i * b.N + (r + 1))
    from_one(eng, b.weighed, i * b.N + (r - 1))
    copy(b.PT[:, r % 2, 0:width], b.psT[:, r % 2, 0:width]).then_inc(b.copied[r % 2], 1)


class Step:
    def __init__(self, width, q, k, v, bias, start):
        self.width, self.q, self.k, self.v, self.bias, self.start = width, q, k, v, bias, start


class Bundle:

    def __init__(self, m, steps, phases, psS, psT, psO, ident):
        self.steps, self.N, self.phases = steps, len(steps), phases
        self.psS, self.psT, self.psO, self.ident = psS, psT, psO, ident
        self.S = m.sb("S", [P, 4, SEQ])
        self.PT = m.sb("PT", [P, 2, SEQ])
        self.nmax = m.sb("nmax", [P, self.N])
        self.sums = m.sb("sums", [P, self.N])
        self.scored, self.shifted, self.expd, self.turned, c0, c1, self.weighed, self.taken, self.passed = m.sem(
            "scored", "shifted", "expd", "turned", "copied0", "copied1", "weighed", "taken", "passed")
        self.copied = [c0, c1]
        self.pe_ready, self.dve_ready = {}, {}

    def wait_ready(self, eng, ready, i, n):
        if n % self.N in ready:
            sem, per_pair = ready[n % self.N]
            eng.wait_ge(sem, i * per_pair + per_pair * (n // self.N + 1))


class Tiles:

    def __init__(self, m, w_tiles):
        self.w_tiles = w_tiles
        self.raw = m.sb("wt", [P, 2, KD, P])
        self.hi = m.sb("wt_hi", [P, 2, KD, P], F32R)
        self.lo = m.sb("wt_lo", [P, 2, KD, P], F32R)
        self.landed = m.sem("wt_in0", "wt_in1")
        self.first = [*range(KV_TILES), KV_TILES, KV_TILES + PAIRS]

    def load(self, sp, n):
        load(sp, self.raw[:, n % 2], self.w_tiles[self.first[n]].rearrange("p (k c) -> p k c", k=KD),
             self.landed[n % 2])

    def prefetch(self, sp):
        for n in range(2):
            self.load(sp, n)


def attention(nc, m, a_hi, a_lo, ident, oT, w, tiles):
    qN = m.sb("qN", [P, SEQ])
    qS = m.sb("qS", [P, SEQ])
    wt, wt_hi, wt_lo = tiles.raw, tiles.hi, tiles.lo
    ksT = m.sb("ksT", [P, SEQ])
    kwT = m.sb("kwT", [P, SEQ])
    kdT = m.sb("kdT", [P, SEQ])
    nat = m.sb("nat", [P, TT, NAT])
    gsig = m.sb("gsig", [P, TT, 3, NSA_HEADS])
    kcT = m.sb("kcT", [P, NCMP])
    vcn = m.sb("vcn", [NCMP, 2, HD])
    Tbase = m.sb("Tbase", [P, SEQ])
    Tcmp = m.sb("Tcmp", [P, TT, NCMP])
    Tswa = m.sb("Tswa", [P, 2 * P])
    slopes = m.sb("slopes", [P, 2 * NSA_HEADS])
    sinks = m.sb("sinks", [P, SWA_HEADS])
    nsink = m.sb("nsink", [P, SWA_HEADS])
    tables, nsinked = m.sem("tables", "nsinked")

    with ExitStack() as ctx:
        k = Mem(nc, ctx)
        wn = k.sb("wn", [P, KD, NAT])
        wn_hi = k.sb("wn_hi", [P, KD, NAT], F32R)
        wn_lo = k.sb("wn_lo", [P, KD, NAT], F32R)
        X = k.sb("X", [P, 2, LP, CC])
        w1 = k.sb("w1", [P, 2, LP, CMP_HID])
        w2 = k.sb("w2", [P, 2, 2, HD])
        pe_sb = k.sb("pe_sb", [P, 2, LP])
        cb = k.sb("cb", [P, 4])
        hid = k.sb("hid", [P, 4, 2 * NCMP])
        ge = k.sb("ge", [P, TT, 3 * NSA_HEADS])
        psA = k.ps("psA", [P, 2, 512])
        psN = k.ps("psN", [P, 2, 512])
        psH = k.ps("psH", [P, 2, 512])
        psK = k.ps("psK", [P, 512])
        psV = k.ps("psV", [P, 512])
        wt_in = tiles.landed
        wn_in, w1_in, w2_in, pe_in = k.sem("wn_in", "w1_in", "w2_in", "pe_in")
        wt_high, wt_low, wn_high, wn_low = k.sem("wt_high", "wt_low", "wn_high", "wn_low")
        (projected, kept, keptx, pe_put, natured, nat_kept, gexp, gadd, gdone, hidden, bias_put, gelud,
         kc_made, kc_kept) = k.sem("projected", "kept", "keptx", "pe_put", "natured", "nat_kept", "gexp", "gadd",
                                   "gdone", "hidden", "bias_put", "gelud", "kc_made", "kc_kept")

        dsts = (None, None, ksT, kwT, kdT, qN, qS)
        NT = len(tiles.first)

        def act_tile(act, n, s, landed):
            act.wait_ge(wt_in[s], landed)
            from_one(act, projected, n - 1)
            act.copy(wt_hi[:, s], wt[:, s]).then_inc(wt_high, 1)

        def dve_tile(dve, n, s):
            dve.wait_ge(wt_high, n + 1)
            dve.tensor_tensor(wt_lo[:, s], wt[:, s], wt_hi[:, s].bitcast(F32), ALU.subtract).then_inc(wt_low, 1)

        def pe_tile(pe, n, s):
            pe.wait_ge(wt_low, n + 1)
            for c in range(KD):
                pe.matmul(psA[:, s, :], wt_hi[:, s, c, :], a_hi[:, c, :], start=(c == 0), stop=False)
                pe.matmul(psA[:, s, :], wt_hi[:, s, c, :], a_lo[:, c, :], start=False, stop=False)
                mm = pe.matmul(psA[:, s, :], wt_lo[:, s, c, :], a_hi[:, c, :], start=False, stop=(c == KD - 1))
            mm.then_inc(projected, 1)

        KEPT = 8
        with nc.Block() as block:

            @block.sync
            def _(sp):
                load(sp, pe_sb[:, :, :], w["pe"].rearrange("p (a l) -> p a l", a=2), pe_in)
                for n in range(2, NT):
                    sp.wait_ge(wt_low, n - 1)
                    tiles.load(sp, n)
                load(sp, w1[:, :, :, :], w["w1"].rearrange("p (a l c) -> p a l c", a=2, l=LP), w1_in)
                load(sp, wn[:, :, :], w["w_nat"].rearrange("p (k c) -> p k c", k=KD), wn_in)
                load(sp, w2[:, :, :, :], w["w2"].rearrange("p (a l c) -> p a l c", a=2, l=2), w2_in)
                load(sp, Tbase[:, :], w["t_nsa"], tables)
                load(sp, Tcmp[:, :, :], w["t_cmp"].rearrange("p (a c) -> p a c", a=TT), tables)
                load(sp, Tswa[:, :], w["t_swa"], tables)
                load(sp, slopes[:, :], w["slopes"], tables)
                load(sp, sinks[:, :], w["sinks"].partition_broadcast(P), tables)

            @block.tensor
            def _(pe):
                for n in range(NT):
                    if n >= 2:
                        pe.wait_ge(keptx if n == 3 else kept, KEPT + (n - 3 if n >= 4 else 0))
                    pe_tile(pe, n, n % 2)
                pe.wait_ge(keptx, 8)
                pe.wait_ge(kept, 8)
                pe.wait_ge(pe_put, 1)
                pe.wait_ge(w1_in, 16)
                for kv in range(2):
                    for hc in range(2):
                        for lp in range(LP):
                            mm = pe.matmul(psH[:, kv, hc * 64:hc * 64 + CC], w1[:, kv, lp, hc * P:(hc + 1) * P],
                                           X[:, kv, lp, :], start=(lp == 0), stop=(lp == LP - 1))
                        mm.then_inc(hidden, 1)
                pe.wait_ge(wn_low, 1)
                for t in range(TT):
                    if t >= 2:
                        pe.wait_ge(nat_kept, t - 1)
                    ts = slice(t * P, (t + 1) * P)
                    for c in range(KD):
                        pe.matmul(psN[:, t % 2, 0:NAT], a_hi[:, c, ts], wn_hi[:, c, :], start=(c == 0), stop=False)
                        pe.matmul(psN[:, t % 2, 0:NAT], a_hi[:, c, ts], wn_lo[:, c, :], start=False, stop=False)
                        mm = pe.matmul(psN[:, t % 2, 0:NAT], a_lo[:, c, ts], wn_hi[:, c, :], start=False,
                                       stop=(c == KD - 1))
                    mm.then_inc(natured, 1)
                pe.wait_ge(gelud, 4)
                pe.wait_ge(w2_in, 16)
                for g in range(2):
                    for hc in range(2):
                        mm = pe.matmul(psK[g * HD:(g + 1) * HD, 0:NCMP], w2[:, 0, hc, :],
                                       hid[:, hc, g * NCMP:(g + 1) * NCMP], start=(hc == 0), stop=(hc == 1))
                mm.then_inc(kc_made, 1)
                for g in range(2):
                    for hc in range(2):
                        mm = pe.matmul(psV[0:NCMP, g * HD:(g + 1) * HD],
                                       hid[:, 2 + hc, g * NCMP:(g + 1) * NCMP], w2[:, 1, hc, :],
                                       start=(hc == 0), stop=(hc == 1))
                mm.then_inc(kc_made, 1)

            def spread(copy, kv, par, done):
                for g in range(2):
                    for q in range(2):
                        raw = psA[g * HD:(g + 1) * HD, kv, :].rearrange("p (n l a) -> p a l n", a=2, l=LP // 2)
                        copy(X[par * HD:(par + 1) * HD, kv, q * 8:(q + 1) * 8, g * NCMP:(g + 1) * NCMP],
                             raw[:, par, :, q:q + NCMP]).then_inc(done, 1)

            @block.scalar
            def _(act):
                act_tile(act, 0, 0, 16)
                act_tile(act, 1, 1, 16)
                for n, dst in enumerate(dsts):
                    act.wait_ge(projected, n + 1)
                    if n == 0:
                        spread(act.copy, 0, 0, kept)
                        spread(act.copy, 0, 1, kept)
                    elif 2 <= n < KV_TILES:
                        act.copy(dst[:, :], psA[:, n % 2, :]).then_inc(kept, 1)
                    elif n >= KV_TILES:
                        act.activation(dst[:, :], psA[:, n % 2, :], ACT.Copy, scale=-(HD ** -0.5)).then_inc(kept, 1)
                    if n + 2 < NT:
                        act_tile(act, n + 2, n % 2, 16 * (n // 2 + 2))
                act.wait_ge(wn_in, 16)
                act.copy(wn_hi[:, :, :], wn[:, :, :]).then_inc(wn_high, 1)
                for j in range(4):
                    act.wait_ge(bias_put, 2 * (j // 2) + 2)
                    act.activation(hid[:, j, :], psH[:, j // 2, (j % 2) * 64:(j % 2) * 64 + 2 * NCMP],
                                   ACT.Gelu_apprx_tanh, bias=cb[:, j:j + 1]).then_inc(gelud, 1)
                act.wait_ge(nat_kept, TT)
                act.activation(ge[:, :, :], nat[:, :, GATES:NAT], ACT.Exp, scale=-1.0).then_inc(gexp, 1)

            @block.vector
            def _(dve):
                dve.wait_ge(pe_in, 16)
                dve.tensor_copy(X[:, :, :, CC - 1], pe_sb[:, :, :]).then_inc(pe_put, 1)
                for n in range(NT):
                    if n == 3:
                        dve.wait_ge(projected, 2)
                        spread(dve.tensor_copy, 1, 0, keptx)
                        spread(dve.tensor_copy, 1, 1, keptx)
                    dve_tile(dve, n, n % 2)
                dve.wait_ge(wn_high, 1)
                dve.tensor_tensor(wn_lo[:, :, :], wn[:, :, :], wn_hi[:, :, :].bitcast(F32),
                                  ALU.subtract).then_inc(wn_low, 1)
                for j in range(4):
                    dve.wait_ge(hidden, 2 * (j // 2) + 2)
                    dve.tensor_copy(cb[:, j:j + 1],
                                    psH[:, j // 2, (j % 2) * 64 + CC - 1:(j % 2) * 64 + CC]).then_inc(bias_put, 1)
                for t in range(TT):
                    dve.wait_ge(natured, t + 1)
                    dve.tensor_copy(nat[:, t, :], psN[:, t % 2, 0:NAT]).then_inc(nat_kept, 1)
                dve.wait_ge(gexp, 1)
                dve.tensor_scalar(ge[:, :, :], ge[:, :, :], 1.0, None, ALU.add).then_inc(gadd, 1)
                dve.wait_ge(gadd, 1)
                dve.reciprocal(gsig[:, :, :, :], ge[:, :, :].rearrange("p t (c h) -> p t c h", c=3)).then_inc(gdone, 1)
                dve.wait_ge(kc_made, 1)
                dve.tensor_copy(kcT[:, :], psK[:, 0:NCMP]).then_inc(kc_kept, 1)
                dve.wait_ge(kc_made, 2)
                dve.tensor_copy(vcn[:, :, :], psV[0:NCMP, 0:P].rearrange("p (g d) -> p g d", g=2)).then_inc(kc_kept, 1)
                dve.wait_ge(tables, 80)
                dve.tensor_scalar(nsink[:, :], sinks[:, :], -1.0, None, ALU.mult).then_inc(nsinked, 1)

    wo = m.sb("wo", [P, KD, D])
    wo_in = m.sem("wo_in")
    with ExitStack() as ctx:
        k = Mem(nc, ctx)
        Th = k.sb("Th", [P, 2, SEQ])
        sTh = k.sb("sTh", [P, 2, 2 * P])
        Tc = k.sb("Tc", [P, 2, TT, NCMP])
        ns = k.sb("ns", [P, 2])
        gp = k.sb("gp", [P, 3, 2, TT])
        fac = k.sb("fac", [P, 6, TT])
        sfac = k.sb("sfac", [P, 2, TT])
        es = k.sb("es", [P, 2, TT])
        Sc = k.sb("Sc", [P, 2, TT, NCMP])
        cmin = k.sb("cmin", [P, 2 * TT])
        csum = k.sb("csum", [P, 2 * TT])
        PTc = k.sb("PTc", [NCMP, 2, TT, P])
        part = k.sb("part", [P, TT, HD])
        op = k.sb("op", [P, TT, 2, HD])
        sop = k.sb("sop", [P, TT, 2, HD])
        psS = k.ps("psS", [P, 2, 512])
        psT = k.ps("psT", [P, 2, 512])
        psO = k.ps("psO", [P, 2, 512])
        psC = k.ps("psC", [P, 512])
        psQ = k.ps("psQ", [P, 512])
        q_in = k.sem("qw_in0", "qw_in1")
        q_high, q_low, q_made, qn_kept, qs_kept = k.sem("qw_high", "qw_low", "q_made", "qn_kept", "qs_kept")
        (nsa_ready, swa_ready, gated, c_scored, c_chain, c_sum, c_exp, c_turned, c_copied, c_weighed, c_taken, facs,
         o_added, o_turned, o_kept, s_chain, s_exp, so_turned, so_kept, pool_passed) = k.sem(
            "nsa_ready", "swa_ready", "gated", "c_scored", "c_chain", "c_sum", "c_exp", "c_turned", "c_copied",
            "c_weighed", "c_taken", "facs", "o_added", "o_turned", "o_kept", "s_chain", "s_exp", "so_turned",
            "so_kept", "p_passed")
        steps = []
        for hh in range(2):
            r = slice(hh * HD, (hh + 1) * HD)
            for kT, voff in ((ksT, V_S), (kwT, V_W)):
                for t in range(TT):
                    width = (t + 1) * P
                    steps.append(Step(width, qN[r, t * P:(t + 1) * P], kT[r, 0:width],
                                      [nat[:, c, voff + hh * HD:voff + (hh + 1) * HD] for c in range(t + 1)],
                                      Th[:, hh, SEQ - width:SEQ], CLAMP))
        NSA = len(steps)
        for hh in range(2):
            r = slice(hh * HD, (hh + 1) * HD)
            for t in range(TT):
                k0 = max(t - 1, 0)
                width = (t + 1 - k0) * P
                steps.append(Step(width, qS[r, t * P:(t + 1) * P], kdT[r, k0 * P:k0 * P + width],
                                  [nat[:, c, V_SWA:V_SWA + HD] for c in range(k0, t + 1)],
                                  sTh[:, hh, 2 * P - width:2 * P], ns[:, hh:hh + 1]))
        b = Bundle(k, steps, 6, psS, psT, psO, ident)
        N = b.N
        b.pe_ready = {0: (qn_kept, 1), NSA: (qs_kept, 1)}
        b.dve_ready = {0: (nsa_ready, 4), NSA: (swa_ready, 3)}
        LEAD = 3

        def turns(eng, turn):
            with eng.Fori(0, PAIRS - 1) as i:
                turn(eng, i, False)
            turn(eng, PAIRS - 1, True)

        def pe_compressed_scores(pe, i):
            pe.wait_ge(so_kept, i + 1)
            pe.wait_ge(qs_kept, i + 1)
            for hh, ps in enumerate((psC, psQ)):
                r = slice(hh * HD, (hh + 1) * HD)
                for t in range(TT):
                    mm = pe.matmul(ps[:, t * NCMP:(t + 1) * NCMP], qN[r, t * P:(t + 1) * P], kcT[r, :],
                                   start=True, stop=True)
                mm.then_inc(c_scored, 1)

        def pe_compressed_turn(pe, i, hh):
            if hh == 0:
                pe.wait_ge(c_exp, i + 1)
            else:
                pe.wait_ge(c_copied, i * 2 + 1)
            for t in range(TT):
                mm = pe.transpose(psC[0:NCMP, t * P:(t + 1) * P], Sc[:, hh, t, :], ident[:, :])
            mm.then_inc(c_turned, 1)

        def pe_compressed_weigh(pe, i):
            pe.wait_ge(c_copied, i * 2 + 2)
            for hh in range(2):
                for t in range(TT):
                    x = hh * TT + t
                    mm = pe.matmul(psC[:, x * HD:(x + 1) * HD], PTc[:, hh, t, :], vcn[:, hh, :],
                                   start=True, stop=True)
            mm.then_inc(c_weighed, 1)

        SPREAD = {n: (0, 24 * (n - 6) // 11, 24 * (n - 5) // 11) for n in range(6, 17)}
        SPREAD.update({n: (1, 24 * (n - 18) // 9, 24 * (n - 17) // 9) for n in range(18, 27)})

        def pe_queries(pe, i, s, first, end):
            if first == 0:
                pe.wait_ge(q_low, i * 2 + (s + 3))
                if s == 0:
                    pe.wait_ge(c_chain, i * 4 + 2)
                else:
                    pe.wait_ge(qn_kept, i + 2)
            for x in range(first, end):
                c, j = x // 3, x % 3
                u, a = ((wt_hi, a_hi), (wt_hi, a_lo), (wt_lo, a_hi))[j]
                mm = pe.matmul(psQ[:, :], u[:, s, c, :], a[:, c, :], start=(x == 0), stop=(x == 3 * KD - 1))
            if end == 3 * KD:
                mm.then_inc(q_made, 1)

        def pe_out_nsa(pe, i):
            pe.wait_ge(o_added, i * 4 + 5)
            for t in range(TT):
                mm = pe.transpose(psC[:, t * P:(t + 1) * P], op[:, t, :, :], ident[:, :])
            mm.then_inc(o_turned, 1)

        def pe_out_swa(pe, i):
            pe.wait_ge(b.taken, i * 6 + 8)
            pe.wait_ge(o_kept, i + 1)
            for t in range(TT):
                mm = pe.transpose(psC[:, t * P:(t + 1) * P], sop[:, t, :, :], ident[:, :])
            mm.then_inc(so_turned, 1)

        def pe_pair(pe, i, last):
            extra = {4: pe_compressed_scores, 8: lambda *a: pe_compressed_turn(*a, 0),
                     10: lambda *a: pe_compressed_turn(*a, 1), 13: pe_compressed_weigh, 22: pe_out_nsa}
            for n in range(LEAD, N + LEAD):
                if n < N or not last:
                    pe_scores(pe, i, n, b)
                if n in extra:
                    extra[n](pe, i)
                if n in SPREAD and not last:
                    pe_queries(pe, i, *SPREAD[n])
                if n - 2 < N or not last:
                    pe_turn(pe, i, n - 2, b)
                pe_weigh(pe, i, n - LEAD, b)
            pe_out_swa(pe, i)

        def act_pair(act, i, last):
            for n in range(LEAD, N + LEAD):
                if n < N or not last:
                    act_exp(act, i, n, b)
                if n == 6:
                    act.wait_ge(c_chain, i * 4 + 4)
                    act.activation(Sc[:, :, :, :], Sc[:, :, :, :], ACT.Exp, scale=-1.0).then_inc(c_exp, 1)
                if n in (9, 11):
                    hh = (n - 9) // 2
                    act.wait_ge(c_turned, i * 2 + (hh + 1))
                    act.copy(PTc[:, hh, :, :], psC[0:NCMP, :].rearrange("p (t q) -> p t q", t=TT)
                             ).then_inc(c_copied, 1)
                if n in (3, 12) and not last:
                    s = n // 12
                    act.wait_ge(q_in[s], i * 16 + 16)
                    act.wait_ge(q_made, i * 2 + (s + 1))
                    act.copy(wt_hi[:, s], wt[:, s]).then_inc(q_high, 1)
                if n == 17 and not last:
                    act.wait_ge(q_made, i * 2 + 3)
                    act.activation(qN[:, :], psQ[:, :], ACT.Copy, scale=-(HD ** -0.5)).then_inc(qn_kept, 1)
                if n == 23:
                    act.wait_ge(o_turned, i + 1)
                    act.copy(oT[:, bass.ds(i, 1), :].rearrange("p a t -> p (a t)"), psC[:, :]).then_inc(o_kept, 1)
                if n == 25:
                    act.wait_ge(s_chain, i * 5 + 1)
                    act.activation(es[:, :, :], es[:, :, :], ACT.Exp).then_inc(s_exp, 1)
                if n % 2 == 0 and (n - 2 < N or not last):
                    copy_turned(act, act.copy, i, n - 2, b)
            if not last:
                act.wait_ge(q_made, i * 2 + 4)
                act.activation(qS[:, :], psQ[:, :], ACT.Copy, scale=-(HD ** -0.5)).then_inc(qs_kept, 1)
            act.wait_ge(so_turned, i + 1)
            act.copy(oT[:, bass.ds(i + PAIRS, 1), :].rearrange("p a t -> p (a t)"), psC[:, :]).then_inc(so_kept, 1)

        def dve_gates(dve, i):
            for hh in range(2):
                dve.tensor_copy(gp[:, :, hh, :], gsig[:, :, :, bass.ds(i + 4 * hh, 1)].rearrange(
                    "p t c a -> p c (t a)")).then_inc(gated, 1)

        def dve_compressed(dve, i):
            for hh, ps in enumerate((psC, psQ)):
                dve.wait_ge(c_scored, i * 2 + (hh + 1))
                dve.tensor_tensor(Sc[:, hh, :, :], Tc[:, hh, :, :],
                                  ps[:, 0:TT * NCMP].rearrange("p (t n) -> p t n", t=TT),
                                  ALU.add).then_inc(c_chain, 1)
            dve.wait_ge(c_chain, i * 4 + 2)
            flat = Sc[:, :, :, :].rearrange("p h t n -> p (h t) n")
            dve.tensor_reduce(cmin[:, :], flat, AX.X, ALU.min).then_inc(c_sum, 1)
            dve.wait_ge(c_sum, i * 2 + 1)
            dve.tensor_scalar(cmin[:, :], cmin[:, :], CLAMP, None, ALU.min).then_inc(c_chain, 1)
            dve.wait_ge(c_chain, i * 4 + 3)
            dve.tensor_tensor(flat, flat, cmin[:, :].unsqueeze(2).to_broadcast([P, 2 * TT, NCMP]),
                              ALU.subtract).then_inc(c_chain, 1)

        def dve_compressed_sums(dve, i):
            dve.wait_ge(c_exp, i + 1)
            dve.tensor_reduce(csum[:, :], Sc[:, :, :, :].rearrange("p h t n -> p (h t) n"), AX.X,
                              ALU.add).then_inc(c_sum, 1)

        def factor(dve, i, use, c, hh, sums):
            f = fac[:, use, :]
            dve.tensor_scalar(f, sums, 1e-30, None, ALU.max).then_inc(facs, 1)
            dve.wait_ge(facs, i * 18 + (3 * use + 1))
            dve.reciprocal(f, f).then_inc(facs, 1)
            dve.wait_ge(facs, i * 18 + (3 * use + 2))
            dve.tensor_tensor(f, f, gp[:, c, hh, :], ALU.mult).then_inc(facs, 1)
            dve.wait_ge(facs, i * 18 + (3 * use + 3))
            return f.unsqueeze(2).to_broadcast([P, TT, HD])

        def dve_take(dve, i, phase):
            hh, c = phase // 2, (1, 2)[phase % 2]
            if phase == 0:
                dve.wait_ge(gated, i * 2 + 2)
            f = factor(dve, i, phase, c, hh, b.sums[:, 4 * phase:4 * phase + 4])
            dve.wait_ge(b.weighed, i * N + (4 * phase + 4))
            o = psO[:, phase % 2, 0:TT * HD].rearrange("p (t d) -> p t d", t=TT)
            if c == 1:
                dve.tensor_tensor(op[:, :, hh, :], f, o, ALU.mult).then_inc(b.taken, 1)
                return
            dve.wait_ge(o_added, i * 4 + (hh + 1))
            dve.tensor_tensor(part[:, :, :], f, o, ALU.mult).then_inc(b.taken, 1)
            dve.wait_ge(b.taken, i * 6 + (phase + 3))
            dve.tensor_tensor(op[:, :, hh, :], op[:, :, hh, :], part[:, :, :], ALU.add).then_inc(o_added, 1)

        def dve_take_compressed(dve, i, hh):
            if hh == 0:
                dve.wait_ge(c_sum, i * 2 + 2)
            f = factor(dve, i, 4 + hh, 0, hh, csum[:, hh * TT:(hh + 1) * TT])
            dve.wait_ge(c_weighed, i + 1)
            dve.wait_ge(o_added, i * 4 + (hh + 3))
            dve.tensor_tensor(part[:, :, :], f, psC[:, hh * TT * HD:(hh + 1) * TT * HD].rearrange("p (t d) -> p t d", t=TT),
                              ALU.mult).then_inc(c_taken, 1)
            dve.wait_ge(c_taken, i * 2 + (hh + 1))
            dve.tensor_tensor(op[:, :, hh, :], op[:, :, hh, :], part[:, :, :], ALU.add).then_inc(o_added, 1)

        def dve_sinks(dve, i):
            dve.wait_ge(b.shifted, i * N + N)
            dve.tensor_tensor(es[:, :, :], b.nmax[:, NSA:N].rearrange("p (h t) -> p h t", h=2),
                              ns[:, :].unsqueeze(2).to_broadcast([P, 2, TT]), ALU.subtract).then_inc(s_chain, 1)

        def dve_window_factors(dve, i):
            dve.wait_ge(s_exp, i + 1)
            dve.wait_ge(b.expd, i * N + N)
            dve.tensor_tensor(sfac[:, :, :], es[:, :, :], b.sums[:, NSA:N].rearrange("p (h t) -> p h t", h=2),
                              ALU.add).then_inc(s_chain, 1)
            dve.wait_ge(s_chain, i * 5 + 2)
            dve.reciprocal(sfac[:, :, :], sfac[:, :, :]).then_inc(s_chain, 3)

        def dve_take_windows(dve, i):
            dve.wait_ge(s_chain, i * 5 + 5)
            for hh in range(2):
                dve.wait_ge(b.weighed, i * N + (NSA + 4 * hh + 4))
                dve.tensor_tensor(sop[:, :, hh, :], sfac[:, hh, :].unsqueeze(2).to_broadcast([P, TT, HD]),
                                  psO[:, hh, 0:TT * HD].rearrange("p (t d) -> p t d", t=TT),
                                  ALU.mult).then_inc(b.taken, 1)

        def dve_pair(dve, i, last):
            for n in range(LEAD, N + LEAD):
                if n < N or not last:
                    dve_shift(dve, i, n, b)
                if n % 2 == 1:
                    copy_turned(dve, dve.tensor_copy, i, n - 2, b)
                if n == 4:
                    dve_gates(dve, i)
                if n == 5:
                    dve_compressed(dve, i)
                if n == 10:
                    dve_compressed_sums(dve, i)
                if n in (7, 11, 15, 19):
                    dve_take(dve, i, (n - 7) // 4)
                if n == 20:
                    for hh in range(2):
                        dve_take_compressed(dve, i, hh)
                if n == 24:
                    dve_sinks(dve, i)
                if n == 26:
                    dve_window_factors(dve, i)
            dve_take_windows(dve, i)

        def pool_nsa(pool, i):
            for hh in range(2):
                s = slopes[:, bass.ds(i + (8 + 4 * hh), 1)]
                pool.tensor_tensor(Th[:, hh, :], Tbase[:, :], s.to_broadcast([P, SEQ]), ALU.mult).then_inc(nsa_ready, 1)
                pool.tensor_tensor(Tc[:, hh, :, :], Tcmp[:, :, :], s.unsqueeze(2).to_broadcast([P, TT, NCMP]),
                                   ALU.mult).then_inc(nsa_ready, 1)

        def pool_swa(pool, i):
            for hh in range(2):
                s = slopes[:, bass.ds(i * 2 + hh, 1)]
                pool.tensor_tensor(sTh[:, hh, :], Tswa[:, :], s.to_broadcast([P, 2 * P]),
                                   ALU.mult).then_inc(swa_ready, 1)
            pool.tensor_copy(ns[:, :], nsink[:, bass.ds(i * 2, 2)]).then_inc(swa_ready, 1)

        with nc.Block() as block:

            @block.sync
            def _(sp):
                with sp.Fori(0, PAIRS - 1) as i:
                    for s in range(2):
                        sp.wait_ge(q_low, i * 2 + (s + 1))
                        load(sp, wt[:, s], w["w_tiles"][bass.ds(i + (KV_TILES + PAIRS * s + 1), 1)].rearrange(
                            "a p (k c) -> p (a k) c", k=KD), q_in[s])
                load(sp, wo[:, :, :], w["w_out"].rearrange("p (k n) -> p k n", n=D), wo_in)

            @block.tensor
            def _(pe):
                prime(pe, q_made, 2)
                prime(pe, b.taken, 2)
                for n in range(LEAD):
                    pe_scores(pe, 0, n, b)
                pe_turn(pe, 0, 0, b)
                turns(pe, pe_pair)

            @block.scalar
            def _(act):
                prime(act, o_kept, 1)
                prime(act, so_kept, 1)
                prime(act, qn_kept, 1)
                prime(act, qs_kept, 1)
                for n in range(LEAD):
                    act_exp(act, 0, n, b)
                copy_turned(act, act.copy, 0, 0, b)
                turns(act, act_pair)

            @block.vector
            def _(dve):
                prime(dve, o_added, 1)
                for n in range(LEAD):
                    dve_shift(dve, 0, n, b)
                turns(dve, dve_pair)

            @block.gpsimd
            def _(pool):
                pool_nsa(pool, 0)
                pool_swa(pool, 0)
                prime(pool, q_low, 2)
                with pool.Fori(0, PAIRS - 1) as i:
                    for s in range(2):
                        pool.wait_ge(q_high, i * 2 + (s + 1))
                        pool.tensor_tensor(wt_lo[:, s], wt[:, s], wt_hi[:, s].bitcast(F32),
                                           ALU.subtract).then_inc(q_low, 1)
                    pool.wait_ge(b.shifted, i * N + NSA)
                    hold(pool, pool_passed)
                    pool_nsa(pool, i + 1)
                    pool.wait_ge(b.shifted, i * N + N)
                    pool.wait_ge(s_chain, i * 5 + 1)
                    hold(pool, pool_passed)
                    pool_swa(pool, i + 1)
    return wo, wo_in


def project_out(nc, oT, acc, wo, wo_in, sums):
    with ExitStack() as ctx:
        m = Mem(nc, ctx)
        o_hi = m.sb("o_hi", [P, 2, SEQ], F32R)
        o_lo = m.sb("o_lo", [P, 2, SEQ], F32R)
        wo_hi = m.sb("wo_hi", [P, 2, D], F32R)
        wo_lo = m.sb("wo_lo", [P, 2, D], F32R)
        ps = m.ps("psW", [P, 2 * TT, HALF])
        high, low, made = m.sem("wo_high", "wo_low", "wo_made")
        added, summed, squared = m.sem("wo_added", "wo_summed", "wo_squared")
        sq = m.sb("wo_sq", [P, D])
        with nc.Block() as block:

            @block.scalar
            def _(act):
                for c in range(KD):
                    if c >= 2:
                        act.wait_ge(summed, c - 1)
                    act.copy(o_hi[:, c % 2, :], oT[:, c, :]).then_inc(high, 1)
                    if c == 0:
                        act.wait_ge(wo_in, 16)
                    act.copy(wo_hi[:, c % 2, :], wo[:, c, :]).then_inc(high, 1)
                for t in range(TT):
                    act.wait_ge(added, 2 * t + 2)
                    act.activation(sq[:, :], acc[:, t, :], ACT.Square, accum_out=sums[:, t:t + 1]).then_inc(squared, 1)
                    act.wait_ge(squared, t + 1)

            @block.vector
            def _(dve):
                for c in range(KD):
                    dve.wait_ge(high, 2 * c + 1)
                    dve.tensor_tensor(o_lo[:, c % 2, :], oT[:, c, :], o_hi[:, c % 2, :].bitcast(F32),
                                      ALU.subtract).then_inc(low, 1)
                    dve.wait_ge(high, 2 * c + 2)
                    dve.tensor_tensor(wo_lo[:, c % 2, :], wo[:, c, :], wo_hi[:, c % 2, :].bitcast(F32),
                                      ALU.subtract).then_inc(low, 1)
                for n in range(2 * TT):
                    t, h = n // 2, n % 2
                    dve.wait_ge(made, n + 1)
                    a = acc[:, t, h * HALF:(h + 1) * HALF]
                    dve.tensor_tensor(a, a, ps[:, n, :], ALU.add).then_inc(added, 1)

            @block.tensor
            def _(pe):
                for c in range(KD):
                    pe.wait_ge(low, 2 * c + 2)
                    for n in range(2 * TT):
                        ts, hs = slice(n // 2 * P, (n // 2 + 1) * P), slice(n % 2 * HALF, (n % 2 + 1) * HALF)
                        pe.matmul(ps[:, n, :], o_hi[:, c % 2, ts], wo_hi[:, c % 2, hs], start=(c == 0), stop=False)
                        pe.matmul(ps[:, n, :], o_hi[:, c % 2, ts], wo_lo[:, c % 2, hs], start=False, stop=False)
                        mm = pe.matmul(ps[:, n, :], o_lo[:, c % 2, ts], wo_hi[:, c % 2, hs], start=False,
                                       stop=(c == KD - 1))
                        if c == KD - 1:
                            mm.then_inc(made, 1)
                    if c < KD - 1:
                        mm.then_inc(summed, 1)


class Activations:

    AHEAD = 4

    def __init__(self, m, h_hi, h_lo, uT):
        self.h_hi, self.h_lo, self.uT = h_hi, h_lo, uT
        self.raw = m.sb("u_raw", [P, 2, KD, P])
        self.hi = m.sb("u_hi", [P, 2, KD, P], F32R)
        self.lo = m.sb("u_lo", [P, 2, KD, P], F32R)
        self.ps = m.ps("psA2", [P, 2, 512])
        self.landed = m.sem("u_in0", "u_in1")
        self.high, self.low, self.made, self.gelued = m.sem("u_high", "u_low", "a_made", "gelued")

    def prime(self, sp, pe, act, pool):
        for eng, sems in ((pe, [self.made]), (act, [self.high, self.gelued]), (pool, [self.low])):
            if eng is not None:
                for sem in sems:
                    prime(eng, sem, self.AHEAD)

    def load(self, sp, b, s):
        sp.wait_ge(self.low, b + (self.AHEAD - 1))
        load(sp, self.raw[:, s, :, :], self.uT[bass.ds(b, 1)].rearrange("a p (k e) -> p (a k) e", k=KD),
             self.landed[s])

    def load_first(self, sp, s):
        load(sp, self.raw[:, s, :, :], self.uT[s].rearrange("p (k e) -> p k e", k=KD), self.landed[s])

    def split_high(self, act, b, s, landed):
        act.wait_ge(self.landed[s], landed)
        act.wait_ge(self.made, b + (self.AHEAD - 1))
        act.copy(self.hi[:, s, :, :], self.raw[:, s, :, :]).then_inc(self.high, 1)

    def split_low(self, eng, b, s):
        eng.wait_ge(self.high, b + (self.AHEAD + 1))
        eng.tensor_tensor(self.lo[:, s, :, :], self.raw[:, s, :, :], self.hi[:, s, :, :].bitcast(F32),
                          ALU.subtract).then_inc(self.low, 1)

    def product(self, pe, b, s, first=0, end=KD):
        if first == 0:
            pe.wait_ge(self.low, b + (self.AHEAD + 1))
            pe.wait_ge(self.gelued, b + (self.AHEAD - 1))
        for c in range(first, end):
            pe.matmul(self.ps[:, s, :], self.hi[:, s, c, :], self.h_hi[:, c, :], start=(c == 0), stop=False)
            pe.matmul(self.ps[:, s, :], self.hi[:, s, c, :], self.h_lo[:, c, :], start=False, stop=False)
            mm = pe.matmul(self.ps[:, s, :], self.lo[:, s, c, :], self.h_hi[:, c, :], start=False,
                           stop=(c == KD - 1))
        if end == KD:
            mm.then_inc(self.made, 1)

    def gelu(self, act, b, s, out, passed=None):
        act.wait_ge(self.made, b + (self.AHEAD + 1))
        if passed is not None:
            hold(act, passed)
        act.activation(out, self.ps[:, s, :], ACT.Gelu_apprx_tanh).then_inc(self.gelued, 1)


def block_of(early, b):
    return early[:, bass.ds(b, 1), :].rearrange("p a t -> p (a t)")


class Queries:

    def __init__(self, m, w):
        self.w = w
        self.wq = m.sb("wq", [P, 2, KD, P])
        self.keys = m.sb("keys", [P, 2, NK])
        self.wq_in = m.sem("wq_in0", "wq_in1")
        self.keys_in = m.sem("keys_in")

    def load_weights(self, sp, h, c):
        load(sp, self.wq[:, c], self.w["wq"][bass.ds(h * 2 + c, 1)].rearrange("a p (k c) -> p (a k) c", k=KD),
             self.wq_in[c])

    def load_keys(self, sp, h):
        load(sp, self.keys[:, :, :], self.w["keys"][bass.ds(h, 1)].rearrange("a p (c n) -> p (a c) n", c=2),
             self.keys_in)

    def prefetch(self, sp):
        for c in range(2):
            self.load_weights(sp, 0, c)
        self.load_keys(sp, 0)


def choose_experts(nc, iota, sel_w, sel_e, w, blocks, early, queries):
    with ExitStack() as ctx:
        m = Mem(nc, ctx)
        wq, keys, wq_in, keys_in = queries.wq, queries.keys, queries.wq_in, queries.keys_in
        wq_hi = m.sb("wq_hi", [P, 2, KD, P], F32R)
        wq_lo = m.sb("wq_lo", [P, 2, KD, P], F32R)
        qp = m.sb("qp", [P, 2, SEQ])
        sc = m.sb("sc", [P, 2, TT, NK])
        rest = m.sb("rest", [P, 2, TT, NK])
        top = m.sb("top", [P, 2, TT, TOPK])
        at = m.sb("at", [P, 2, TT, TOPK], U32)
        atf = m.sb("atf", [P, 2, TT, TOPK])
        cand = m.sb("cand", [P, TT, TOPK * TOPK])
        crest = m.sb("crest", [P, TT, TOPK * TOPK])
        best = m.sb("best", [P, TT, TOPK])
        cat = m.sb("cat", [P, TT, TOPK], U32)
        ab = m.sb("ab", [P, 2, TT, TOPK], U32)
        abf = m.sb("abf", [P, 2, TT, TOPK])
        eq = m.sb("eq", [P, 2 * TT, TOPK, TOPK])
        gsum = m.sb("gsum", [P, TT * PH])
        psQ = m.ps("psQ2", [P, 2, 512])
        psS = m.ps("psS2", [P, 2, TT, NK])
        wq_high, wq_low = m.sem("wq_high", "wq_low")
        passed, a_passed, pool_passed = m.sem("e_passed", "ea_passed", "ep_passed")
        (q_made, q_kept, s_made, s_kept, max1, cut1, max2, at2, cands, cmax1, ccut1, cmax2, cat2, split,
         eqd, mulled, picked, g1) = m.sem(
            "pq_made", "pq_kept", "ps_made", "ps_kept", "max1", "cut1", "max2", "at2", "cands", "cmax1",
            "ccut1", "cmax2", "cat2", "split", "eqd", "mulled", "picked", "g1")

        key_numbers = atf[:, :, :, :].rearrange("p c t j -> p (c t) j").unsqueeze(2).to_broadcast(
            [P, 2 * TT, TOPK, TOPK])

        def sp_head(sp, h, par):
            for c in range(2):
                sp.wait_ge(wq_low, h * 2 + (c + 3))
                queries.load_weights(sp, h + 1, c)
            blocks.load(sp, h + 2, par)
            sp.wait_ge(s_made, h * 2 + 4)
            queries.load_keys(sp, h + 1)

        with nc.Block() as block:

            @block.sync
            def _(sp):
                with sp.Fori(0, PH // 2 - 1) as i:
                    for par in range(2):
                        sp_head(sp, i * 2 + par, par)
                sp_head(sp, PH - 2, 0)
                blocks.load(sp, PH + 1, 1)
                for b in range(PH, EARLY0):
                    blocks.load(sp, b + 2, b % 2)

            @block.tensor
            def _(pe):
                blocks.prime(None, pe, None, None)
                prime(pe, q_made, 2)
                prime(pe, s_made, 2)
                with pe.Fori(0, PH // 2) as i:
                    for par in range(2):
                        h = i * 2 + par
                        for c in range(2):
                            pe.wait_ge(wq_low, h * 2 + (c + 3))
                            for k in range(KD):
                                pe.matmul(psQ[:, c, :], wq_hi[:, c, k, :], blocks.h_hi[:, k, :], start=(k == 0),
                                          stop=False)
                                pe.matmul(psQ[:, c, :], wq_hi[:, c, k, :], blocks.h_lo[:, k, :], start=False,
                                          stop=False)
                                mm = pe.matmul(psQ[:, c, :], wq_lo[:, c, k, :], blocks.h_hi[:, k, :], start=False,
                                               stop=(k == KD - 1))
                            mm.then_inc(q_made, 1)
                        blocks.product(pe, h, par)
                        pe.wait_ge(keys_in, h * 16 + 16)
                        for c in range(2):
                            pe.wait_ge(q_kept, h * 2 + c + 1)
                            pe.wait_ge(s_kept, h * 2 + 2)
                            for t in range(TT):
                                mm = pe.matmul(psS[:, c, t, :], qp[:, c, t * P:(t + 1) * P], keys[:, c, :],
                                               start=True, stop=True)
                            mm.then_inc(s_made, 1)
                for b in range(PH, EARLY0):
                    blocks.product(pe, b, b % 2)

            def act_head(act, h, i, par, split_next=True):
                for c in range(2):
                    act.wait_ge(s_made, h * 2 + 2)
                    act.wait_ge(q_made, h * 2 + (c + 3))
                    act.copy(qp[:, c, :], psQ[:, c, :]).then_inc(q_kept, 1)
                if split_next:
                    for c in range(2):
                        act.wait_ge(wq_in[c], h * 16 + 32)
                        act.copy(wq_hi[:, c, :, :], wq[:, c, :, :]).then_inc(wq_high, 1)
                blocks.gelu(act, h, par, block_of(early, h), a_passed)
                blocks.split_high(act, h + 2, par, i * 16 + 32)
                act.wait_ge(cut1, h * 16 + 16)
                for c in range(2):
                    act.wait_ge(s_made, h * 2 + (c + 3))
                    act.copy(sc[:, c, :, :], psS[:, c, :, :]).then_inc(s_kept, 1)

            @block.scalar
            def _(act):
                blocks.prime(None, None, act, None)
                prime(act, s_kept, 2)
                for c in range(2):
                    act.wait_ge(wq_in[c], 16)
                    act.copy(wq_hi[:, c, :, :], wq[:, c, :, :]).then_inc(wq_high, 1)
                for s in range(2):
                    blocks.split_high(act, s, s, 16)
                with act.Fori(0, PH // 2 - 1) as i:
                    for par in range(2):
                        act_head(act, i * 2 + par, i, par)
                act_head(act, PH - 2, PH // 2 - 1, 0)
                act_head(act, PH - 1, PH // 2 - 1, 1, split_next=False)
                for b in range(PH, EARLY0):
                    blocks.gelu(act, b, b % 2, early[:, b, :])
                    blocks.split_high(act, b + 2, b % 2, 16 * ((b + 2) // 2 + 1))

                act.wait_ge(g1, 1)
                act.activation(sel_w[:, :, :], sel_w[:, :, :], ACT.Exp).then_inc(g1, 1)

            def pool_head(pool, h, par):
                blocks.split_low(pool, h + 2, par)
                pool.wait_ge(picked, h * 3 + 3)
                pool.wait_ge(split, h * 4 + 4)
                hold(pool, pool_passed)
                for j in range(TOPK):
                    pool.tensor_scalar(eq[:, :, :, j], abf[:, :, :, :].rearrange("p c t s -> p (c t) s"), float(j),
                                       None, ALU.is_equal).then_inc(eqd, 1)
                pool.wait_ge(eqd, h * TOPK + TOPK)
                pool.tensor_tensor(eq[:, :, :, :], eq[:, :, :, :], key_numbers, ALU.mult).then_inc(mulled, 1)

            @block.gpsimd
            def _(pool):
                blocks.prime(None, None, None, pool)
                for s in range(2):
                    blocks.split_low(pool, s, s)
                prime(pool, mulled, 1)
                with pool.Fori(0, PH // 2 - 1) as i:
                    for par in range(2):
                        pool_head(pool, i * 2 + par, par)
                pool_head(pool, PH - 2, 0)
                for b in range(PH + 1, EARLY0 + 1):
                    blocks.split_low(pool, b, b % 2)

            def dve_wq(dve, h):
                for c in range(2):
                    dve.wait_ge(wq_high, h * 2 + (c + 1))
                    dve.tensor_tensor(wq_lo[:, c, :, :], wq[:, c, :, :], wq_hi[:, c, :, :].bitcast(F32),
                                      ALU.subtract).then_inc(wq_low, 1)

            def dve_pick(dve, h):
                dve.wait_ge(mulled, h + 2)
                for c in range(2):
                    dve.tensor_reduce(sel_e[:, c, :, bass.ds(h * TOPK, TOPK)],
                                      eq[:, c * TT:(c + 1) * TT, :, :], AX.X, ALU.add).then_inc(picked, 1)

            def dve_head(dve, h, h_before, split_next=True):
                ct = [(c, t) for c in range(2) for t in range(TT)]
                if split_next:
                    dve_wq(dve, h + 1)
                for c, t in ct:
                    if t == 0:
                        dve.wait_ge(s_kept, h * 2 + (c + 3))
                        hold(dve, passed)
                    dve.max(top[:, c, t, 0:8], sc[:, c, t, :]).then_inc(max1, 1)
                dve.wait_ge(max1, h * 8 + 8)
                hold(dve, passed)
                for c, t in ct:
                    dve.max_index(at[:, c, t, 0:8], top[:, c, t, 0:8], sc[:, c, t, :]).then_inc(cut1, 1)
                    dve.match_replace(rest[:, c, t, :], top[:, c, t, 0:8], sc[:, c, t, :],
                                      -3.0e38).then_inc(cut1, 1)
                dve.wait_ge(cut1, h * 16 + 32)
                hold(dve, passed)
                for c, t in ct:
                    dve.max(top[:, c, t, 8:16], rest[:, c, t, :]).then_inc(max2, 1)
                dve.wait_ge(max2, h * 8 + 8)
                dve.tensor_tensor(cand[:, :, :].rearrange("p t (a b) -> p t a b", a=TOPK),
                                  top[:, 0].unsqueeze(3).to_broadcast([P, TT, TOPK, TOPK]),
                                  top[:, 1].unsqueeze(2).to_broadcast([P, TT, TOPK, TOPK]),
                                  ALU.add).then_inc(cands, 1)
                for c, t in ct:
                    dve.max_index(at[:, c, t, 8:16], top[:, c, t, 8:16], rest[:, c, t, :]).then_inc(at2, 1)
                dve.wait_ge(cands, h + 1)
                hold(dve, passed)
                for t in range(TT):
                    dve.max(best[:, t, 0:8], cand[:, t, :]).then_inc(cmax1, 1)
                dve.wait_ge(cmax1, h * 4 + 4)
                hold(dve, passed)
                for t in range(TT):
                    dve.max_index(cat[:, t, 0:8], best[:, t, 0:8], cand[:, t, :]).then_inc(ccut1, 1)
                    dve.match_replace(crest[:, t, :], best[:, t, 0:8], cand[:, t, :], -3.0e38).then_inc(ccut1, 1)
                dve.wait_ge(at2, h * 8 + 8)
                if h_before is not None:
                    dve_pick(dve, h_before)
                dve.tensor_copy(atf[:, :, :, :], at[:, :, :, :]).then_inc(split, 1)
                dve.wait_ge(ccut1, h * 8 + 8)
                hold(dve, passed)
                for t in range(TT):
                    dve.max(best[:, t, 8:16], crest[:, t, :]).then_inc(cmax2, 1)
                dve.wait_ge(cmax2, h * 4 + 4)
                hold(dve, passed)
                for t in range(TT):
                    dve.max_index(cat[:, t, 8:16], best[:, t, 8:16], crest[:, t, :]).then_inc(cat2, 1)
                dve.wait_ge(cat2, h * 4 + 4)
                dve.tensor_single_scalar(ab[:, 0, :, :], cat[:, :, :], 4, ALU.logical_shift_right).then_inc(split, 1)
                dve.tensor_single_scalar(ab[:, 1, :, :], cat[:, :, :], 15, ALU.bitwise_and).then_inc(split, 1)
                dve.wait_ge(split, h * 4 + 3)
                dve.tensor_copy(abf[:, :, :, :], ab[:, :, :, :]).then_inc(split, 1)
                dve.wait_ge(cmax2, h * 4 + 4)
                dve.tensor_tensor(sel_w[:, :, bass.ds(h * TOPK, TOPK)], best[:, :, :],
                                  best[:, :, 0:1].to_broadcast([P, TT, TOPK]), ALU.subtract).then_inc(picked, 1)

            @block.vector
            def _(dve):
                prime(dve, cut1, 16)
                prime(dve, picked, 3)
                prime(dve, wq_low, 2)
                dve_wq(dve, 0)
                dve_head(dve, 0, None)
                with dve.Fori(1, PH - 1) as h:
                    dve_head(dve, h, h - 1)
                dve_head(dve, PH - 1, PH - 2, split_next=False)
                dve.wait_ge(picked, 3 * PH + 1)
                dve.engine_nop().then_inc(g1, 1)
                dve.wait_ge(split, PH * 4)
                dve.tensor_tensor(eq[:, :, :, :],
                                  abf[:, :, :, :].rearrange("p c t s -> p (c t) s").unsqueeze(3).to_broadcast(
                                      [P, 2 * TT, TOPK, TOPK]),
                                  iota[:, 0:TOPK].unsqueeze(1).unsqueeze(1).to_broadcast([P, 2 * TT, TOPK, TOPK]),
                                  ALU.is_equal).then_inc(eqd, 1)
                dve.wait_ge(eqd, (PH - 1) * TOPK + 1)
                dve.tensor_tensor(eq[:, :, :, :], eq[:, :, :, :], key_numbers, ALU.mult).then_inc(mulled, 1)
                dve_pick(dve, PH - 1)
                dve.wait_ge(g1, 2)
                slots = sel_w[:, :, :].rearrange("p t (h s) -> p (t h) s", s=TOPK)
                dve.tensor_reduce(gsum[:, :], slots, AX.X, ALU.add).then_inc(g1, 1)
                dve.wait_ge(g1, 3)
                dve.reciprocal(gsum[:, :], gsum[:, :]).then_inc(g1, 1)
                dve.wait_ge(g1, 4)
                dve.tensor_tensor(slots, slots, gsum[:, :].unsqueeze(2).to_broadcast([P, TT * PH, TOPK]),
                                  ALU.mult).then_inc(g1, 1)


def gate_matrix(nc, ident, iota, sel_w, sel_e, gates, blocks, early):
    QUADS = TC // 4
    RING = 4
    with ExitStack() as ctx:
        m = Mem(nc, ctx)
        eT = m.sb("eT", [P, 2, SEQ], BF16)
        iota4 = m.sb("iota4", [P, P, 4], BF16)
        rest = m.sb("w_rest", [P, 3, SEQ])
        parts = m.sb("w_part", [P, 3, SEQ], BF16)
        hot = m.sb("hot", [P, RING, 5, P, 4], BF16)
        stage = m.sb("stage", [P, 2, NK, TC])
        psT = m.ps("gpsT", [P, 2, SEQ])
        psG = m.ps("psG", [P, RING, 4, P])
        pool_passed, laid = m.sem("g_passed", "iota_laid")
        turned, kept, high, low, one_hot, scaled, scaled2, summed, staged, a_passed = m.sem(
            "g_turned", "g_kept", "g_high", "g_low", "one_hot", "hot_scaled", "hot_scaled2", "g_summed", "g_staged",
            "ga_passed")
        stored = m.sem("g_stored0", "g_stored1")
        PARTS = {n: (s, 2 * j, 2 * j + 2) for s in range(2) for j, n in enumerate(range(8 * s, 8 * s + 8, 2))}
        MADE = (6, 14)
        with nc.Block() as block:

            @block.tensor
            def _(pe):
                for n, src in enumerate((sel_e[:, 0], sel_e[:, 1], sel_w)):
                    if n == 2:
                        pe.wait_ge(kept, 1)
                    for t in range(TT):
                        mm = pe.transpose(psT[:, n % 2, t * P:(t + 1) * P], src[:, t, :], ident[:, :])
                    mm.then_inc(turned, 1)
                prime(pe, summed, RING)
                with pe.Fori(0, SEQ // TC // 2) as i:
                    for q in range(2 * QUADS):
                        n = i * (2 * QUADS) + q
                        pe.wait_ge(scaled, n + 1)
                        pe.wait_ge(scaled2, n + 1)
                        pe.wait_ge(staged, n + 1)
                        for a in range(4):
                            for part in range(3):
                                mm = pe.matmul(psG[:, q % RING, a, :], hot[:, q % RING, 0, :, a],
                                               hot[:, q % RING, part + 2, :, a], start=(part == 0),
                                               stop=(part == 2))
                        mm.then_inc(summed, 1)
                        if q in PARTS:
                            s, first, end = PARTS[q]
                            blocks.product(pe, i * 2 + (EARLY0 + s), s, first, end)

            def spread(e, i, q):
                kinds = e.shape[1]
                return e[:, :, bass.ds(i * (2 * TC) + q * 4, 4)].unsqueeze(2).to_broadcast([P, kinds, P, 4])

            @block.gpsimd
            def _(pool):
                pool.wait_ge(low, 2)
                with pool.Fori(0, SEQ // TC // 2) as i:
                    for q in range(2 * QUADS):
                        pool.wait_ge(one_hot, i * (2 * QUADS) + q + 1)
                        hold(pool, pool_passed)
                        pool.tensor_tensor(hot[:, q % RING, 4, :, :], hot[:, q % RING, 1, :, :],
                                           parts[:, 2, bass.ds(i * (2 * TC) + q * 4, 4)].unsqueeze(1).to_broadcast(
                                               [P, P, 4]), ALU.mult).then_inc(scaled2, 1)
                        if q == 3:
                            blocks.split_low(pool, i * 2 + (EARLY0 + 1), 1)
                blocks.split_low(pool, EARLY + 1, 1)

            @block.vector
            def _(dve):
                dve.tensor_copy(iota4[:, :, :], iota[:, :].unsqueeze(2).to_broadcast([P, P, 4])).then_inc(laid, 1)
                for n, dst in enumerate((eT[:, 1, :], eT[:, 0, :], rest[:, 0, :])):
                    dve.wait_ge(turned, n + 1)
                    dve.tensor_copy(dst, psT[:, n % 2, :]).then_inc(kept, 1)
                dve.wait_ge(kept, 3)
                for n in range(3):
                    dve.tensor_copy(parts[:, n, :], rest[:, n, :]).then_inc(high, 1)
                    dve.wait_ge(high, n + 1)
                    if n < 2:
                        dve.tensor_tensor(rest[:, n + 1, :], rest[:, n, :], parts[:, n, :],
                                          ALU.subtract).then_inc(low, 1)
                        dve.wait_ge(low, n + 1)
                dve.wait_ge(laid, 1)
                with dve.Fori(0, SEQ // TC // 2) as i:
                    for q in range(2 * QUADS):
                        if q % 2 == 0:
                            for r in (q, q + 1):
                                dve.wait_ge(summed, i * (2 * QUADS) + r + 1)
                                dve.tensor_tensor(
                                    hot[:, r % RING, 0:2, :, :],
                                    iota4[:, :, :].unsqueeze(1).to_broadcast([P, 2, P, 4]),
                                    spread(eT[:, :, :], i, r), ALU.is_equal).then_inc(one_hot, 1)
                        dve.wait_ge(one_hot, i * (2 * QUADS) + q + 1)
                        dve.tensor_tensor(
                            hot[:, q % RING, 2:4, :, :],
                            hot[:, q % RING, 1, :, :].unsqueeze(1).to_broadcast([P, 2, P, 4]),
                            spread(parts[:, 0:2, :], i, q), ALU.mult).then_inc(scaled, 1)
                        if q == 13:
                            dve.wait_ge(blocks.low, i * 2 + (EARLY0 + 2 + blocks.AHEAD))
                            blocks.split_low(dve, i * 2 + (EARLY0 + 2), 0)

            @block.scalar
            def _(act):
                prime(act, staged, RING)
                for s in range(2):
                    prime(act, stored[s], 16)
                with act.Fori(0, SEQ // TC // 2) as i:
                    for q in range(2 * QUADS):
                        act.wait_ge(summed, i * (2 * QUADS) + q + (RING + 1))
                        s = q // QUADS
                        if q % QUADS == 0:
                            act.wait_ge(stored[s], i * 16 + 16)
                        t = (q % QUADS) * 4
                        act.copy(stage[:, s, :, t:t + 4], psG[:, q % RING, :, :].rearrange("p a i -> p i a")
                                 ).then_inc(staged, 1)
                        if q - 1 in MADE:
                            s = MADE.index(q - 1)
                            blocks.gelu(act, i * 2 + (EARLY0 + s), s, block_of(early, i * 2 + (EARLY0 + s)), a_passed)
                            blocks.split_high(act, i * 2 + (EARLY0 + s + 2), s, i * 16 + 16 * (EARLY0 // 2 + 2))

            @block.sync
            def _(sp):
                with sp.Fori(0, SEQ // TC // 2) as i:
                    for s in range(2):
                        blocks.load(sp, i * 2 + (EARLY0 + s + 2), s)
                        sp.wait_ge(staged, i * (2 * QUADS) + ((s + 1) * QUADS + RING))
                        sp.dma_start(gates[bass.ds(i * 2 + s, 1)].rearrange("a p i t -> p (a i) t"),
                                     stage[:, s, :, :]).then_inc(stored[s], 16)
                for s in range(2):
                    sp.wait_ge(stored[s], 16 + 16 * (SEQ // TC // 2))


def experts(nc, acc, gates, w, blocks, early):
    A = blocks.AHEAD
    with ExitStack() as ctx:
        m = Mem(nc, ctx)
        v_raw = m.sb("v_raw", [P, BG, HALF])
        v_hi = m.sb("v_hi", [P, BG, HALF], F32R)
        v_lo = m.sb("v_lo", [P, BG, HALF], F32R)
        g_sb = m.sb("g_sb", [P, 2, SEQ // TC, BG, TC])
        activ = early[:, 0:BG, :]
        w_hi = m.sb("w_hi", [P, 2, BG, SEQ], F32R)
        w_lo = m.sb("w_lo", [P, 2, BG, SEQ], F32R)
        psB = m.ps("psB", [P, TT, HALF])
        v_in = m.sem(*[f"v_in{blk}" for blk in range(BG)])
        g_in = m.sem("g_in0", "g_in1")
        (v_high, v_low, multiplied, w_high, w_low, b_step, b_made, drained) = m.sem(
            "v_high", "v_low", "multiplied", "w_high", "w_low", "b_step", "b_made", "drained")

        def pe_b(pe, g, par, half):
            for blk in range(BG):
                if half == 0:
                    pe.wait_ge(w_low, g * 4 + (blk + 1))
                pe.wait_ge(v_low, g * 8 + (half * 4 + blk + 1))
                for t in range(TT):
                    if blk == 0:
                        pe.wait_ge(drained, g * 8 + (half * 4 + t + 1))
                    ts = slice(t * P, (t + 1) * P)
                    pe.matmul(psB[:, t, :], w_hi[:, par, blk, ts], v_hi[:, blk, :], start=(blk == 0), stop=False)
                    pe.matmul(psB[:, t, :], w_hi[:, par, blk, ts], v_lo[:, blk, :], start=False, stop=False)
                    mm = pe.matmul(psB[:, t, :], w_lo[:, par, blk, ts], v_hi[:, blk, :], start=False,
                                   stop=(blk == BG - 1))
                    if blk == BG - 1:
                        mm.then_inc(b_made, 1)
                if blk < BG - 1:
                    mm.then_inc(b_step, 1)

        def slot_free(eng, g, half, blk):
            if blk < BG - 1:
                from_one(eng, b_step, (g * 2 + half - 1) * 3 + blk + 1)
            else:
                from_one(eng, b_made, (g * 2 + half) * 4 + 1)

        def act_u(act, gb, k):
            blocks.split_high(act, gb * 4 + k, k % 2, gb * 32 + 16 * (k // 2 + 1))

        def w_in(b, k, made_early):
            return block_of(early, b) if made_early else activ[:, k, :]

        def act_w(act, gb, par, k, made_early):
            b = gb * 4 + k
            if not made_early:
                act.wait_ge(w_low, b - 3)
                blocks.gelu(act, b, k % 2, activ[:, k, :])
            act.wait_ge(multiplied, b + 1)
            from_one(act, b_made, (gb - 1) * 8 + 1)
            act.copy(w_hi[:, par, k, :], w_in(b, k, made_early)).then_inc(w_high, 1)

        def act_v(act, g, half, blk):
            act.wait_ge(v_in[blk], g * 32 + half * 16 + 16)
            slot_free(act, g, half, blk)
            act.copy(v_hi[:, blk, :], v_raw[:, blk, :]).then_inc(v_high, 1)

        def dve_u(dve, gb, k):
            blocks.split_low(dve, gb * 4 + k, k % 2)

        def dve_w(dve, gb, par, k, g_count, made_early):
            b = gb * 4 + k
            dve.wait_ge(g_in[par], g_count)
            if not made_early:
                dve.wait_ge(blocks.gelued, b + (A + 1))
            a = w_in(b, k, made_early)
            chunks = a.rearrange("p (c t) -> p c t", t=TC)
            dve.tensor_tensor(chunks, chunks, g_sb[:, par, :, k, :], ALU.mult).then_inc(multiplied, 1)
            dve.wait_ge(w_high, b + 1)
            dve.tensor_tensor(w_lo[:, par, k, :], a, w_hi[:, par, k, :].bitcast(F32),
                              ALU.subtract).then_inc(w_low, 1)

        def dve_v(dve, g, half, blk):
            dve.wait_ge(v_high, g * 8 + (half * 4 + blk + 1))
            dve.tensor_tensor(v_lo[:, blk, :], v_raw[:, blk, :], v_hi[:, blk, :].bitcast(F32),
                              ALU.subtract).then_inc(v_low, 1)

        def dve_drain(dve, g, half):
            for t in range(TT):
                dve.wait_ge(b_made, g * 8 + (half * 4 + t + 2))
                a = acc[:, t, half * HALF:(half + 1) * HALF]
                dve.tensor_tensor(a, a, psB[:, t, :], ALU.add).then_inc(drained, 1)

        def sp_u(sp, gb, k):
            blocks.load(sp, gb * 4 + k, k % 2)

        def sp_v(sp, g, half):
            for blk in range(BG):
                from_one(sp, v_low, g * 8 + (half * 4 + blk - 3))
                load(sp, v_raw[:, blk, :], w["v"][bass.ds(g * 4 + blk, 1), :, half * HALF:(half + 1) * HALF].rearrange(
                    "b p d -> p (b d)"), v_in[blk])

        def sp_g(sp, gb, par):
            from_one(sp, multiplied, gb * 4 - 4)
            load(sp, g_sb[:, par, :, :, :], gates[:, :, bass.ds(gb * 4, 4), :].rearrange(
                "c p i t -> p c (i t)"), g_in[par])

        ALL, EARLIER, HALF_EARLIER, NONE = range(4)

        def made_early(a, k):
            return a == EARLIER or (a == HALF_EARLIER and k < 2)

        def sp_turn(sp, g, par, a=ALL, u=True, v=True, gs=True):
            if gs:
                sp_g(sp, g + 2, par)
            for half in range(2):
                if a in (ALL, HALF_EARLIER) and u:
                    for k in (2 * half, 2 * half + 1):
                        sp_u(sp, g + 2, k)
                if v:
                    sp_v(sp, g + 1, half)

        def pe_turn(pe, g, par, a=ALL):
            for half in range(2):
                for k in (2 * half, 2 * half + 1):
                    if a != NONE and not made_early(a, k):
                        blocks.product(pe, (g + 1) * 4 + k, k % 2)
                pe_b(pe, g, par, half)

        def next_u(split, eng, gb, k):
            split(eng, gb + k // 2, (k + 2) % 4)

        def act_turn(act, g, par, a=ALL, u=True, v=True):
            for half in range(2):
                if a != NONE:
                    for k in (2 * half, 2 * half + 1):
                        if a != EARLIER and (u or k < 2):
                            next_u(act_u, act, g + 1, k)
                        act_w(act, g + 1, 1 - par, k, made_early(a, k))
                if half == 0 or v:
                    for blk in range(BG):
                        act_v(act, g + half, 1 - half, blk)

        def dve_turn(dve, g, par, g_count, a=ALL, u=True, v=True):
            for half in range(2):
                if a != NONE:
                    for k in (2 * half, 2 * half + 1):
                        if a != EARLIER and (u or k < 2):
                            next_u(dve_u, dve, g + 1, k)
                        dve_w(dve, g + 1, 1 - par, k, g_count, made_early(a, k))
                if half == 0 or v:
                    for blk in range(BG - 1):
                        dve_v(dve, g + half, 1 - half, blk)
                dve_drain(dve, g, half)
                if half == 0 or v:
                    dve_v(dve, g + half, 1 - half, BG - 1)

        FIRST = EARLY // BG - 1
        assert EARLY % BG == 0 and FIRST % 2 == 0
        LAST = GROUPS - 2
        with nc.Block() as block:

            @block.sync
            def _(sp):
                sp_g(sp, 0, 0)
                sp_v(sp, 0, 0)
                sp_g(sp, 1, 1)
                sp_v(sp, 0, 1)
                for k in (2, 3):
                    sp_u(sp, FIRST + 1, k)
                with sp.Fori(0, FIRST // 2) as i:
                    for par in range(2):
                        sp_turn(sp, i * 2 + par, par, a=EARLIER)
                sp_turn(sp, FIRST, 0, a=HALF_EARLIER)
                sp_turn(sp, FIRST + 1, 1)
                with sp.Fori(FIRST // 2 + 1, LAST // 2) as i:
                    for par in range(2):
                        sp_turn(sp, i * 2 + par, par)
                sp_turn(sp, LAST, 0, u=False, gs=False)

            @block.tensor
            def _(pe):
                prime(pe, b_made, 1)
                for b in (EARLY, EARLY + 1):
                    blocks.product(pe, b, b % 2)
                with pe.Fori(0, FIRST // 2) as i:
                    for par in range(2):
                        pe_turn(pe, i * 2 + par, par, a=EARLIER)
                pe_turn(pe, FIRST, 0, a=HALF_EARLIER)
                pe_turn(pe, FIRST + 1, 1)
                with pe.Fori(FIRST // 2 + 1, LAST // 2) as i:
                    for par in range(2):
                        pe_turn(pe, i * 2 + par, par)
                pe_turn(pe, LAST, 0)
                pe_turn(pe, LAST + 1, 1, a=NONE)

            @block.scalar
            def _(act):
                for k in range(BG):
                    act_v(act, 0, 0, k)
                    act_w(act, 0, 0, k, True)
                for b in (EARLY, EARLY + 1):
                    blocks.gelu(act, b, b % 2, early[:, b, :])
                with act.Fori(0, FIRST // 2) as i:
                    for par in range(2):
                        act_turn(act, i * 2 + par, par, a=EARLIER)
                act_turn(act, FIRST, 0, a=HALF_EARLIER)
                act_turn(act, FIRST + 1, 1)
                with act.Fori(FIRST // 2 + 1, LAST // 2) as i:
                    for par in range(2):
                        act_turn(act, i * 2 + par, par)
                act_turn(act, LAST, 0, u=False)
                act_turn(act, LAST + 1, 1, a=NONE, v=False)

            @block.vector
            def _(dve):
                prime(dve, drained, TT)
                for k in range(BG):
                    dve_v(dve, 0, 0, k)
                    dve_w(dve, 0, 0, k, 16, True)
                with dve.Fori(0, FIRST // 2) as i:
                    for par in range(2):
                        dve_turn(dve, i * 2 + par, par, (i + 1 + par) * 16, a=EARLIER)
                dve_turn(dve, FIRST, 0, (FIRST // 2 + 1) * 16, a=HALF_EARLIER)
                dve_turn(dve, FIRST + 1, 1, (FIRST // 2 + 2) * 16)
                with dve.Fori(FIRST // 2 + 1, LAST // 2) as i:
                    for par in range(2):
                        dve_turn(dve, i * 2 + par, par, (i + 1 + par) * 16)
                dve_turn(dve, LAST, 0, (GROUPS // 2) * 16, u=False)
                dve_turn(dve, LAST + 1, 1, 0, a=NONE, v=False)


def final_norm(nc, acc, out, w):
    with ExitStack() as ctx:
        m = Mem(nc, ctx)
        gain = m.sb("f_gain", [P, D])
        sq = m.sb("f_sq", [P, D])
        ss = m.sb("f_ss", [P, TT])
        ms = m.sb("f_ms", [P, TT])
        half = m.sb("f_half", [P, TT])
        rstd = m.sb("f_rstd", [P, TT])
        gain_in, squared, mean, rooted, scaled, out_done = m.sem("f_gain_in", "f_squared", "f_mean", "f_rooted",
                                                                 "f_scaled", "out_done")
        with nc.Block() as block:

            @block.sync
            def _(sp):
                load(sp, gain[:, :], w["lnf"].partition_broadcast(P), gain_in)
                for t in range(TT):
                    sp.wait_ge(scaled, t + 1)
                    sp.dma_start(out[t * P:(t + 1) * P, :], acc[:, t, :]).then_inc(out_done, 16)
                sp.wait_ge(out_done, 16 * TT)

            @block.scalar
            def _(act):
                for t in range(TT):
                    act.activation(sq[:, :], acc[:, t, :], ACT.Square, accum_out=ss[:, t:t + 1]).then_inc(squared, 1)
                    act.wait_ge(squared, t + 1)

            @block.gpsimd
            def _(pool):
                pool.memset(half[:, :], -0.5).then_inc(mean, 1)
                pool.wait_ge(squared, TT)
                pool.tensor_scalar(ms[:, :], ss[:, :], 1.0 / D, EPS, ALU.mult, ALU.add).then_inc(mean, 1)
                pool.wait_ge(mean, 2)
                pool.tensor_tensor(rstd[:, :], ms[:, :], half[:, :], ALU.pow).then_inc(rooted, 1)

            @block.vector
            def _(dve):
                dve.wait_ge(gain_in, 16)
                dve.wait_ge(rooted, 1)
                for t in range(TT):
                    dve.scalar_tensor_tensor(out=acc[:, t, :], in0=acc[:, t, :], scalar=rstd[:, t:t + 1],
                                             in1=gain[:, :], op0=ALU.mult, op1=ALU.mult).then_inc(scaled, 1)


def program(nc, w, out):
    with ExitStack() as ctx:
        m = Mem(nc, ctx)
        acc = m.sb("acc", [P, TT, D])
        ident = m.sb("ident", [P, P])
        gains = m.sb("gains", [P, 2, KD])
        iota = m.sb("iota", [P, P])
        sums = m.sb("sums_of_squares", [P, TT])
        x_in = m.sem(*[f"x_in{t}" for t in range(TT)])
        small_in, dbg_out = m.sem("small_in", "dbg_out")
        with nc.Block() as block:

            @block.sync
            def _(sp):
                for t in range(TT):
                    load(sp, acc[:, t, :], w["x"][t * P:(t + 1) * P, :], x_in[t])
                load(sp, ident[:, :], w["ident"], small_in)
                load(sp, iota[:, :], w["iota"], small_in)
                load(sp, gains[:, :, :], w["gains"].rearrange("p (a k) -> p a k", a=2), small_in)

        with ExitStack() as ctx2:
            m2 = Mem(nc, ctx2)
            oT = m2.sb("oT", [P, KD, SEQ])
            with ExitStack() as ctx3:
                m3 = Mem(nc, ctx3)
                a_hi = m3.sb("a_hi", [P, KD, SEQ], F32R)
                a_lo = m3.sb("a_lo", [P, KD, SEQ], F32R)
                tiles = Tiles(m3, w["w_tiles"])
                norm_transposed(nc, "n1", acc, [[(x_in[t], 16)] for t in range(TT)], gains[:, 0, :],
                                [(small_in, 48)], ident, a_hi, a_lo, tiles.prefetch)
                wo, wo_in = attention(nc, m3, a_hi, a_lo, ident, oT, w, tiles)
                project_out(nc, oT, acc, wo, wo_in, sums)

        gates = nc.dram_tensor("gate_scratch", (SEQ // TC, P, NK, TC), F32, kind="Internal").ap()
        h_hi = m.sb("h_hi", [P, KD, SEQ], F32R)
        h_lo = m.sb("h_lo", [P, KD, SEQ], F32R)
        blocks = Activations(m, h_hi, h_lo, w["uT"])
        early = m.sb("early", [P, EARLY + 2, SEQ])
        with ExitStack() as ctx2:
            m2 = Mem(nc, ctx2)
            sel_w = m2.sb("sel_w", [P, TT, SEL])
            sel_e = m2.sb("sel_e", [P, 2, TT, SEL])
            with ExitStack() as ctx3:
                keys = Queries(Mem(nc, ctx3), w)

                def prefetch(sp):
                    keys.prefetch(sp)
                    for s in range(2):
                        blocks.load_first(sp, s)

                norm_transposed(nc, "n2", acc, [[]] * TT, gains[:, 1, :], [(small_in, 48)], ident, h_hi, h_lo,
                                prefetch, sums)
                choose_experts(nc, iota, sel_w, sel_e, w, blocks, early, keys)
            gate_matrix(nc, ident, iota, sel_w, sel_e, gates, blocks, early)
        experts(nc, acc, gates, w, blocks, early)
        final_norm(nc, acc, out, w)


def constants():
    q = np.arange(P)[:, None]
    dist = 384 + q - np.arange(SEQ)[None]
    t_nsa = np.where(dist >= 0, dist, MASKED)
    tq = np.arange(SEQ).reshape(TT, P).T[:, :, None]
    dc = tq - (np.arange(NCMP) * CMP_STRIDE + CMP_LEN - 1)[None, None]
    t_cmp = np.where(dc >= 0, dc, MASKED).reshape(P, -1)
    ds = P + q - np.arange(2 * P)[None]
    t_swa = np.where((ds >= 0) & (ds < SWA_WIN), ds, MASKED)
    n = NSA_HEADS + SWA_HEADS
    slopes = (2.0 ** (-8.0 * (np.arange(n) + 1) / n)).astype(np.float32)
    f = lambda a: np.ascontiguousarray(a, np.float32)
    return {"t_nsa": f(t_nsa), "t_cmp": f(t_cmp), "t_swa": f(t_swa),
            "slopes": f(np.broadcast_to(slopes, (P, n))), "ident": f(np.eye(P)),
            "iota": f(np.broadcast_to(np.arange(P), (P, P)))}


def layouts(x, ln1_g, w_in, cmp_pe_k, cmp_w1_k, cmp_w2_k, cmp_pe_v, cmp_w1_v, cmp_w2_v, swa_sinks, w_out,
            ln2_g, peer_wq, peer_keys, peer_u, peer_v, lnf_g):
    c = np.ascontiguousarray
    w_in = np.asarray(w_in)[0]
    cut = np.cumsum([512, 128, 128, 128, 128, 128, 128, 24, 512, 64, 64])[:-1]
    q_n, kc, vc, ks, vs, kw, vw, gt, q_s, k_s, v_s = np.split(w_in, cut, axis=1)
    head = lambda q, h: q[:, h * HD:(h + 1) * HD]
    tiles = [kc, vc, ks, kw, np.concatenate([k_s, k_s], 1)]
    tiles += [np.concatenate([head(q_n, j), head(q_n, j + 4)], 1) for j in range(PAIRS)]
    tiles += [q_s[:, j * P:(j + 1) * P] for j in range(PAIRS)]
    chunked = lambda a: a.reshape(KD, P, -1).transpose(1, 0, 2).reshape(P, -1)
    gates = gt.reshape(D, NSA_HEADS, 3).transpose(0, 2, 1).reshape(D, 24)
    nat = np.concatenate([vs, vw, v_s, gates], 1)
    pe = [np.asarray(a)[0].reshape(LP, 2, HD).transpose(1, 2, 0).reshape(P, LP) for a in (cmp_pe_k, cmp_pe_v)]
    w1 = [np.asarray(a)[0].reshape(LP, P, CMP_HID).transpose(1, 0, 2).reshape(P, -1) for a in (cmp_w1_k, cmp_w1_v)]
    w2 = [np.asarray(a)[0].reshape(2, P, HD).transpose(1, 0, 2).reshape(P, -1) for a in (cmp_w2_k, cmp_w2_v)]
    wo = np.asarray(w_out)[0].reshape(16, HD, D)
    order = [h for j in range(PAIRS) for h in (j, j + 4)] + list(range(8, 16))
    wo = chunked(wo[order].reshape(D, D))
    wq = np.asarray(peer_wq)[0].reshape(KD, P, PH * 2, P).transpose(2, 1, 0, 3).reshape(PH * 2, P, KD * P)
    keys = np.asarray(peer_keys)[0].transpose(0, 3, 1, 2).reshape(PH, P, 2 * NK)
    uT = np.asarray(peer_u)[0].reshape(NK, P, KD, P).transpose(0, 3, 2, 1).reshape(NK, P, KD * P)
    v = np.asarray(peer_v)[0].reshape(NK, P, D)
    return {"x": c(np.asarray(x)[0]), "gains": c(np.concatenate(
        [np.asarray(g)[0].reshape(KD, P).T for g in (ln1_g, ln2_g)], 1)),
        "w_tiles": c(np.stack([chunked(a) for a in tiles])), "w_nat": c(chunked(nat)),
        "pe": c(np.concatenate(pe, 1)), "w1": c(np.concatenate(w1, 1)), "w2": c(np.concatenate(w2, 1)),
        "sinks": c(np.asarray(swa_sinks)[0]), "w_out": c(wo), "wq": c(wq), "keys": c(keys),
        "uT": c(uT), "v": c(v), "lnf": c(np.asarray(lnf_g))}


def kernel(**inputs):
    import concourse.bacc as _bacc
    from concourse.bass_utils import run_bass_kernel_spmd as _run

    nc = _bacc.Bacc("TRN2", target_bir_lowering=False, num_devices=1)
    arrays = {**layouts(**inputs), **constants()}
    w = {n: nc.dram_tensor(f"in_{n}", a.shape, mybir.dt.from_np(a.dtype), kind="ExternalInput").ap()
         for n, a in arrays.items()}
    out = nc.dram_tensor("out", (SEQ, D), F32, kind="ExternalOutput").ap()
    program(nc, w, out)
    r = _run(nc, [{f"in_{n}": a for n, a in arrays.items()}], core_ids=[0])
    return r.results[0]["out"].reshape(1, SEQ, D)
```
